# Optimizing a Trainium2 kernel written in Bass

```python
import jax, jax.numpy as jnp
from jax import lax
import numpy as np

D_MODEL = 1024
BATCH = 1
SEQ = 512
DEPTH = 1

HEAD_DIM = 64
ROPE_THETA = 10000.0
EPS = 1e-6
GRID_W = 64
DIL_PAIRS = ((128, 1), (512, 4), (2048, 16))
N_GROUPS_A = len(DIL_PAIRS)
HEADS_PER_GROUP_A = 4
A_QBLOCK = 64
N_Q_HEADS_B = 8
N_KV_HEADS_B = 2
B_QBLOCK = 128
N_BRANCHES = 2
A_QKV_WIDTH = N_GROUPS_A * 3 * HEADS_PER_GROUP_A * HEAD_DIM
A_OUT_WIDTH = HEADS_PER_GROUP_A * HEAD_DIM
B_Q_WIDTH = N_Q_HEADS_B * HEAD_DIM
B_KV_WIDTH = 2 * N_KV_HEADS_B * HEAD_DIM
IN_WIDTH = A_QKV_WIDTH + B_Q_WIDTH + B_KV_WIDTH + N_BRANCHES * D_MODEL
N_EXPERTS = 64
N_EXPERT_GROUPS = 8
TOPK_GROUPS = 4
TOP_K = 8
EXPERT_FF = D_MODEL // 4
ROUTED_SCALE = 2.5
MOE_BLOCK = 128

kernel_name = 'hybrid_dilated_gqa2d_gated_moe_encoder'

def rms_norm(x, g):
    xf = x.astype(jnp.float32)
    y = xf * lax.rsqrt(jnp.mean(xf * xf, axis=-1, keepdims=True) + EPS)
    return (y * g.astype(jnp.float32)).astype(x.dtype)

def rope_tables(pos, dim):
    inv = ROPE_THETA ** (-jnp.arange(0, dim, 2, dtype=jnp.float32) / dim)
    ang = pos.astype(jnp.float32)[:, None] * inv[None, :]
    ang = jnp.concatenate([ang, ang], axis=-1)
    return jnp.cos(ang), jnp.sin(ang)

def apply_rope(x, cos, sin):
    s, dim = cos.shape
    bshape = (s,) + (1,) * (x.ndim - 3) + (dim,)
    xf = x.astype(jnp.float32)
    x1, x2 = xf[..., : dim // 2], xf[..., dim // 2:]
    rot = jnp.concatenate([-x2, x1], axis=-1)
    return (xf * cos.reshape(bshape) + rot * sin.reshape(bshape)).astype(x.dtype)

def apply_rope_2d(x, cos_r, sin_r, cos_c, sin_c):
    half = HEAD_DIM // 2
    return jnp.concatenate([apply_rope(x[..., :half], cos_r, sin_r),
                            apply_rope(x[..., half:], cos_c, sin_c)], axis=-1)

def _split_blocks(t, block):
    b, s = t.shape[:2]
    return t.reshape((b, s // block, block) + t.shape[2:]).swapaxes(0, 1)

def _merge_blocks(t):
    nb, b, blk = t.shape[:3]
    return t.swapaxes(0, 1).reshape((b, nb * blk) + t.shape[3:])

def _dilated_group(q, k, v, dilation, radius):
    b, s, h, hd = q.shape
    pad = dilation * radius
    offs = dilation * jnp.arange(-radius, radius + 1)
    k_p = jnp.pad(k, ((0, 0), (pad, pad), (0, 0), (0, 0)))
    v_p = jnp.pad(v, ((0, 0), (pad, pad), (0, 0), (0, 0)))
    q_blocks = _split_blocks(q, A_QBLOCK)
    starts = jnp.arange(s // A_QBLOCK) * A_QBLOCK
    scale = HEAD_DIM ** -0.5

    def block(args):
        qb, s0 = args
        kpos = s0 + jnp.arange(A_QBLOCK)[:, None] + offs[None, :]
        valid = (kpos >= 0) & (kpos < s)
        kb = k_p[:, kpos + pad]
        vb = v_p[:, kpos + pad].astype(jnp.float32)
        sc = jnp.einsum('bqhd,bqjhd->bqhj', qb, kb, preferred_element_type=jnp.float32) * scale
        sc = jnp.where(valid[None, :, None, :], sc, -jnp.inf)
        m = sc.max(axis=-1)
        p = jnp.exp(sc - m[..., None])
        den = p.sum(axis=-1)
        o = jnp.einsum('bqhj,bqjhd->bqhd', p, vb) / den[..., None]
        return o, m, den

    o, m, den = lax.map(block, (q_blocks, starts))
    return _merge_blocks(o), _merge_blocks(m), _merge_blocks(den)

def dilated_attention(q, k, v):
    b, s = q.shape[:2]
    outs, maxes, dens = [], [], []
    for g, (window, dilation) in enumerate(DIL_PAIRS):
        o, m, den = _dilated_group(q[:, :, g], k[:, :, g], v[:, :, g], dilation, window // (2 * dilation))
        outs.append(o); maxes.append(m); dens.append(den)
    o = jnp.stack(outs)
    m = jnp.stack(maxes)
    den = jnp.stack(dens)
    wts = den * jnp.exp(m - m.max(axis=0, keepdims=True))
    out = (wts[..., None] * o).sum(axis=0) / wts.sum(axis=0)[..., None]
    return out.reshape(b, s, HEADS_PER_GROUP_A * HEAD_DIM).astype(q.dtype)

def gqa_attention(q, k, v):
    b, s, hq, hd = q.shape
    hkv = k.shape[2]
    rep = hq // hkv
    q_blocks = _split_blocks(q.reshape(b, s, hkv, rep, hd), B_QBLOCK)
    vf = v.astype(jnp.float32)
    scale = HEAD_DIM ** -0.5

    def block(qb):
        sc = jnp.einsum('bqgrd,bkgd->bgrqk', qb, k, preferred_element_type=jnp.float32) * scale
        p = jax.nn.softmax(sc, axis=-1)
        return jnp.einsum('bgrqk,bkgd->bqgrd', p, vf)

    o = _merge_blocks(lax.map(block, q_blocks))
    return o.reshape(b, s, hq * hd).astype(q.dtype)

def moe_ffn(xn, w_router, router_bias, we_gate, we_up, we_down, ws_gate, ws_up, ws_down):
    b, s, d = xn.shape
    n = b * s
    xf = xn.reshape(n, d)
    scores = jax.nn.sigmoid(jnp.dot(xf, w_router, preferred_element_type=jnp.float32))
    sel = scores + router_bias.astype(jnp.float32)
    gsel = sel.reshape(n, N_EXPERT_GROUPS, N_EXPERTS // N_EXPERT_GROUPS)
    gscore = lax.top_k(gsel, 2)[0].sum(axis=-1)
    _, gidx = lax.top_k(gscore, TOPK_GROUPS)
    gmask = (gidx[..., None] == jnp.arange(N_EXPERT_GROUPS)).any(axis=-2)
    emask = jnp.repeat(gmask, N_EXPERTS // N_EXPERT_GROUPS, axis=-1)
    _, eidx = lax.top_k(jnp.where(emask, sel, -jnp.inf), TOP_K)
    w = jnp.take_along_axis(scores, eidx, axis=-1)
    w = w / w.sum(axis=-1, keepdims=True) * ROUTED_SCALE
    nk = n * TOP_K
    flat_e = eidx.reshape(-1)
    flat_tok = jnp.arange(nk, dtype=jnp.int32) // TOP_K
    flat_w = w.reshape(-1)
    order = jnp.argsort(flat_e)
    se, stok, sw = flat_e[order], flat_tok[order], flat_w[order]
    counts = jnp.bincount(flat_e, length=N_EXPERTS)
    padded = (counts + MOE_BLOCK - 1) // MOE_BLOCK * MOE_BLOCK
    start = jnp.cumsum(counts) - counts
    pend = jnp.cumsum(padded)
    pstart = pend - padded
    dest = pstart[se] + jnp.arange(nk) - start[se]
    n_blocks = -(-(nk + N_EXPERTS * (MOE_BLOCK - 1)) // MOE_BLOCK)
    p_len = n_blocks * MOE_BLOCK
    buf_tok = jnp.zeros((p_len,), jnp.int32).at[dest].set(stok)
    buf_w = jnp.zeros((p_len,), jnp.float32).at[dest].set(sw)
    block_e = jnp.minimum(jnp.searchsorted(pend, jnp.arange(n_blocks) * MOE_BLOCK, side='right'),
                          N_EXPERTS - 1)
    shared = jnp.dot(jax.nn.silu(jnp.dot(xf, ws_gate)) * jnp.dot(xf, ws_up), ws_down).astype(jnp.float32)

    def step(acc, inp):
        tok, wb, e = inp
        xb = xf[tok]
        hb = jax.nn.silu(jnp.dot(xb, we_gate[e])) * jnp.dot(xb, we_up[e])
        yb = jnp.dot(hb, we_down[e]).astype(jnp.float32)
        return acc.at[tok].add(wb[:, None] * yb), None

    out, _ = lax.scan(step, shared, (buf_tok.reshape(n_blocks, MOE_BLOCK),
                                     buf_w.reshape(n_blocks, MOE_BLOCK), block_e))
    return out.astype(xn.dtype).reshape(b, s, d)

def setup_inputs(seed: int = 0) -> dict:
    key = jax.random.key(seed)
    ks = jax.random.split(key, 20)

    def nrm(k, shape, scale):
        return jax.random.normal(k, shape, jnp.float32) * scale

    return {
        'x': nrm(ks[0], (BATCH, SEQ, D_MODEL), 1.0),
        'norm1_g': 1.0 + nrm(ks[1], (DEPTH, D_MODEL), 0.02),
        'w_in': nrm(ks[2], (DEPTH, D_MODEL, IN_WIDTH), D_MODEL ** -0.5),
        'q_norm_a': 1.0 + nrm(ks[3], (DEPTH, HEAD_DIM), 0.02),
        'k_norm_a': 1.0 + nrm(ks[4], (DEPTH, HEAD_DIM), 0.02),
        'q_norm_b': 1.0 + nrm(ks[5], (DEPTH, HEAD_DIM), 0.02),
        'k_norm_b': 1.0 + nrm(ks[6], (DEPTH, HEAD_DIM), 0.02),
        'w_branch_a': nrm(ks[7], (DEPTH, A_OUT_WIDTH, D_MODEL), A_OUT_WIDTH ** -0.5),
        'w_branch_b': nrm(ks[8], (DEPTH, B_Q_WIDTH, D_MODEL), B_Q_WIDTH ** -0.5),
        'w_out': nrm(ks[9], (DEPTH, D_MODEL, D_MODEL), D_MODEL ** -0.5),
        'norm2_g': 1.0 + nrm(ks[10], (DEPTH, D_MODEL), 0.02),
        'w_router': nrm(ks[11], (DEPTH, D_MODEL, N_EXPERTS), D_MODEL ** -0.5),
        'router_bias': nrm(ks[12], (DEPTH, N_EXPERTS), 0.01),
        'we_gate': nrm(ks[13], (DEPTH, N_EXPERTS, D_MODEL, EXPERT_FF), D_MODEL ** -0.5),
        'we_up': nrm(ks[14], (DEPTH, N_EXPERTS, D_MODEL, EXPERT_FF), D_MODEL ** -0.5),
        'we_down': nrm(ks[15], (DEPTH, N_EXPERTS, EXPERT_FF, D_MODEL), EXPERT_FF ** -0.5),
        'ws_gate': nrm(ks[16], (DEPTH, D_MODEL, EXPERT_FF), D_MODEL ** -0.5),
        'ws_up': nrm(ks[17], (DEPTH, D_MODEL, EXPERT_FF), D_MODEL ** -0.5),
        'ws_down': nrm(ks[18], (DEPTH, EXPERT_FF, D_MODEL), EXPERT_FF ** -0.5),
    }

def reference(x, norm1_g, w_in, q_norm_a, k_norm_a, q_norm_b, k_norm_b, w_branch_a, w_branch_b,
              w_out, norm2_g, w_router, router_bias, we_gate, we_up, we_down, ws_gate, ws_up, ws_down):
    b, s, d = x.shape
    rows = s // GRID_W
    pos = jnp.arange(s)
    row_idx = jnp.repeat(jnp.arange(rows), GRID_W)
    col_idx = jnp.tile(jnp.arange(GRID_W), rows)
    cos1, sin1 = rope_tables(pos, HEAD_DIM)
    cos_r, sin_r = rope_tables(row_idx, HEAD_DIM // 2)
    cos_c, sin_c = rope_tables(col_idx, HEAD_DIM // 2)
    o1 = A_QKV_WIDTH
    o2 = o1 + B_Q_WIDTH
    o3 = o2 + B_KV_WIDTH

    h = x
    for l in range(DEPTH):
        xn = rms_norm(h, norm1_g[l])
        proj = jnp.dot(xn, w_in[l])
        a_qkv = proj[..., :o1].reshape(b, s, N_GROUPS_A, 3, HEADS_PER_GROUP_A, HEAD_DIM)
        qa = apply_rope(rms_norm(a_qkv[:, :, :, 0], q_norm_a[l]), cos1, sin1)
        ka = apply_rope(rms_norm(a_qkv[:, :, :, 1], k_norm_a[l]), cos1, sin1)
        va = a_qkv[:, :, :, 2]
        ya = dilated_attention(qa, ka, va)
        qb = proj[..., o1:o2].reshape(b, s, N_Q_HEADS_B, HEAD_DIM)
        kvb = proj[..., o2:o3].reshape(b, s, 2, N_KV_HEADS_B, HEAD_DIM)
        qb = apply_rope_2d(rms_norm(qb, q_norm_b[l]), cos_r, sin_r, cos_c, sin_c)
        kb = apply_rope_2d(rms_norm(kvb[:, :, 0], k_norm_b[l]), cos_r, sin_r, cos_c, sin_c)
        vb = kvb[:, :, 1]
        yb = gqa_attention(qb, kb, vb)
        gates = jax.nn.sigmoid(proj[..., o3:].reshape(b, s, N_BRANCHES, d))
        merged = gates[:, :, 0] * jnp.dot(ya, w_branch_a[l]) + gates[:, :, 1] * jnp.dot(yb, w_branch_b[l])
        h = h + jnp.dot(merged, w_out[l])
        h = h + moe_ffn(rms_norm(h, norm2_g[l]), w_router[l], router_bias[l], we_gate[l], we_up[l],
                        we_down[l], ws_gate[l], ws_up[l], ws_down[l])
    return h


_drawn_inputs = setup_inputs


def setup_inputs(seed=0):
    import zlib

    import numpy as np

    out = dict(_drawn_inputs(seed))
    spreads = {}
    factors = {'norm1_g': 2.899, 'k_norm_a': 3.505, 'q_norm_b': 8.0, 'k_norm_b': 3.285}
    for name, (base, spread) in spreads.items():
        noise = np.random.default_rng([zlib.crc32(name.encode()), seed]).standard_normal(out[name].shape)
        drawn = base * np.exp(spread * noise) if base else spread * noise
        out[name] = __import__('jax').numpy.asarray(drawn.astype(out[name].dtype))
    for name, factor in factors.items():
        out[name] = (out[name] * factor).astype(out[name].dtype)
    return out
```

```python
from contextlib import ExitStack

import numpy as np

import concourse.bass as bass
from concourse import mybir

F32 = mybir.dt.float32
BF16 = mybir.dt.bfloat16
I32 = mybir.dt.int32
ALU = mybir.AluOpType
ACT = mybir.ActivationFunctionType
AXIS = mybir.AxisListType

P = 128
S, D = 512, 1024
T = S // P
K = D // P
HD = 64
HALF = 512
GRID_W = 64
THETA = 10000.0
EPS = 1e-6
DILATIONS = (1, 4, 16)
RADIUS = 64
HA, HB, HKV = 4, 8, 2
A_WIDTH = 3 * 3 * HA * HD
E, FF = 64, D // 4
EG, TOPG, TOPK = 8, 4, 8
ROUTED_SCALE = 2.5
MASKED = -1.0e30
AWAY = 65536
CAP = 96
BLOCKS = -(-S // CAP)
NOV = (S * TOPK) // (CAP + 1)

NSLOT = 3
SLOT = 3 * K * FF
QKV_CHUNKS = 6
L_GATE = QKV_CHUNKS
L_OUT = L_GATE + 4
L_SHARED = L_OUT + 2
L_EXPERT = L_SHARED + 1
GATE_COL0 = A_WIDTH + HB * HD + 2 * HKV * HD

QA, KA, QB, KB = range(4)
PAIR_QB = 12
PAIR_KB = 16
NPAIR = 18


def q_pair(g, h):
    return 4 * g + h // 2


def k_pair(g, h):
    return 4 * g + 2 + h // 2


CHUNKS = [
    dict(norm=[(QA, 0, 4, 0, 1), (KA, 256, 4, 4, 1)], value=[], pairs=[0, 1, 2, 3]),
    dict(norm=[(QA, 256, 4, 0, 1)], value=[(0, 256, ("A", 0))], pairs=[4, 5]),
    dict(norm=[(KA, 0, 4, 0, 1)], value=[(256, 256, ("A", 1))], pairs=[6, 7]),
    dict(norm=[(QA, 0, 4, 0, 1), (KA, 256, 4, 4, 1)], value=[], pairs=[8, 9, 10, 11]),
    dict(norm=[(QB, 256, 4, 0, 1)], value=[(0, 256, ("A", 2))], pairs=[12, 13]),
    dict(norm=[(QB, 0, 4, 0, 1), (KB, 256, 2, 4, 2)], value=[(384, 128, ("B", 0))],
         pairs=[14, 15, 16, 17]),
]


def host_constants():
    tok = np.arange(S)

    def angles(pos, dim):
        inv = np.float32(THETA) ** (-np.arange(0, dim, 2, dtype=np.float32) / np.float32(dim))
        a = pos.astype(np.float32)[:, None] * inv[None, :].astype(np.float32)
        sin = np.sin(a)
        return np.concatenate([np.cos(a)] * 2, -1), np.concatenate([-sin, sin], -1)

    c1, s1 = angles(tok, HD)
    cr, sr = angles(tok // GRID_W, HD // 2)
    cc, sc = angles(tok % GRID_W, HD // 2)
    rope = np.stack([c1, s1, np.concatenate([cr, cc], -1), np.concatenate([sr, sc], -1)])
    rope = rope.reshape(4, P, T, HD).transpose(1, 0, 2, 3).reshape(P, 4 * T * HD)
    q, k = np.arange(P)[:, None], np.arange(P)[None, :]
    band = np.stack([np.where(np.abs(4 * (k - q) + d) <= RADIUS, 0.0, MASKED) for d in range(-3, 4)])
    by4 = np.where(np.abs(k - q) <= RADIUS, 0.0, MASKED)
    by16 = np.where((k - q) % 4 == 0, 0.0, MASKED)
    masks = np.concatenate([band.transpose(1, 0, 2).reshape(P, 7 * P), by4, by16], -1)
    ident = np.eye(P)
    below = (q < k).astype(np.float64)
    slots = np.broadcast_to(k, (P, P))
    token = 4 * q + np.arange(T)[None, :]
    row = TOPK * token
    away = np.full_like(token, -AWAY)
    parts = np.stack([token % 256, token - token % 256, away, row % 256, row - row % 256, away], -1)
    misc = np.concatenate([ident, below, slots, parts.reshape(P, T * 6)], -1)
    return (np.ascontiguousarray(rope, np.float32), np.ascontiguousarray(masks, np.float32),
            np.ascontiguousarray(misc, np.float32))


class Expert:

    def __init__(self, c, i=None):
        self.c, self.i, self.buf = c, i, c % 3
        self.n = c if i is None else 3 * i + c
        self.third = c // 3 if i is None else i + c // 3

    def next(self, d):
        return Expert(self.c + d, self.i)


def wait_for(eng, sem, n):
    if not isinstance(n, int) or n > 0:
        eng.wait_ge(sem, n)


class Steps:

    def __init__(self, eng, sem):
        self.eng, self.sem, self.n, self.at = eng, sem, 0, 0

    def done(self, ins):
        ins.then_inc(self.sem, 1)
        self.n += 1
        return self.n

    def wait(self):
        self.eng.wait_ge(self.sem, self.at + self.n)


def build(nc, a, out, xn2_rows, y_rows):
    ctx = ExitStack()
    with ctx:
        def sb(name, words, dt=F32):
            return ctx.enter_context(nc.sbuf_tensor(name, [P, words], dt))

        def sem(name):
            return ctx.enter_context(nc.semaphore(name))

        ring = sb("ring", NSLOT * SLOT)
        xs_t = sb("xs", T * D)
        xT_t = sb("xT", K * S)
        pairs_t = sb("pairs", NPAIR * S)
        v_t = sb("v", 3 * T * 256 + T * 128)
        mask_t = sb("masks", 9 * P)
        tab_t = sb("tables", 8 * T * HD)
        prob_t = sb("prob", 2 * (768 + 2 * HALF))
        work_t = sb("work", 8 * HALF)
        misc_t = sb("misc", 3 * P + T * 6)
        ones_t = sb("ones", P)
        bf_t = sb("consts_bf", 2 * P, BF16)
        small_t = sb("small", 256)
        gain_t = sb("gains", 4 * HD + E)
        ps_t = ctx.enter_context(nc.psum_tensor("banks", [P, 8 * HALF], F32))

        def view(t, off, *shape):
            n = int(np.prod(shape))
            v = t[:, off:off + n]
            if len(shape) == 1:
                return v
            names = "abcd"[:len(shape)]
            return v.rearrange(f"p ({' '.join(names)}) -> p {' '.join(names)}",
                               **{c: s for c, s in zip(names[1:], shape[1:])})

        def bank(b, n=HALF, off=0):
            return ps_t[:, b * HALF + off:b * HALF + off + n]

        xs = view(xs_t, 0, T, D)
        xT = view(xT_t, 0, K, S)
        pairs = view(pairs_t, 0, NPAIR, S)
        merged = view(pairs_t, 0, T, D)
        x2T = view(pairs_t, T * D, K, S)
        vA = view(v_t, 0, T, 3, 256)
        vB = view(v_t, 3 * T * 256, T, 128)
        band = view(mask_t, 0, 7 * P)
        strided_mask = view(mask_t, 7 * P, 2 * P)
        cosg = [view(tab_t, i * T * HD, T, HD) for i in range(4)]
        sing = [view(tab_t, (4 + i) * T * HD, T, HD) for i in range(4)]
        rope_raw = [view(pairs_t, i * T * HD, T, HD) for i in range(4)]
        prob = [view(prob_t, o, w) for o, w in ((0, 768), (768, HALF), (1280, HALF))]
        probT = [view(prob_t, o, w, P) for o, w in ((1792, 6), (2560, 4), (3072, 4))]
        xnorm = [view(prob_t, i * D, D) for i in range(2)]
        yT = view(work_t, 0, 6, S)
        squares = [view(work_t, i * HALF, 8, HD) for i in range(2)]
        normed = [view(work_t, (2 + i) * HALF, 8, HD) for i in range(2)]
        turned = [view(work_t, (4 + i) * HALF, 8, HD) for i in range(2)]
        rotated = [view(work_t, (6 + i) * HALF, 8, HD) for i in range(2)]
        ident = misc_t[:, 0:P]
        below_f = misc_t[:, P:2 * P]
        slot_row = misc_t[:, 2 * P:3 * P]
        place_parts = view(misc_t, 3 * P, T, 6)
        below_b, ones_b = bf_t[:, 0:P], bf_t[:, P:2 * P]
        g1c, g2c = view(small_t, 0, K), view(small_t, K, K)
        ssq, std, rstd = (view(small_t, 16 + 4 * i, T) for i in range(3))
        ssq2, std2, rstd2 = (view(small_t, 28 + 4 * i, T) for i in range(3))
        hss, hstd, hrstd = ([view(small_t, 40 + 16 * i + 8 * j, 8) for j in range(2)] for i in range(3))
        neg_max = [view(small_t, 88 + i, 1) for i in range(3)]
        den = [view(small_t, 91 + i, 1) for i in range(3)]
        rden = [view(small_t, 94 + i, 1) for i in range(3)]
        pmax = [view(small_t, 97 + i, 1) for i in range(2)]
        gains = view(gain_t, 0, 4, HD)
        bias_b = view(gain_t, 4 * HD, E)
        row_t = sb("gain_row", 4 * HD + E)
        eps_c = small_t[:, 100:101]

        gated = [view(v_t, i * HALF, HALF) for i in range(2)]
        gatedB = [view(v_t, (2 + i) * HALF, HALF) for i in range(2)]
        xg = [view(v_t, i * D, D) for i in range(3)]
        xgT = [view(xT_t, i * D, K, P)[:, :, 0:CAP] for i in range(3)]
        h_s = view(xT_t, 3 * D, FF)
        act_s = view(xT_t, 3 * D + FF, FF)
        hT_s = view(xT_t, 3 * D + 2 * FF, 2, P)
        y_s = [view(pairs_t, i * D, D) for i in range(3)]

        junk1 = view(work_t, 0, D)
        junk2 = view(v_t, 2 * D, D)

        def bank2(b):
            return ps_t[:, b * HALF:(b + 2) * HALF]

        scores = view(prob_t, 0, T, E)
        sel = view(prob_t, 256, T, E)
        selm = view(prob_t, 512, T, E)
        repl = view(prob_t, 768, T, E)
        mask = view(prob_t, 1024, T, E)
        wts = view(prob_t, 1280, T, E)
        pos = view(prob_t, 1536, T, E)
        m8 = view(prob_t, 1792, T, EG, 8)
        rank = view(prob_t, 2048, T, E)
        low = view(prob_t, 2304, T, E)
        low_ones = view(prob_t, 2816, E)
        tmp_w = view(prob_t, 2560, T, E)
        gs16 = view(work_t, 0, T, 16)
        gr16 = view(work_t, 64, T, 16)
        gm8 = view(work_t, 128, T, 8)
        gpen = view(work_t, 160, T, EG)
        gmask = view(work_t, 192, T, EG)
        top8 = view(work_t, 224, T, 8)
        wsum = view(work_t, 256, T)
        wrec = view(work_t, 260, T)
        cnt = view(work_t, 264, E)
        maskb = view(work_t, 512, T * E // 2).bitcast(BF16).rearrange("p (t e) -> p t e", t=T)
        placed = view(work_t, 704, E, 3)
        placed_i = view(work_t, 896, E, 2).bitcast(I32)
        tok_b = view(work_t, 1088, 4).bitcast(I32)
        dst_b = view(work_t, 1092, 4).bitcast(I32)
        w_b = view(work_t, 1096, 4)
        onehot = [view(tab_t, i * 256, 256).bitcast(BF16).rearrange("p (t s) -> p t s", t=T)[:, :, 0:CAP]
                  for i in range(3)]
        moving = view(tab_t, 768, T * E * 9 // 2).bitcast(BF16).rearrange("p (t e c) -> p t e c", t=T, e=E)
        moving_flat = moving.rearrange("p t e c -> p t (e c)")
        more_f = view(work_t, 1100, E)
        upto_f = view(work_t, 1164, E)
        le_f = view(v_t, 0, NOV, E)
        ov_e = view(work_t, 1228, NOV)
        ov_x = view(work_t, 1276, NOV)
        ov_base = view(work_t, 1324, NOV)
        ov_list = view(work_t, 1372, NOV + 1).bitcast(I32)
        ov_pos = view(work_t, 1424, T)
        ov_placed3 = view(work_t, 1432, 3)
        ov_num = view(work_t, 1443, 1)

        x_loaded = [sem(f"x_loaded{t}") for t in range(T)]
        first_loaded = sem("first_consts_loaded")
        second_loaded = sem("second_consts_loaded")
        gains_ready = sem("gains_ready")
        tok_copied = sem("token_index_copied")
        dst_copied = sem("row_index_copied")
        ring_loaded = [sem(f"ring_loaded{i}") for i in range(NSLOT)]
        ones_ready = sem("ones_ready")
        gains_ps = sem("gains_broadcast_ps")
        dve = sem("dve_steps")
        act = sem("act_steps")
        pool = sem("pool_steps")
        tables_ready = sem("tables_ready")
        std1_ready = sem("std1_ready")
        xn_ready = sem("xn_ready")
        xn_turned = sem("xn_turned")
        xT_ready = sem("xT_ready")
        proj_done = sem("proj_done")
        squares_ready = sem("squares_ready")
        sums_ready = sem("sums_ready")
        hstd_ready = sem("hstd_ready")
        normed_ready = sem("normed_ready")
        cos_done = sem("cos_done")
        rotated_ready = sem("rotated_ready")
        pairs_turned = sem("pairs_turned")
        pairs_ready = sem("pairs_ready")
        scores_done = sem("scores_done")
        max_ready = sem("max_ready")
        probs_ready = sem("probs_ready")
        probs_turned = sem("probs_turned")
        probT_act = sem("probT_act")
        probT_dve = sem("probT_dve")
        pv_done = sem("pv_done")
        probs_scaled = sem("probs_scaled")
        yT_a_ready = sem("yT_a_ready")
        yT_b_ready = sem("yT_b_ready")
        gate_done = sem("gate_done")
        gated_ready = sem("gated_ready")
        product_ready = sem("product_ready")
        merged_ready = sem("merged_ready")
        merged_turned = sem("merged_turned")
        mT_ready = sem("mT_ready")
        out_done = sem("out_done")
        h_ready = sem("h_ready")
        std2_ready = sem("std2_ready")
        xn2_ready = sem("xn2_ready")
        xn2_stored = [sem(f"xn2_stored{i}") for i in range(2)]
        x2_turned = sem("x2_turned")
        x2T_ready = sem("x2T_ready")
        logits_done = sem("logits_done")
        scores_ready = sem("scores_ready")
        mask_ready = sem("mask_ready")
        pos_done = sem("pos_done")
        moving_ready = sem("moving_ready")
        onehot_ready = sem("onehot_ready")
        placed_done = sem("placed_done")
        parts_summed = sem("parts_summed")
        index_ready = sem("index_ready")
        gu_done = sem("gate_up_done")
        silu_ready = sem("silu_ready")
        hid_ready = sem("hidden_ready")
        hid_turned = sem("hidden_turned")
        hidT_ready = sem("hiddenT_ready")
        down_done = sem("down_done")
        shared_added = sem("shared_added")
        w_ready = sem("slot_weight_ready")
        y_scaled = sem("y_scaled")
        gathered = [sem(f"gathered{i}") for i in range(3)]
        g_turned = sem("gathered_turned")
        gT_ready = sem("gatheredT_ready")
        scattered = [sem(f"scattered{i}") for i in range(3)]
        more_counted = sem("further_blocks_counted")
        more_listed = sem("further_blocks_listed")
        further_step = sem("further_index_steps")
        ov_onehot = sem("further_onehot_ready")
        ov_placed = sem("further_index_product_done")
        ov_indexed = sem("further_index_ready")
        ov_gathered = sem("further_gathered")
        ov_scattered = sem("further_scattered")
        pool_waited = sem("pool_waited")
        more_ended = sem("further_block_ended")
        rows_loaded = [sem(f"rows_loaded{i}") for i in range(NSLOT)]
        rows_summed = sem("rows_summed")
        out_ready = sem("out_ready")
        out_stored = sem("out_stored")

        x_rows = a["x"][0].rearrange("(p t) d -> p t d", t=T)
        out_rows = out[0].rearrange("(p t) d -> p t d", t=T)
        w_in = a["w_in"][0].rearrange("(p k) n -> p k n", k=K)
        w_out = a["w_out"][0].rearrange("(p k) n -> p k n", k=K)
        wba = a["w_branch_a"][0].rearrange("(j p) n -> p j n", p=P)
        wbb = a["w_branch_b"][0].rearrange("(j p) n -> p j n", p=P)
        w_router = a["w_router"][0].rearrange("(p k) e -> p k e", k=K)
        wr_s = sb("w_router_s", K * E)
        wr = wr_s[:, :].rearrange("p (k e) -> p k e", k=K)
        xn2_t = xn2_rows.rearrange("(p t) d -> p t d", t=T)
        y_tok = y_rows.rearrange("(p t c) d -> p t c d", t=T, c=TOPK)

        def slot(load):
            return ring[:, (load % NSLOT) * SLOT:(load % NSLOT + 1) * SLOT]

        def chunk_w(load):
            return slot(load)[:, 0:K * HALF].rearrange("p (k n) -> p k n", k=K)


        DMAS = {n: 2 if L_GATE <= n < L_OUT else 3 if n == L_SHARED else 1 for n in range(L_EXPERT)}
        landed, per_slot = {}, [0] * NSLOT
        for n in range(L_EXPERT):
            per_slot[n % NSLOT] += 16 * DMAS[n]
            landed[n] = per_slot[n % NSLOT]

        def wait_load(eng, n):
            eng.wait_ge(ring_loaded[n % NSLOT], landed[n])

        def expert_slot(ex):
            return (L_EXPERT + ex.c) % NSLOT

        def wait_expert(eng, ex):
            s = expert_slot(ex)
            eng.wait_ge(ring_loaded[s], per_slot[s] + 48 * (ex.third + 1))

        EXPERTS_IN_0 = sum((L_EXPERT + e) % NSLOT == 0 for e in range(E))

        def ffn_parts(s):
            w = ring[:, s * SLOT:(s + 1) * SLOT]
            return (w[:, 0:2 * K * FF].rearrange("p (s k f) -> p s k f", s=2, k=K),
                    w[:, 2 * K * FF:].rearrange("p (c d) -> p c d", c=2))

        NP = QKV_CHUNKS * T
        UNITS = []
        for r in range(T * HA):
            t, h = divmod(r, HA)
            UNITS += [("A", t, h), ("B", t, 2 * h), ("B", t, 2 * h + 1)]
        NU = len(UNITS)
        NM = 2 * 2 * T
        NC = 2 * T
        LOOP0, LOOPS = 4, (E - 8) // 3
        LAST0 = LOOP0 + 3 * LOOPS

        block = ctx.enter_context(nc.Block())

        def store_out(sp, u):
            t, half = divmod(u, 2)
            sp.wait_ge(out_ready, u + 1)
            sp.dma_start(out_rows[:, t, half * HALF:(half + 1) * HALF],
                         xs[:, t, half * HALF:(half + 1) * HALF]).then_inc(out_stored, 16)

        def further_blocks(eng, body):
            eng.wait_ge(more_counted, 1)
            count = eng.value_load(ov_list[0:1, 0:1], min_val=0, max_val=NOV)
            with eng.If(count > 0):
                eng.wait_ge(more_listed, 1)
                with eng.Fori(0, count) as j:
                    body(j, eng.value_load(ov_list[0:1, bass.ds(j + 1, 1)], min_val=0, max_val=E - 1))

        @block.sync
        def _(sp):
            for t in range(T):
                sp.dma_start(xs[:, t, :], x_rows[:, t, :]).then_inc(x_loaded[t], 16)

            def load(n, dst, src):
                sp.dma_start(dst, src).then_inc(ring_loaded[n % NSLOT], 16)

            for n in range(QKV_CHUNKS):
                if n >= NSLOT:
                    sp.wait_ge(proj_done, T * (n - NSLOT + 1))
                load(n, chunk_w(n), w_in[:, :, n * HALF:(n + 1) * HALF])
            for i in range(4):
                half, br = i // 2, i % 2
                n = L_GATE + i
                if i < NSLOT:
                    sp.wait_ge(proj_done, T * (n - NSLOT + 1))
                else:
                    sp.wait_ge(gate_done, T)
                c0 = GATE_COL0 + br * D + half * HALF
                load(n, chunk_w(n), w_in[:, :, c0:c0 + HALF])
                src, rows = ((wba, 2), (wbb, 4))[br]
                load(n, slot(n)[:, K * HALF:(K + rows) * HALF].rearrange("p (j n) -> p j n", j=rows),
                     src[:, :, half * HALF:(half + 1) * HALF])
            for i in range(2):
                sp.wait_ge(gate_done, T * (i + 2))
                load(L_OUT + i, chunk_w(L_OUT + i), w_out[:, :, i * HALF:(i + 1) * HALF])

            def load_ffn(n, gate, up, down, wait=True):
                w = slot(n)
                load(n, w[:, 0:K * FF], gate.rearrange("(p k) f -> p (k f)", k=K))
                load(n, w[:, K * FF:2 * K * FF], up.rearrange("(p k) f -> p (k f)", k=K))
                load(n, w[:, 2 * K * FF:], down.rearrange("(p c) d -> p (c d)", c=2))

            sp.wait_ge(gate_done, NM)
            load_ffn(L_SHARED, a["ws_gate"][0], a["ws_up"][0], a["ws_down"][0])

            def store_xn2(t):
                sp.wait_ge(xn2_ready, t + 1)
                sp.dma_start(xn2_t[:, t, :], xnorm[t % 2]).then_inc(xn2_stored[t % 2], 16)

            def load_expert(ex, free_sem, free_at):
                if free_sem is not None:
                    sp.wait_ge(free_sem, free_at)
                n = ex.n
                load_ffn(L_EXPERT + ex.c, pick(a["we_gate"][0], n), pick(a["we_up"][0], n),
                         pick(a["we_down"][0], n))

            def pick(w, n):
                if isinstance(n, int):
                    return w[n]
                return w[bass.ds(n, 1)].rearrange("o r c -> (o r) c")

            for t in range(T - 1):
                store_xn2(t)
            load_expert(Expert(0), out_done, 2 * T)
            store_xn2(T - 1)
            load_expert(Expert(1), out_done, 2 * T)
            load_expert(Expert(2), down_done, T)
            load_expert(Expert(3), down_done, T + 1)
            with sp.Fori(0, LOOPS) as i:
                for j in range(3):
                    ex = Expert(LOOP0 + j, i)
                    load_expert(ex, down_done, ex.n + (T - 2))
            for c in range(LAST0, E):
                load_expert(Expert(c), down_done, c + T - 2)

            def further(j, e):
                sp.wait_ge(down_done, j + (E + T))
                w = ring[:, 0:SLOT]
                for i, name in enumerate(("we_gate", "we_up")):
                    sp.dma_start(w[:, i * K * FF:(i + 1) * K * FF],
                                 pick(a[name][0], e).rearrange("(p k) f -> p (k f)", k=K)
                                 ).then_inc(ring_loaded[0], 16)
                sp.dma_start(w[:, 2 * K * FF:], pick(a["we_down"][0], e).rearrange("(p c) d -> p (c d)", c=2)
                             ).then_inc(ring_loaded[0], 16)
                sp.wait_ge(ov_scattered, 16 * j + 16)
                sp.sem_inc(more_ended, 1)

            further_blocks(sp, further)
            for b in range(3):
                sp.wait_ge(scattered[b], 16 * ((E - b + 2) // 3))
            for u in range(NC):
                t, half = divmod(u, 2)
                if u < NSLOT:
                    sp.wait_ge(down_done, E + T)
                else:
                    sp.wait_ge(rows_summed, u - NSLOT + 1)
                sp.dma_start(ring[:, (u % NSLOT) * SLOT:(u % NSLOT) * SLOT + TOPK * HALF]
                             .rearrange("p (c d) -> p c d", c=TOPK),
                             y_tok[:, t, :, half * HALF:(half + 1) * HALF]).then_inc(rows_loaded[u % NSLOT], 16)
                if u >= 2:
                    store_out(sp, u - 2)
            store_out(sp, NC - 2)
            store_out(sp, NC - 1)
            sp.wait_ge(out_stored, 16 * NC)

        @block.scalar
        def _(act_e):
            for dst, src in [
                (misc_t[:, :], a["misc"]), (g1c, a["norm1_g"].rearrange("o (p k) -> (o p) k", k=K)),
                (row_t[0:1, 0:64], a["q_norm_a"]), (row_t[0:1, 64:128], a["k_norm_a"]),
                (row_t[0:1, 128:192], a["q_norm_b"]), (row_t[0:1, 192:256], a["k_norm_b"]),
                (row_t[0:1, 256:320], a["router_bias"]),
            ]:
                act_e.dma_start(dst, src).then_inc(first_loaded, 16)
            for dst, src in [
                (pairs_t[:, 0:4 * T * HD], a["rope"]), (mask_t[:, :], a["masks"]), (wr, w_router),
                (g2c, a["norm2_g"].rearrange("o (p k) -> (o p) k", k=K)),
            ]:
                act_e.dma_start(dst, src).then_inc(second_loaded, 16)

            act_e.wait_ge(ones_ready, 1)
            for t in range(T):
                act_e.wait_ge(x_loaded[t], 16)
                nc.scalar.activation(junk1, xs[:, t, :], ACT.Square, accum_out=ssq[:, t:t + 1]).then_inc(act, 1)
                act_e.wait_ge(act, t + 1)
                nc.scalar.activation(std[:, t:t + 1], ssq[:, t:t + 1], ACT.Sqrt, bias=eps_c,
                                     scale=1.0 / D).then_inc(std1_ready, 1)

            def store_pairs(m):
                c, t = divmod(m, T)
                pr = CHUNKS[c]["pairs"]
                act_e.wait_ge(pairs_turned, m + 1)
                if m == 0:
                    act_e.wait_ge(tables_ready, 1)
                nc.scalar.copy(pairs[:, pr[0]:pr[0] + len(pr), t * P:(t + 1) * P],
                               bank(4 + m % 2, len(pr) * P).rearrange("p (j q) -> p j q", q=P)
                               ).then_inc(pairs_ready, 1)

            for m in range(NP):
                c, t = divmod(m, T)
                act_e.wait_ge(proj_done, m + 1)
                wait_for(act_e, sums_ready, m - 1)
                nc.scalar.activation(squares[m % 2], bank(m % 4).rearrange("p (h d) -> p h d", d=HD),
                                     ACT.Square).then_inc(squares_ready, 1)
                for c0, n, (br, g) in CHUNKS[c]["value"]:
                    dst = vA[:, t, g, :] if br == "A" else vB[:, t, :]
                    nc.scalar.copy(dst, bank(m % 4, n, c0))
                act_e.wait_ge(sums_ready, m + 1)
                wait_for(act_e, normed_ready, m - 1)
                nc.scalar.activation(hstd[m % 2], hss[m % 2], ACT.Sqrt, bias=eps_c,
                                     scale=1.0 / HD).then_inc(hstd_ready, 1)
                if m >= 1:
                    store_pairs(m - 1)
            store_pairs(NP - 1)

            for n in range(NU + 1):
                if n < NU:
                    a_unit, i = n % 3 == 0, n % 3
                    act_e.wait_ge(max_ready, n + 1)
                    wait_for(act_e, probs_turned, n - 2)
                    nc.scalar.activation(prob[i], prob[i] if a_unit else bank(1 + i), ACT.Exp, bias=neg_max[i],
                                         accum_out=den[i]).then_inc(probs_ready, 1)
                if n >= 1:
                    m = n - 1
                    act_e.wait_ge(probs_turned, m + 1)
                    wait_for(act_e, pv_done, m - 2)
                    nc.scalar.copy(probT[m % 3][:, 0:4, :],
                                   bank(5 if m % 3 == 2 else 4).rearrange("p (j q) -> p j q", q=P)
                                   ).then_inc(probT_act, 1)

            for m in range(NM):
                act_e.wait_ge(gate_done, m + 1)
                wait_for(act_e, product_ready, m - 1)
                nc.scalar.activation(gated[m % 2], bank(4 + 2 * (m % 2)), ACT.Sigmoid).then_inc(gated_ready, 1)
            for t in range(T):
                act_e.wait_ge(merged_turned, t + 1)
                b = 2 * (t % 2)
                nc.scalar.copy(xT[:, 0:4, t * P:(t + 1) * P], bank(b).rearrange("p (j q) -> p j q", q=P))
                nc.scalar.copy(xT[:, 4:8, t * P:(t + 1) * P],
                               bank(b + 1).rearrange("p (j q) -> p j q", q=P)).then_inc(mT_ready, 1)
            for t in range(T):
                act_e.wait_ge(h_ready, 2 * t + 2)
                nc.scalar.activation(junk2, xs[:, t, :], ACT.Square, accum_out=ssq2[:, t:t + 1]).then_inc(act, 1)
                act_e.wait_ge(act, T + t + 1)
                nc.scalar.activation(std2[:, t:t + 1], ssq2[:, t:t + 1], ACT.Sqrt, bias=eps_c,
                                     scale=1.0 / D).then_inc(std2_ready, 1)
            act_e.wait_ge(logits_done, 1)
            for i in range(2):
                act_e.wait_ge(xn2_stored[i], 16 * (T // 2))
            nc.scalar.activation(scores, bank(7, T * E).rearrange("p (t e) -> p t e", e=E),
                                 ACT.Sigmoid).then_inc(scores_ready, 1)

            def silu(u, m=CAP):
                act_e.wait_ge(gu_done, u + 1)
                wait_for(act_e, hid_ready, u)
                nc.scalar.activation(act_s[0:m], bank(2, FF)[0:m], ACT.Silu).then_inc(silu_ready, 1)

            def scale_rows(ex):
                act_e.wait_ge(down_done, ex.n + (T + 1))
                act_e.wait_ge(w_ready, ex.n + 1)
                wait_for(act_e, scattered[ex.buf], 16 * ex.third)
                nc.scalar.activation(y_s[ex.buf][0:CAP], bank2(4)[0:CAP], ACT.Copy,
                                     scale=w_b[0:CAP, ex.buf:ex.buf + 1]).then_inc(y_scaled, 1)

            for u in range(T):
                silu(u, P)
            silu(T)
            for c in range(1, LOOP0):
                silu(T + c)
                scale_rows(Expert(c - 1))
            with act_e.Fori(0, LOOPS) as i:
                for j in range(3):
                    ex = Expert(LOOP0 + j, i)
                    silu(ex.n + T)
                    scale_rows(ex.next(-1))
            for c in range(LAST0, E):
                silu(T + c)
                scale_rows(Expert(c - 1))
            scale_rows(Expert(E - 1))

            def further(j, e):
                silu(j + (E + T))
                act_e.wait_ge(down_done, j + (E + T + 1))
                nc.scalar.activation(y_s[0][0:CAP], bank2(4)[0:CAP], ACT.Copy,
                                     scale=w_b[0:CAP, 0:1]).then_inc(y_scaled, 1)

            further_blocks(act_e, further)

        @block.vector
        def _(v):
            step = Steps(v, dve)
            nc.vector.memset(ones_t[:, :], 1.0)
            nc.vector.memset(eps_c, EPS).then_inc(ones_ready, 1)
            v.wait_ge(gains_ps, 1)
            for i, f in enumerate((0.125, 1.0, 0.125, 1.0)):
                nc.vector.tensor_scalar(gains[:, i, :], bank(7, HD, i * HD), f, None, ALU.mult)
            nc.vector.tensor_copy(bias_b, bank(7, E, 4 * HD)).then_inc(gains_ready, 1)
            nc.vector.tensor_copy(below_b, below_f)
            step.done(nc.vector.memset(ones_b, 1.0))

            def spread(col, n, w):
                return col.unsqueeze(2).to_broadcast([P, n, w])

            def norm_rows(t, std_sem, std_c, rstd_c, waits):
                v.wait_ge(std_sem, t + 1)
                step.done(nc.vector.reciprocal(rstd_c[:, t:t + 1], std_c[:, t:t + 1]))
                step.wait()
                for s_, n_ in waits:
                    wait_for(v, s_, n_)
                return nc.vector.tensor_scalar(xnorm[t % 2], xs[:, t, :], rstd_c[:, t:t + 1], None, ALU.mult)

            def store_turned(t, src0, gain, dst):
                for h in range(2):
                    ins = nc.vector.tensor_tensor(
                        dst[:, 4 * h:4 * h + 4, t * P:(t + 1) * P],
                        bank(src0 + h).rearrange("p (j q) -> p j q", q=P),
                        spread(gain[:, 4 * h:4 * h + 4], 4, P), ALU.mult)
                return ins

            v.wait_ge(first_loaded, 16 * 7)
            for t in range(T + 1):
                if t < T:
                    norm_rows(t, std1_ready, std, rstd, [(xn_turned, t - 1)]).then_inc(xn_ready, 1)
                if t >= 1:
                    v.wait_ge(xn_turned, t)
                    store_turned(t - 1, 2 * ((t - 1) % 2), g1c, xT).then_inc(xT_ready, 1)

            for m in range(NP):
                c, t = divmod(m, T)
                b = m % 2
                v.wait_ge(squares_ready, m + 1)
                nc.vector.tensor_reduce(hss[b], squares[b], AXIS.X, ALU.add).then_inc(sums_ready, 1)
                v.wait_ge(hstd_ready, m + 1)
                step.done(nc.vector.reciprocal(hrstd[b], hstd[b]))
                step.wait()
                wait_for(v, cos_done, m - 1)
                nc.vector.tensor_tensor(normed[b], bank(m % 4).rearrange("p (h d) -> p h d", d=HD),
                                        spread(hrstd[b], 8, HD), ALU.mult).then_inc(normed_ready, 1)
                v.wait_ge(normed_ready, m + 1)
                if m == 0:
                    v.wait_ge(tables_ready, 1)
                heads = 0
                for kind, c0, n, o0, copies in CHUNKS[c]["norm"]:
                    blocks = 1 if kind in (QA, KA) else 2
                    hw = HD // (2 * blocks)
                    src = normed[b][:, c0 // HD:c0 // HD + n, :].rearrange("p h (b s x) -> p h b s x", b=blocks, s=2)
                    tab = sing[kind][:, t, :].rearrange("p (b s x) -> p b s x", b=blocks, s=2)
                    for cp in range(copies):
                        dst = turned[b][:, o0 + cp:o0 + cp + copies * (n - 1) + 1:copies, :].rearrange(
                            "p h (b s x) -> p h b s x", b=blocks, s=2)
                        for s_ in range(2):
                            if blocks == 1:
                                last = nc.vector.tensor_tensor(
                                    dst[:, :, 0, s_, :], src[:, :, 0, 1 - s_, :],
                                    tab[:, 0, s_, :].unsqueeze(1).to_broadcast([P, n, hw]), ALU.mult)
                            else:
                                last = nc.vector.tensor_tensor(
                                    dst[:, :, :, s_, :], src[:, :, :, 1 - s_, :],
                                    tab[:, :, s_, :].unsqueeze(1).to_broadcast([P, n, blocks, hw]), ALU.mult)
                    heads = o0 + n * copies
                step.done(last)
                step.wait()
                v.wait_ge(cos_done, m + 1)
                nc.vector.tensor_tensor(rotated[b][:, 0:heads, :], rotated[b][:, 0:heads, :],
                                        turned[b][:, 0:heads, :], ALU.add).then_inc(rotated_ready, 1)

            for n in range(NU + 3):
                if n < NU:
                    br, t, h = UNITS[n]
                    i = n % 3
                    v.wait_ge(scores_done, n + 1)
                    if br == "A":
                        wait_for(v, probs_turned, n - 2)
                        if n == 0:
                            v.wait_ge(second_loaded, 16 * 4)
                        nc.vector.tensor_tensor_reduce(
                            out=prob[0][:, 0:HALF], in0=bank(0), in1=band[:, (3 - t) * P:(7 - t) * P],
                            scale=1.0, scalar=-3.0e38, op0=ALU.add, op1=ALU.max, accum_out=pmax[0])
                        step.done(nc.vector.tensor_tensor_reduce(
                            out=prob[0][:, HALF:768], in0=bank(1, 256), in1=strided_mask,
                            scale=1.0, scalar=-3.0e38, op0=ALU.add, op1=ALU.max, accum_out=pmax[1]))
                        step.wait()
                        nc.vector.tensor_scalar(neg_max[0], pmax[0], pmax[1], -1.0,
                                                ALU.max, ALU.mult).then_inc(max_ready, 1)
                    else:
                        wait_for(v, probs_ready, n - 2)
                        nc.vector.tensor_reduce(neg_max[i], bank(1 + i), AXIS.X, ALU.max,
                                                negate=True).then_inc(max_ready, 1)
                if 1 <= n <= NU:
                    m = n - 1
                    i = m % 3
                    v.wait_ge(probs_ready, m + 1)
                    step.done(nc.vector.reciprocal(rden[i], den[i]))
                    step.wait()
                    nc.vector.tensor_scalar(prob[i], prob[i], rden[i], None, ALU.mult).then_inc(probs_scaled, 1)
                if 2 <= n <= NU + 1 and (n - 2) % 3 == 0:
                    m = n - 2
                    v.wait_ge(probs_turned, m + 1)
                    wait_for(v, pv_done, m - 2)
                    nc.vector.tensor_copy(probT[0][:, 4:6, :], bank(5, 2 * P).rearrange("p (j q) -> p j q", q=P)
                                          ).then_inc(probT_dve, 1)
                if n >= 3:
                    m = n - 3
                    br, t, h = UNITS[m]
                    if h % 2:
                        v.wait_ge(pv_done, m + 1)
                        j, b, ready = (h // 2, 7, yT_a_ready) if br == "A" else (2 + h // 2, 6, yT_b_ready)
                        nc.vector.tensor_copy(yT[:, j, t * P:(t + 1) * P], bank(b, P)).then_inc(ready, 1)

            for m in range(NM):
                hb, t = divmod(m, T)
                half, br = divmod(hb, 2)
                v.wait_ge(gated_ready, m + 1)
                if br == 0:
                    dst = merged[:, t, half * HALF:(half + 1) * HALF]
                else:
                    i = half * T + t
                    wait_for(v, merged_ready, i - 1)
                    dst = gatedB[i % 2]
                nc.vector.tensor_tensor(dst, gated[m % 2], bank(5 + 2 * (m % 2)), ALU.mult).then_inc(product_ready, 1)
            for o in range(2 * T):
                t, half = divmod(o, 2)
                v.wait_ge(out_done, o + 1)
                x_part = xs[:, t, half * HALF:(half + 1) * HALF]
                nc.vector.tensor_tensor(x_part, x_part, bank(4 + o % 4), ALU.add).then_inc(h_ready, 1)
            for t in range(T + 1):
                if t < T:
                    norm_rows(t, std2_ready, std2, rstd2,
                              [(x2_turned, t - 1), (xn2_stored[t % 2], 16 * (t // 2))]).then_inc(xn2_ready, 1)
                if t >= 1:
                    v.wait_ge(x2_turned, t)
                    store_turned(t - 1, 2 * ((t - 1) % 2), g2c, x2T).then_inc(x2T_ready, 1)

            def group(x):
                return x.rearrange("p t (g e) -> p t g e", e=8)

            def route_a():
                v.wait_ge(scores_ready, 1)
                for i in range(2):
                    v.wait_ge(xn2_stored[i], 16 * (T // 2))
                step.done(nc.vector.tensor_tensor(sel, scores, bias_b.unsqueeze(1).to_broadcast([P, T, E]), ALU.add))
                nc.vector.memset(gs16, MASKED)
                nc.vector.memset(low_ones, 1.0)
                step.done(nc.vector.memset(low, 1.0))
                step.wait()
                for t in range(T):
                    for g in range(EG):
                        ins = nc.vector.max(out=m8[:, t, g, :], in_=sel[:, t, 8 * g:8 * g + 8])
                step.done(ins)
                step.wait()
                step.done(nc.vector.tensor_tensor(gs16[:, :, 0:EG], m8[:, :, :, 0], m8[:, :, :, 1], ALU.add))
                step.wait()

            def route_b():
                for t in range(T):
                    ins = nc.vector.max(out=gm8[:, t, :], in_=gs16[:, t, :])
                step.done(ins)
                step.wait()
                step.done(nc.vector.memset(gm8[:, :, TOPG:8], MASKED))
                step.wait()
                for t in range(T):
                    ins = nc.vector.match_replace(out=gr16[:, t, :], in_to_replace=gm8[:, t, :],
                                                  in_values=gs16[:, t, :], imm_value=2 * MASKED)
                step.done(ins)
                step.wait()
                step.done(nc.vector.tensor_tensor(gmask, gr16[:, :, 0:EG], gs16[:, :, 0:EG], ALU.not_equal))
                step.wait()
                nc.vector.tensor_scalar(gpen, gmask, -MASKED, MASKED, ALU.mult, ALU.add)
                step.done(nc.vector.tensor_tensor(group(selm), group(sel),
                                                  gmask.unsqueeze(3).to_broadcast([P, T, EG, 8]), ALU.mult))
                step.wait()
                step.done(nc.vector.tensor_tensor(group(selm), group(selm),
                                                  gpen.unsqueeze(3).to_broadcast([P, T, EG, 8]), ALU.add))
                step.wait()
                for t in range(T):
                    ins = nc.vector.max(out=top8[:, t, :], in_=selm[:, t, :])
                step.done(ins)
                step.wait()
                for t in range(T):
                    ins = nc.vector.match_replace(out=repl[:, t, :], in_to_replace=top8[:, t, :],
                                                  in_values=selm[:, t, :], imm_value=3 * MASKED)
                step.done(ins)
                step.wait()
                step.done(nc.vector.tensor_tensor(mask, repl, selm, ALU.not_equal))
                step.wait()
                nc.vector.tensor_copy(maskb, mask).then_inc(mask_ready, 1)

            def route_c():
                step.done(nc.vector.tensor_tensor(wts, scores, mask, ALU.mult))
                step.wait()
                step.done(nc.vector.tensor_reduce(wsum, wts, AXIS.X, ALU.add))
                step.wait()
                step.done(nc.vector.reciprocal(wrec, wsum))
                step.wait()
                step.done(nc.vector.tensor_scalar(wrec, wrec, ROUTED_SCALE, None, ALU.mult))
                for t in range(T):
                    ins = nc.vector.tensor_tensor_scan(rank[:, t, :], low[:, t, :], mask[:, t, :], 0.0,
                                                       ALU.mult, ALU.add)
                step.done(ins)
                step.wait()
                nc.vector.tensor_tensor(rank, rank, mask, ALU.subtract)
                step.done(nc.vector.tensor_tensor(wts, wts, spread(wrec, T, E), ALU.mult))
                step.wait()

            def route_d():
                for t in range(T):
                    nc.vector.tensor_copy(moving[:, t, :, 0:6],
                                          place_parts[:, t, :].unsqueeze(1).to_broadcast([P, E, 6]))
                step.done(nc.vector.tensor_copy(moving[:, :, :, 6], wts))
                step.wait()
                nc.vector.tensor_tensor(moving[:, :, :, 3], moving[:, :, :, 3], rank, ALU.add)
                step.done(nc.vector.tensor_tensor(low, wts, moving[:, :, :, 6], ALU.subtract))
                step.wait()
                step.done(nc.vector.tensor_copy(moving[:, :, :, 7], low))
                step.wait()
                step.done(nc.vector.tensor_tensor(tmp_w, low, moving[:, :, :, 7], ALU.subtract))
                step.wait()
                step.done(nc.vector.tensor_copy(moving[:, :, :, 8], tmp_w))
                step.wait()
                step.done(nc.vector.tensor_scalar(pos, mask, -4096.0, 4096.0, ALU.mult, ALU.add))
                step.wait()
                v.wait_ge(pos_done, 1)
                nc.vector.tensor_tensor(pos, pos, bank(7, T * E).rearrange("p (t e) -> p t e", e=E),
                                        ALU.add)
                nc.vector.tensor_copy(cnt, bank(7, E, T * E)).then_inc(moving_ready, 1)

            def product(u, m=CAP):
                v.wait_ge(silu_ready, u + 1)
                wait_for(v, hid_turned, u)
                nc.vector.tensor_tensor(h_s[0:m], act_s[0:m], bank(2, FF, FF)[0:m], ALU.mult).then_inc(hid_ready, 1)

            def store_hidT(u, m=CAP):
                v.wait_ge(hid_turned, u + 1)
                wait_for(v, down_done, u)
                nc.vector.tensor_copy(hT_s[:, :, 0:m], bank(3, FF).rearrange("p (c q) -> p c q", q=P)[:, :, 0:m]
                                      ).then_inc(hidT_ready, 1)

            def add_shared(u):
                v.wait_ge(down_done, u + 1)
                nc.vector.tensor_tensor(xs[:, u, :], xs[:, u, :], bank2(4), ALU.add).then_inc(shared_added, 1)

            for u, part in enumerate((route_a, route_b, route_c, route_d)):
                if u == 0:
                    part()
                product(u, P)
                if u >= 1:
                    add_shared(u - 1)
                    part()
                store_hidT(u, P)
            add_shared(T - 1)
            v.wait_ge(moving_ready, 1)
            step.done(nc.vector.tensor_scalar(more_f, cnt, float(CAP), None, ALU.is_gt))
            for q in range(2, BLOCKS):
                step.wait()
                step.done(nc.vector.scalar_tensor_tensor(out=more_f, in0=cnt, scalar=float(CAP * q), in1=more_f,
                                                         op0=ALU.is_gt, op1=ALU.add))
            step.wait()
            step.done(nc.vector.tensor_reduce(ov_num, more_f, AXIS.X, ALU.add))
            step.wait()
            nc.vector.tensor_copy(ov_list[:, 0:1], ov_num).then_inc(more_counted, 1)

            def slots(x):
                return x[0:CAP]

            def one_hot(ex):
                wait_for(v, placed_done, ex.n - 2)
                nc.vector.tensor_tensor(onehot[ex.buf], slot_row[:, 0:CAP].unsqueeze(1).to_broadcast([P, T, CAP]),
                                        pos[:, :, bass.ds(ex.n, 1)].to_broadcast([P, T, CAP]),
                                        ALU.is_equal).then_inc(onehot_ready, 1)

            def store_places(ex):
                v.wait_ge(placed_done, ex.n + 1)
                nc.vector.tensor_reduce(slots(placed[:, bass.ds(ex.n, 1), :]).rearrange("p o c -> p (o c)"),
                                        slots(bank(6, 9)).rearrange("p (c j) -> p c j", j=3), AXIS.X, ALU.add
                                        ).then_inc(parts_summed, 1)
                v.wait_ge(parts_summed, ex.n + 1)
                nc.vector.tensor_scalar(slots(placed_i[:, bass.ds(ex.n, 1), :]), slots(placed[:, bass.ds(ex.n, 1), 0:2]),
                                        float(AWAY), None, ALU.add).then_inc(index_ready, 1)

            AHEAD = 4
            for c in range(3):
                one_hot(Expert(c))
            for c in range(AHEAD + 1):
                store_places(Expert(c))
                if c + 3 < AHEAD + 1:
                    one_hot(Expert(c + 3))

            def store_gT(ex):
                v.wait_ge(g_turned, ex.n + 1)
                wait_for(v, gu_done, ex.n + (T - 2))
                for h in range(2):
                    ins = nc.vector.tensor_tensor(
                        xgT[ex.buf][:, 4 * h:4 * h + 4, :],
                        bank(h).rearrange("p (j q) -> p j q", q=P)[:, :, 0:CAP],
                        spread(g2c[:, 4 * h:4 * h + 4], 4, CAP), ALU.mult)
                ins.then_inc(gT_ready, 1)

            def slot_weight(ex):
                wait_for(v, y_scaled, ex.n - 2)
                nc.vector.tensor_copy(w_b[0:CAP, ex.buf:ex.buf + 1],
                                      placed[0:CAP, bass.ds(ex.n, 1), 2]).then_inc(w_ready, 1)

            store_gT(Expert(0))
            store_gT(Expert(1))
            slot_weight(Expert(0))
            product(T)

            def turn(ex):
                if ex.i is not None or ex.c + 1 < E:
                    store_gT(ex.next(1))
                store_hidT(ex.n + (T - 1))
                ahead = ex.i is not None or ex.c + AHEAD < E
                if ahead:
                    one_hot(ex.next(AHEAD))
                slot_weight(ex)
                product(ex.n + T)
                if ahead:
                    store_places(ex.next(AHEAD))
            for c in range(1, LOOP0):
                turn(Expert(c))
            with v.Fori(0, LOOPS) as i:
                for j in range(3):
                    turn(Expert(LOOP0 + j, i))
            for c in range(LAST0, E):
                turn(Expert(c))
            store_hidT(T + E - 1)

            def list_further():
                v.wait_ge(g_turned, E)
                for b in range(3):
                    v.wait_ge(scattered[b], 16 * ((E - b + 2) // 3))
                v.wait_ge(y_scaled, E)
                step.done(nc.vector.memset(ov_x, 1.0))
                step.wait()
                step.done(nc.vector.tensor_tensor_scan(upto_f, low_ones, more_f, 0.0, ALU.mult, ALU.add))
                step.done(nc.vector.tensor_tensor_scan(ov_base, ov_x, ov_x, -1.0, ALU.mult, ALU.add))
                step.wait()
                step.done(nc.vector.tensor_tensor(le_f, upto_f.unsqueeze(1).to_broadcast([P, NOV, E]),
                                                  ov_base.unsqueeze(2).to_broadcast([P, NOV, E]), ALU.is_le))
                step.wait()
                step.done(nc.vector.tensor_reduce(ov_e, le_f, AXIS.X, ALU.add))
                step.wait()
                step.done(nc.vector.tensor_tensor(le_f, le_f, upto_f.unsqueeze(1).to_broadcast([P, NOV, E]),
                                                  ALU.mult))
                nc.vector.tensor_scalar(ov_e, ov_e, float(E - 1), None, ALU.min)
                step.wait()
                step.done(nc.vector.tensor_reduce(ov_x, le_f, AXIS.X, ALU.max))
                step.wait()
                step.done(nc.vector.tensor_tensor(ov_base, ov_base, ov_x, ALU.subtract))
                step.wait()
                step.done(nc.vector.tensor_scalar(ov_base, ov_base, 1.0, float(CAP), ALU.add, ALU.mult))
                nc.vector.tensor_copy(ov_list[:, 1:NOV + 1], ov_e).then_inc(more_listed, 1)

            def further(j, e):
                def in_order(ins, k, of):
                    ins.then_inc(further_step, 1)
                    v.wait_ge(further_step, of * j + k)
                FS = 2
                in_order(nc.vector.tensor_scalar(ov_pos, pos[:, :, bass.ds(e, 1)].rearrange("p t o -> p (t o)"), ov_base[:, bass.ds(j, 1)], None,
                                                 ALU.subtract), 1, FS)
                nc.vector.tensor_tensor(onehot[0], slot_row[:, 0:CAP].unsqueeze(1).to_broadcast([P, T, CAP]),
                                        ov_pos.unsqueeze(2).to_broadcast([P, T, CAP]),
                                        ALU.is_equal).then_inc(ov_onehot, 1)
                v.wait_ge(ov_placed, j + 1)
                in_order(nc.vector.tensor_reduce(slots(ov_placed3), slots(bank(6, 9)).rearrange("p (c j) -> p c j", j=3),
                                                 AXIS.X, ALU.add), 2, FS)
                nc.vector.tensor_copy(slots(w_b[:, 0:1]), slots(ov_placed3[:, 2:3]))
                nc.vector.tensor_scalar(slots(tok_b[:, 0:1]), slots(ov_placed3[:, 0:1]), float(AWAY), None, ALU.add)
                nc.vector.tensor_scalar(slots(dst_b[:, 0:1]), slots(ov_placed3[:, 1:2]), float(AWAY), None,
                                        ALU.add).then_inc(ov_indexed, 1)
                v.wait_ge(g_turned, j + (E + 1))
                for h in range(2):
                    ins = nc.vector.tensor_tensor(
                        xgT[0][:, 4 * h:4 * h + 4, :], bank(h).rearrange("p (j q) -> p j q", q=P)[:, :, 0:CAP],
                        spread(g2c[:, 4 * h:4 * h + 4], 4, CAP), ALU.mult)
                ins.then_inc(gT_ready, 1)
                product(j + (E + T))
                store_hidT(j + (E + T))
                v.wait_ge(ov_scattered, 16 * j + 16)

            count = v.value_load(ov_list[0:1, 0:1], min_val=0, max_val=NOV)
            with v.If(count > 0):
                list_further()
                v.wait_ge(more_listed, 1)
                with v.Fori(0, count) as j:
                    further(j, v.value_load(ov_list[0:1, bass.ds(j + 1, 1)], min_val=0, max_val=E - 1))

            for u in range(NC):
                t, half = divmod(u, 2)
                v.wait_ge(rows_loaded[u % NSLOT], 16 * (u // NSLOT + 1))
                rows = ring[:, (u % NSLOT) * SLOT:(u % NSLOT) * SLOT + TOPK * HALF]
                red = view(xT_t, (u % 2) * HALF, HALF)
                nc.vector.tensor_reduce(red, rows.rearrange("p (c d) -> p d c", c=TOPK), AXIS.X, ALU.add
                                        ).then_inc(rows_summed, 1)
                v.wait_ge(rows_summed, u + 1)
                x_part = xs[:, t, half * HALF:(half + 1) * HALF]
                nc.vector.tensor_tensor(x_part, x_part, red, ALU.add).then_inc(out_ready, 1)

        @block.gpsimd
        def _(g):
            g.wait_ge(second_loaded, 16 * 4)
            g.wait_ge(gains_ready, 1)
            for kind in range(4):
                cos_r, sin_r = rope_raw[2 * (kind // 2)], rope_raw[2 * (kind // 2) + 1]
                blocks = 1 if kind in (QA, KA) else 2
                hw = HD // (2 * blocks)
                nc.gpsimd.tensor_tensor(cosg[kind], cos_r, gains[:, kind, :].unsqueeze(1).to_broadcast([P, T, HD]),
                                        ALU.mult)
                for b in range(blocks):
                    for s_ in range(2):
                        o, i = (2 * b + s_) * hw, (2 * b + 1 - s_) * hw
                        last = nc.gpsimd.tensor_tensor(
                            sing[kind][:, :, o:o + hw], sin_r[:, :, o:o + hw],
                            gains[:, kind, i:i + hw].unsqueeze(1).to_broadcast([P, T, hw]), ALU.mult)
            last.then_inc(tables_ready, 1)
            g.wait_ge(tables_ready, 1)
            for m in range(NP):
                c, t = divmod(m, T)
                b = m % 2
                g.wait_ge(normed_ready, m + 1)
                wait_for(g, pairs_turned, m - 1)
                for kind, c0, n, o0, copies in CHUNKS[c]["norm"]:
                    for cp in range(copies):
                        last = nc.gpsimd.tensor_tensor(
                            rotated[b][:, o0 + cp:o0 + cp + copies * (n - 1) + 1:copies, :],
                            normed[b][:, c0 // HD:c0 // HD + n, :],
                            cosg[kind][:, t, :].unsqueeze(1).to_broadcast([P, n, HD]), ALU.mult)
                last.then_inc(cos_done, 1)
            for i in range(2 * T):
                half, t = divmod(i, T)
                g.wait_ge(product_ready, (2 * half + 1) * T + t + 1)
                part = merged[:, t, half * HALF:(half + 1) * HALF]
                nc.gpsimd.tensor_tensor(part, part, gatedB[i % 2], ALU.add).then_inc(merged_ready, 1)

            step = Steps(g, pool)
            g.wait_ge(std2_ready, T)
            for b in range(3):
                last = nc.gpsimd.memset(xg[b], 0.0)
            step.done(last)
            step.wait()
            for i in range(2):
                g.wait_ge(xn2_stored[i], 16 * (T // 2))
            last_token, last_row = g.to_reg(S - 1), g.to_reg(S * TOPK - 1)
            def gather(ex):
                wait_for(g, g_turned, ex.n - 2)
                g.wait_ge(index_ready, ex.n + 1)
                nc.gpsimd.tensor_copy(tok_b[0:CAP, ex.buf:ex.buf + 1],
                                      placed_i[0:CAP, bass.ds(ex.n, 1), 0]).then_inc(tok_copied, 1)
                g.wait_ge(tok_copied, ex.n + 1)
                g.sem_inc(pool_waited, 1)
                nc.gpsimd.indirect_dma_start(
                    out=xg[ex.buf][0:CAP], out_offset=None, in_=xn2_rows[:, :],
                    in_offset=bass.IndirectOffsetOnAxis(ap=tok_b[0:CAP, ex.buf:ex.buf + 1], axis=0),
                    bounds_check=last_token, oob_is_err=False).then_inc(gathered[ex.buf], 16)

            def scatter(ex):
                g.wait_ge(y_scaled, ex.n + 1)
                wait_for(g, scattered[ex.buf], 16 * ex.third)
                nc.gpsimd.tensor_copy(dst_b[0:CAP, ex.buf:ex.buf + 1],
                                      placed_i[0:CAP, bass.ds(ex.n, 1), 1]).then_inc(dst_copied, 1)
                g.wait_ge(dst_copied, ex.n + 1)
                g.sem_inc(pool_waited, 1)
                nc.gpsimd.indirect_dma_start(
                    out=y_rows[:, :],
                    out_offset=bass.IndirectOffsetOnAxis(ap=dst_b[0:CAP, ex.buf:ex.buf + 1], axis=0),
                    in_=y_s[ex.buf][0:CAP], in_offset=None,
                    bounds_check=last_row, oob_is_err=False).then_inc(scattered[ex.buf], 16)

            for c in range(3):
                gather(Expert(c))
            gather(Expert(3))
            for c in range(1, LOOP0):
                gather(Expert(c + 3))
                scatter(Expert(c - 1))
            with g.Fori(0, LOOPS) as i:
                for j in range(3):
                    ex = Expert(LOOP0 + j, i)
                    gather(ex.next(3))
                    scatter(ex.next(-1))
            for c in range(LAST0, E):
                if c + 3 < E:
                    gather(Expert(c + 3))
                scatter(Expert(c - 1))
            scatter(Expert(E - 1))

            def further(j, e):
                g.wait_ge(ov_indexed, j + 1)
                g.sem_inc(pool_waited, 1)
                nc.gpsimd.indirect_dma_start(
                    out=xg[0][0:CAP], out_offset=None, in_=xn2_rows[:, :],
                    in_offset=bass.IndirectOffsetOnAxis(ap=tok_b[0:CAP, 0:1], axis=0),
                    bounds_check=last_token, oob_is_err=False).then_inc(ov_gathered, 16)
                g.wait_ge(y_scaled, j + (E + 1))
                g.sem_inc(pool_waited, 1)
                nc.gpsimd.indirect_dma_start(
                    out=y_rows[:, :], out_offset=bass.IndirectOffsetOnAxis(ap=dst_b[0:CAP, 0:1], axis=0),
                    in_=y_s[0][0:CAP], in_offset=None,
                    bounds_check=last_row, oob_is_err=False).then_inc(ov_scattered, 16)
                g.wait_ge(ov_scattered, 16 * j + 16)

            further_blocks(g, further)

        @block.tensor
        def _(pe):
            mm, turn_to = nc.tensor.matmul, nc.tensor.transpose
            pe.wait_ge(ones_ready, 1)
            pe.wait_ge(first_loaded, 16 * 7)
            mm(bank(7, 4 * HD + E), ones_t[0:1, :], row_t[0:1, :], start=True, stop=True).then_inc(gains_ps, 1)

            def turn_rows(rows, b0, m=P):
                for k in range(K):
                    ins = turn_to(bank(b0 + k // 4, m, (k % 4) * P), rows[0:m, k:D:K], ident[0:m, 0:m])
                return ins

            for t in range(T):
                pe.wait_ge(xn_ready, t + 1)
                wait_for(pe, xT_ready, t - 1)
                turn_rows(xnorm[t % 2], 2 * (t % 2)).then_inc(xn_turned, 1)

            def turn_pairs(m):
                c, t = divmod(m, T)
                pe.wait_ge(rotated_ready, m + 1)
                wait_for(pe, pairs_ready, m - 1)
                if m == 0:
                    pe.wait_ge(gains_ready, 1)
                flat = rotated[m % 2].rearrange("p h d -> p (h d)")
                for j in range(len(CHUNKS[c]["pairs"])):
                    ins = turn_to(bank(4 + m % 2, P, j * P), flat[:, j * P:(j + 1) * P], ident)
                ins.then_inc(pairs_turned, 1)

            for m in range(NP):
                c, t = divmod(m, T)
                if t == 0:
                    wait_load(pe, c)
                if m == 0:
                    pe.wait_ge(xT_ready, T)
                wait_for(pe, normed_ready, m - 3)
                for k in range(K):
                    ins = mm(bank(m % 4), xT[:, k, t * P:(t + 1) * P], chunk_w(c)[:, k, :],
                             start=(k == 0), stop=(k == K - 1))
                ins.then_inc(proj_done, 1)
                if m >= 1:
                    turn_pairs(m - 1)
            turn_pairs(NP - 1)

            def score(n):
                br, t, h = UNITS[n]
                wait_for(pe, probs_ready, n - 2)
                r = HD * (h % 2)
                b0 = (0, 2, 3)[n % 3]
                rows = slice(r, r + HD)
                own = slice(t * P, (t + 1) * P)
                if br == "A":
                    mm(bank(b0), pairs[rows, q_pair(0, h), own], pairs[rows, k_pair(0, h), :], start=True, stop=True)
                    for g in (1, 2):
                        ins = mm(bank(b0 + 1, P, (g - 1) * P), pairs[rows, q_pair(g, h), own],
                                 pairs[rows, k_pair(g, h), own], start=True, stop=True)
                else:
                    ins = mm(bank(b0), pairs[rows, PAIR_QB + h // 2, own],
                             pairs[rows, PAIR_KB + h // (HB // HKV), :], start=True, stop=True)
                ins.then_inc(scores_done, 1)

            def turn_probs(n):
                i = n % 3
                pe.wait_ge(probs_scaled, n + 1)
                wait_for(pe, probT_act, n)
                wait_for(pe, probT_dve, (n + 2) // 3)
                for j in range(6 if i == 0 else 4):
                    b = 5 if i == 2 else 4 + j // 4
                    ins = turn_to(bank(b, P, (j % 4) * P), prob[i][:, j * P:(j + 1) * P], ident)
                ins.then_inc(probs_turned, 1)

            def weigh(n):
                br, t, h = UNITS[n]
                pe.wait_ge(probT_act, n + 1)
                if br == "A":
                    pe.wait_ge(probT_dve, n // 3 + 1)
                    if h % 2 == 0:
                        wait_for(pe, yT_a_ready, n // 6)
                elif h % 2 == 0:
                    wait_for(pe, yT_b_ready, n // 3)
                hs = slice(h * HD, (h + 1) * HD)
                if br == "A":
                    vals = [vA[:, u, 0, hs] for u in range(T)] + [vA[:, t, 1, hs], vA[:, t, 2, hs]]
                else:
                    kv = h // (HB // HKV)
                    vals = [vB[:, u, kv * HD:(kv + 1) * HD] for u in range(T)]
                r = HD * (h % 2)
                for j, val in enumerate(vals):
                    ins = mm(bank(7 if br == "A" else 6, P)[r:r + HD], val, probT[n % 3][:, j, :],
                             start=(j == 0), stop=(j == len(vals) - 1))
                ins.then_inc(pv_done, 1)

            pe.wait_ge(pairs_ready, NP)
            score(0)
            score(1)
            for n in range(NU + 1):
                if n + 2 < NU:
                    score(n + 2)
                if n < NU:
                    turn_probs(n)
                if n >= 1:
                    weigh(n - 1)

            for m in range(NM):
                hb, t = divmod(m, T)
                half, br = divmod(hb, 2)
                n = L_GATE + hb
                if t == 0:
                    wait_load(pe, n)
                wait_for(pe, product_ready, m - 1)
                bg = 4 + 2 * (m % 2)
                for k in range(K):
                    mm(bank(bg), xT[:, k, t * P:(t + 1) * P], chunk_w(n)[:, k, :], start=(k == 0), stop=(k == K - 1))
                if m == 0:
                    pe.wait_ge(yT_a_ready, T * HA // 2)
                    pe.wait_ge(yT_b_ready, T * HB // 2)
                wb = slot(n)[:, K * HALF:]
                js = range(0, 2) if br == 0 else range(2, 6)
                for j in js:
                    ins = mm(bank(bg + 1), yT[:, j, t * P:(t + 1) * P], wb[:, (j - js[0]) * HALF:(j - js[0] + 1) * HALF],
                             start=(j == js[0]), stop=(j == js[-1]))
                ins.then_inc(gate_done, 1)
            for t in range(T + 1):
                if t < T:
                    pe.wait_ge(merged_ready, T + t + 1)
                    wait_for(pe, mT_ready, t - 1)
                    turn_rows(merged[:, t, :], 2 * (t % 2)).then_inc(merged_turned, 1)
                if t == 1:
                    pe.wait_ge(product_ready, NM)
                if t >= 1:
                    pe.wait_ge(mT_ready, t)
                    for half in range(2):
                        o = 2 * (t - 1) + half
                        if t == 1:
                            wait_load(pe, L_OUT + half)
                        wait_for(pe, h_ready, o - 3)
                        for k in range(K):
                            ins = mm(bank(4 + o % 4), xT[:, k, (t - 1) * P:t * P], chunk_w(L_OUT + half)[:, k, :],
                                     start=(k == 0), stop=(k == K - 1))
                        ins.then_inc(out_done, 1)
            for t in range(T):
                pe.wait_ge(xn2_ready, t + 1)
                wait_for(pe, x2T_ready, t - 1)
                turn_rows(xnorm[t % 2], 2 * (t % 2)).then_inc(x2_turned, 1)
            pe.wait_ge(x2T_ready, T)
            pe.wait_ge(h_ready, 2 * T)
            pe.wait_ge(second_loaded, 16 * 4)
            for t in range(T):
                for k in range(K):
                    ins = mm(bank(7, E, t * E), x2T[:, k, t * P:(t + 1) * P], wr[:, k, :],
                             start=(k == 0), stop=(k == K - 1))
            ins.then_inc(logits_done, 1)

            def gate_up(u, lhs, s, m=CAP):
                wait_for(pe, hid_ready, u)
                w, _ = ffn_parts(s)
                for k in range(K):
                    ins = mm(bank(2)[0:m].rearrange("p (s f) -> p s f", s=2), lhs(k), w[:, :, k, :],
                             start=(k == 0), stop=(k == K - 1))
                ins.then_inc(gu_done, 1)

            def turn_hidden(u, m=CAP):
                pe.wait_ge(hid_ready, u + 1)
                wait_for(pe, hidT_ready, u)
                for c in range(2):
                    ins = turn_to(bank(3, m, c * P), h_s[0:m, c:FF:2], ident[0:m, 0:m])
                ins.then_inc(hid_turned, 1)

            def down(u, s, m=CAP):
                pe.wait_ge(hidT_ready, u + 1)
                _, w = ffn_parts(s)
                for half in range(2):
                    for c in range(2):
                        ins = mm(bank(4 + half)[0:m], hT_s[:, c, 0:m], w[:, c, half * HALF:(half + 1) * HALF],
                                 start=(c == 0), stop=(c == 1))
                ins.then_inc(down_done, 1)

            wait_load(pe, L_SHARED)
            s = L_SHARED % NSLOT
            for u in range(T):
                if u >= 1:
                    turn_hidden(u - 1, P)
                gate_up(u, lambda k: x2T[:, k, u * P:(u + 1) * P], s, P)
                if u == T - 1:
                    pe.wait_ge(mask_ready, 1)
                    for t in range(T):
                        mm(bank(7, E, t * E), below_b, maskb[:, t, :], start=True, stop=(t == 0))
                        for q in range(t):
                            mm(bank(7, E, t * E), ones_b, maskb[:, q, :], start=False, stop=(q == t - 1))
                    for t in range(T):
                        ins = mm(bank(7, E, T * E), ones_b, maskb[:, t, :], start=(t == 0), stop=(t == T - 1))
                    ins.then_inc(pos_done, 1)
                if u >= 1:
                    wait_for(pe, shared_added, u - 1)
                    down(u - 1, s, P)
            turn_hidden(T - 1, P)
            pe.wait_ge(shared_added, T - 1)
            down(T - 1, s, P)

            def place(ex):
                pe.wait_ge(onehot_ready, ex.n + 1)
                wait_for(pe, parts_summed, ex.n)
                for t in range(T):
                    ins = mm(bank(6, 9)[0:CAP], onehot[ex.buf][:, t, :], moving_flat[:, t, bass.ds(ex.n * 9, 9)],
                             start=(t == 0), stop=(t == T - 1))
                ins.then_inc(placed_done, 1)

            AHEAD = 4
            pe.wait_ge(moving_ready, 1)
            for c in range(AHEAD + 1):
                place(Expert(c))

            def turn_gathered(ex):
                pe.wait_ge(gathered[ex.buf], 16 * (ex.third + 1))
                wait_for(pe, gT_ready, ex.n)
                turn_rows(xg[ex.buf], 0, CAP).then_inc(g_turned, 1)

            def expert_gate_up(ex):
                wait_expert(pe, ex)
                pe.wait_ge(gT_ready, ex.n + 1)
                gate_up(ex.n + T, lambda k: xgT[ex.buf][:, k, :], expert_slot(ex))

            def expert_down(ex):
                if isinstance(ex.n, int) and ex.n == 0:
                    pe.wait_ge(shared_added, T)
                else:
                    pe.wait_ge(y_scaled, ex.n)
                down(ex.n + T, expert_slot(ex))

            turn_gathered(Expert(0))
            turn_gathered(Expert(1))
            expert_gate_up(Expert(0))


            def turn(ex):
                if ex.i is not None or ex.c + 1 < E:
                    turn_gathered(ex.next(1))
                turn_hidden(ex.n + (T - 1))
                expert_gate_up(ex)
                if ex.i is not None or ex.c + AHEAD < E:
                    place(ex.next(AHEAD))
                expert_down(ex.next(-1))
            for c in range(1, LOOP0):
                turn(Expert(c))
            with pe.Fori(0, LOOPS) as i:
                for j in range(3):
                    turn(Expert(LOOP0 + j, i))
            for c in range(LAST0, E):
                turn(Expert(c))
            turn_hidden(T + E - 1)
            expert_down(Expert(E - 1))

            def further(j, e):
                pe.wait_ge(ov_onehot, j + 1)
                for t in range(T):
                    ins = mm(bank(6, 9)[0:CAP], onehot[0][:, t, :], moving_flat[:, t, bass.ds(e * 9, 9)],
                             start=(t == 0), stop=(t == T - 1))
                ins.then_inc(ov_placed, 1)
                pe.wait_ge(ov_gathered, 16 * j + 16)
                turn_rows(xg[0], 0, CAP).then_inc(g_turned, 1)
                pe.wait_ge(ring_loaded[0], 48 * j + (per_slot[0] + 48 * EXPERTS_IN_0 + 48))
                pe.wait_ge(gT_ready, j + (E + 1))
                gate_up(j + (E + T), lambda k: xgT[0][:, k, :], 0)
                turn_hidden(j + (E + T))
                pe.wait_ge(y_scaled, j + E)
                down(j + (E + T), 0)

            further_blocks(pe, further)


_INS = ["x", "norm1_g", "w_in", "q_norm_a", "k_norm_a", "q_norm_b", "k_norm_b", "w_branch_a", "w_branch_b",
        "w_out", "norm2_g", "w_router", "router_bias", "we_gate", "we_up", "we_down", "ws_gate", "ws_up",
        "ws_down"]


def kernel(**inputs):
    import concourse.bacc as bacc
    from concourse.bass_utils import run_bass_kernel_spmd

    nc = bacc.Bacc("TRN2", target_bir_lowering=False, num_devices=1)
    arrays = {n: np.ascontiguousarray(inputs[n]) for n in _INS}
    arrays["rope"], arrays["masks"], arrays["misc"] = host_constants()
    arrays = {f"in_{n}": x for n, x in arrays.items()}
    aps = {n[3:]: nc.dram_tensor(n, x.shape, mybir.dt.from_np(x.dtype), kind="ExternalInput").ap()
           for n, x in arrays.items()}
    out = nc.dram_tensor("out", (1, S, D), F32, kind="ExternalOutput").ap()
    xn2_rows = nc.dram_tensor("xn2_rows", (S, D), F32, kind="Internal").ap()
    y_rows = nc.dram_tensor("y_rows", (S * TOPK, D), F32, kind="Internal").ap()
    build(nc, aps, out, xn2_rows, y_rows)
    r = run_bass_kernel_spmd(nc, [arrays], core_ids=[0])
    return r.results[0]["out"]
```

```python
from contextlib import ExitStack

import numpy as np

import concourse.bass as bass
from concourse import mybir

F32 = mybir.dt.float32
F32R = mybir.dt.float32r
BF16 = mybir.dt.bfloat16
I32 = mybir.dt.int32
ALU = mybir.AluOpType
ACT = mybir.ActivationFunctionType
AXIS = mybir.AxisListType

P = 128
S, D = 512, 1024
T = S // P
K = D // P
HD = 64
HALF = 512
GRID_W = 64
THETA = 10000.0
EPS = 1e-6
DILATIONS = (1, 4, 16)
RADIUS = 64
HA, HB, HKV = 4, 8, 2
A_WIDTH = 3 * 3 * HA * HD
E, FF = 64, D // 4
EG, TOPG, TOPK = 8, 4, 8
ROUTED_SCALE = 2.5
MASKED = -1.0e30
AWAY = 65536
CAP = 96
BLOCKS = -(-S // CAP)
NOV = (S * TOPK) // (CAP + 1)

NSLOT = 3
SLOT = 3 * K * FF
QKV_CHUNKS = 6
L_GATE = QKV_CHUNKS
L_OUT = L_GATE + 4
L_SHARED = L_OUT + 2
L_EXPERT = L_SHARED + 1
GATE_COL0 = A_WIDTH + HB * HD + 2 * HKV * HD

QA, KA, QB, KB = range(4)
PAIR_QB = 12
PAIR_KB = 16
NPAIR = 18


def q_pair(g, h):
    return 4 * g + h // 2


def k_pair(g, h):
    return 4 * g + 2 + h // 2


CHUNKS = [
    dict(norm=[(QA, 0, 4, 0, 1), (KA, 256, 4, 4, 1)], value=[], pairs=[0, 1, 2, 3]),
    dict(norm=[(QA, 256, 4, 0, 1)], value=[(0, 256, ("A", 0))], pairs=[4, 5]),
    dict(norm=[(KA, 0, 4, 0, 1)], value=[(256, 256, ("A", 1))], pairs=[6, 7]),
    dict(norm=[(QA, 0, 4, 0, 1), (KA, 256, 4, 4, 1)], value=[], pairs=[8, 9, 10, 11]),
    dict(norm=[(QB, 256, 4, 0, 1)], value=[(0, 256, ("A", 2))], pairs=[12, 13]),
    dict(norm=[(QB, 0, 4, 0, 1), (KB, 256, 2, 4, 2)], value=[(384, 128, ("B", 0))],
         pairs=[14, 15, 16, 17]),
]


def host_constants():
    tok = np.arange(S)

    def angles(pos, dim):
        inv = np.float32(THETA) ** (-np.arange(0, dim, 2, dtype=np.float32) / np.float32(dim))
        a = pos.astype(np.float32)[:, None] * inv[None, :].astype(np.float32)
        sin = np.sin(a)
        return np.concatenate([np.cos(a)] * 2, -1), np.concatenate([-sin, sin], -1)

    c1, s1 = angles(tok, HD)
    cr, sr = angles(tok // GRID_W, HD // 2)
    cc, sc = angles(tok % GRID_W, HD // 2)
    rope = np.stack([c1, s1, np.concatenate([cr, cc], -1), np.concatenate([sr, sc], -1)])
    rope = rope.reshape(4, P, T, HD).transpose(1, 0, 2, 3).reshape(P, 4 * T * HD)
    q, k = np.arange(P)[:, None], np.arange(P)[None, :]
    band = np.stack([np.where(np.abs(4 * (k - q) + d) <= RADIUS, 0.0, MASKED) for d in range(-3, 4)])
    by4 = np.where(np.abs(k - q) <= RADIUS, 0.0, MASKED)
    by16 = np.where((k - q) % 4 == 0, 0.0, MASKED)
    masks = np.concatenate([band.transpose(1, 0, 2).reshape(P, 7 * P), by4, by16], -1)
    ident = np.eye(P)
    below = (q < k).astype(np.float64)
    slots = np.broadcast_to(k, (P, P))
    token = 4 * q + np.arange(T)[None, :]
    row = TOPK * token
    away = np.full_like(token, -AWAY)
    parts = np.stack([token % 256, token - token % 256, away, row % 256, row - row % 256, away], -1)
    misc = np.concatenate([ident, below, slots, parts.reshape(P, T * 6)], -1)
    return (np.ascontiguousarray(rope, np.float32), np.ascontiguousarray(masks, np.float32),
            np.ascontiguousarray(misc, np.float32))


class Expert:

    def __init__(self, c, i=None):
        self.c, self.i, self.buf = c, i, c % 3
        self.n = c if i is None else 3 * i + c
        self.third = c // 3 if i is None else i + c // 3

    def next(self, d):
        return Expert(self.c + d, self.i)


def wait_for(eng, sem, n):
    if not isinstance(n, int) or n > 0:
        eng.wait_ge(sem, n)


class Steps:

    def __init__(self, eng, sem):
        self.eng, self.sem, self.n, self.at = eng, sem, 0, 0

    def done(self, ins):
        ins.then_inc(self.sem, 1)
        self.n += 1
        return self.n

    def wait(self):
        self.eng.wait_ge(self.sem, self.at + self.n)


def build(nc, a, out, xn2_rows, y_rows):
    ctx = ExitStack()
    with ctx:
        def sb(name, words, dt=F32):
            return ctx.enter_context(nc.sbuf_tensor(name, [P, words], dt))

        def sem(name):
            return ctx.enter_context(nc.semaphore(name))

        with ExitStack() as front:
            def split_part(name):
                return front.enter_context(nc.sbuf_tensor(name, [P, K * HALF], F32R))

            front.enter_context(nc.sbuf_tensor("loaded_chunk_place", [P, SLOT], F32))
            w_high_t, w_low_t, x_low_t, x_high_t = (split_part(n) for n in ("w_high", "w_low", "x_low", "x_high"))
        ring = sb("ring", NSLOT * SLOT)
        xT_t = sb("xT", K * S)
        xs_t = sb("xs", T * D)
        pairs_t = sb("pairs", NPAIR * S)
        v_t = sb("v", 3 * T * 256 + T * 128)
        mask_t = sb("masks", 9 * P)
        tab_t = sb("tables", 8 * T * HD)
        prob_t = sb("prob", 2 * (768 + 2 * HALF))
        work_t = sb("work", 8 * HALF)
        misc_t = sb("misc", 3 * P + T * 6)
        ones_t = sb("ones", P)
        bf_t = sb("consts_bf", 2 * P, BF16)
        small_t = sb("small", 256)
        gain_t = sb("gains", 4 * HD + E)
        ps_t = ctx.enter_context(nc.psum_tensor("banks", [P, 8 * HALF], F32))

        def view(t, off, *shape):
            n = int(np.prod(shape))
            v = t[:, off:off + n]
            if len(shape) == 1:
                return v
            names = "abcd"[:len(shape)]
            return v.rearrange(f"p ({' '.join(names)}) -> p {' '.join(names)}",
                               **{c: s for c, s in zip(names[1:], shape[1:])})

        def bank(b, n=HALF, off=0):
            return ps_t[:, b * HALF + off:b * HALF + off + n]

        xs = view(xs_t, 0, T, D)
        x_high, x_low = view(x_high_t, 0, K, S), view(x_low_t, 0, K, S)
        w_high, w_low = view(w_high_t, 0, K, HALF), view(w_low_t, 0, K, HALF)
        chunk = view(ring, 0, K, HALF)
        wb_branch = view(ring, K * HALF, 4, HALF)
        wa_branch = view(tab_t, 0, 2, D)
        pairs = view(pairs_t, 0, NPAIR, S)
        merged = view(pairs_t, 0, T, D)
        x_full = view(pairs_t, T * D, K, S)
        x2T = view(pairs_t, T * D, K, S)
        vA = view(v_t, 0, T, 3, 256)
        vB = view(v_t, 3 * T * 256, T, 128)
        band = view(mask_t, 0, 7 * P)
        strided_mask = view(mask_t, 7 * P, 2 * P)
        cosg = [view(tab_t, i * T * HD, T, HD) for i in range(4)]
        sing = [view(tab_t, (4 + i) * T * HD, T, HD) for i in range(4)]
        rope_raw = [view(pairs_t, i * T * HD, T, HD) for i in range(4)]
        prob = [view(prob_t, o, w) for o, w in ((0, 768), (768, HALF), (1280, HALF))]
        probT = [view(prob_t, o, w, P) for o, w in ((1792, 6), (2560, 4), (3072, 4))]
        xnorm = [view(prob_t, i * D, D) for i in range(2)]
        yT = view(work_t, 0, 6, S)
        squares = [view(work_t, i * HALF, 8, HD) for i in range(2)]
        normed = [view(work_t, (2 + i) * HALF, 8, HD) for i in range(2)]
        turned = [view(work_t, (4 + i) * HALF, 8, HD) for i in range(2)]
        rotated = [view(work_t, (6 + i) * HALF, 8, HD) for i in range(2)]
        ident = misc_t[:, 0:P]
        below_f = misc_t[:, P:2 * P]
        slot_row = misc_t[:, 2 * P:3 * P]
        place_parts = view(misc_t, 3 * P, T, 6)
        below_b, ones_b = bf_t[:, 0:P], bf_t[:, P:2 * P]
        g1c, g2c = view(small_t, 0, K), view(small_t, K, K)
        ssq, std, rstd = (view(small_t, 16 + 4 * i, T) for i in range(3))
        ssq2, std2, rstd2 = (view(small_t, 28 + 4 * i, T) for i in range(3))
        hss, hstd, hrstd = ([view(small_t, 40 + 16 * i + 8 * j, 8) for j in range(2)] for i in range(3))
        neg_max = [view(small_t, 88 + i, 1) for i in range(3)]
        den = [view(small_t, 91 + i, 1) for i in range(3)]
        rden = [view(small_t, 94 + i, 1) for i in range(3)]
        pmax = [view(small_t, 97 + i, 1) for i in range(2)]
        gains = view(gain_t, 0, 4, HD)
        bias_b = view(gain_t, 4 * HD, E)
        row_t = sb("gain_row", 4 * HD + E)
        eps_c = small_t[:, 100:101]
        first_root = small_t[:, 101:102]

        gated = [view(v_t, i * HALF, HALF) for i in range(2)]
        gatedB = [view(v_t, (2 + i) * HALF, HALF) for i in range(2)]
        xg = [view(v_t, i * D, D) for i in range(3)]
        xgT = [view(xT_t, i * D, K, P)[:, :, 0:CAP] for i in range(3)]
        h_s = view(xT_t, 3 * D, FF)
        act_s = view(xT_t, 3 * D + FF, FF)
        hT_s = view(xT_t, 3 * D + 2 * FF, 2, P)
        y_s = [view(pairs_t, i * D, D) for i in range(3)]

        junk1 = view(work_t, 0, D)
        junk2 = view(v_t, 2 * D, D)

        def bank2(b):
            return ps_t[:, b * HALF:(b + 2) * HALF]

        logitsT = view(v_t, 0, S)
        scores = view(prob_t, 0, T, E)
        sel = view(prob_t, 256, T, E)
        selm = view(prob_t, 512, T, E)
        repl = view(prob_t, 768, T, E)
        mask = view(prob_t, 1024, T, E)
        wts = view(prob_t, 1280, T, E)
        pos = view(prob_t, 1536, T, E)
        m8 = view(prob_t, 1792, T, EG, 8)
        rank = view(prob_t, 2048, T, E)
        low = view(prob_t, 2304, T, E)
        low_ones = view(prob_t, 2816, E)
        tmp_w = view(prob_t, 2560, T, E)
        gs16 = view(work_t, 0, T, 16)
        gr16 = view(work_t, 64, T, 16)
        gm8 = view(work_t, 128, T, 8)
        gpen = view(work_t, 160, T, EG)
        gmask = view(work_t, 192, T, EG)
        top8 = view(work_t, 224, T, 8)
        wsum = view(work_t, 256, T)
        wrec = view(work_t, 260, T)
        cnt = view(work_t, 264, E)
        maskb = view(work_t, 512, T * E // 2).bitcast(BF16).rearrange("p (t e) -> p t e", t=T)
        placed = view(work_t, 704, E, 3)
        placed_i = view(work_t, 896, E, 2).bitcast(I32)
        tok_b = view(work_t, 1088, 4).bitcast(I32)
        dst_b = view(work_t, 1092, 4).bitcast(I32)
        w_b = view(work_t, 1096, 4)
        onehot = [view(tab_t, i * 256, 256).bitcast(BF16).rearrange("p (t s) -> p t s", t=T)[:, :, 0:CAP]
                  for i in range(3)]
        moving = view(tab_t, 768, T * E * 9 // 2).bitcast(BF16).rearrange("p (t e c) -> p t e c", t=T, e=E)
        moving_flat = moving.rearrange("p t e c -> p t (e c)")
        more_f = view(work_t, 1100, E)
        upto_f = view(work_t, 1164, E)
        le_f = view(v_t, 0, NOV, E)
        ov_e = view(work_t, 1228, NOV)
        ov_x = view(work_t, 1276, NOV)
        ov_base = view(work_t, 1324, NOV)
        ov_list = view(work_t, 1372, NOV + 1).bitcast(I32)
        ov_pos = view(work_t, 1424, T)
        ov_placed3 = view(work_t, 1432, 3)
        ov_num = view(work_t, 1443, 1)

        x_loaded = [sem(f"x_loaded{t}") for t in range(T)]
        first_loaded = sem("first_consts_loaded")
        second_loaded = sem("second_consts_loaded")
        row_loaded = sem("gain_row_loaded")
        rope_loaded = sem("rope_loaded")
        chunk_loaded = sem("chunk_loaded")
        wa_loaded = sem("branch_a_weights_loaded")
        wb_loaded = sem("branch_b_weights_loaded")
        w_high_ready = sem("w_high_ready")
        w_low_dve = sem("w_low_ready_dve")
        w_low_pool = sem("w_low_ready_pool")
        piece_used = sem("weight_piece_used")
        x_high_ready = sem("x_high_ready")
        x_low_ready = sem("x_low_ready")
        m_high_ready = sem("merged_high_ready")
        gains_ready = sem("gains_ready")
        tok_copied = sem("token_index_copied")
        dst_copied = sem("row_index_copied")
        ring_loaded = [sem(f"ring_loaded{i}") for i in range(NSLOT)]
        ones_ready = sem("ones_ready")
        gains_ps = sem("gains_broadcast_ps")
        dve = sem("dve_steps")
        act = sem("act_steps")
        pool = sem("pool_steps")
        tables_ready = sem("tables_ready")
        std1_ready = sem("std1_ready")
        xn_ready = sem("xn_ready")
        xn_turned = sem("xn_turned")
        xT_ready = sem("xT_ready")
        proj_done = sem("proj_done")
        squares_ready = sem("squares_ready")
        sums_ready = sem("sums_ready")
        hstd_ready = sem("hstd_ready")
        normed_ready = sem("normed_ready")
        cos_done = sem("cos_done")
        rotated_ready = sem("rotated_ready")
        pairs_turned = sem("pairs_turned")
        pairs_ready = sem("pairs_ready")
        scores_done = sem("scores_done")
        max_ready = sem("max_ready")
        probs_ready = sem("probs_ready")
        probs_turned = sem("probs_turned")
        probT_act = sem("probT_act")
        probT_dve = sem("probT_dve")
        pv_done = sem("pv_done")
        probs_scaled = sem("probs_scaled")
        yT_a_ready = sem("yT_a_ready")
        yT_b_ready = sem("yT_b_ready")
        gate_done = sem("gate_done")
        gated_ready = sem("gated_ready")
        product_ready = sem("product_ready")
        merged_ready = sem("merged_ready")
        merged_turned = sem("merged_turned")
        mT_ready = sem("mT_ready")
        out_done = sem("out_done")
        h_ready = sem("h_ready")
        std2_ready = sem("std2_ready")
        xn2_ready = sem("xn2_ready")
        xn2_stored = [sem(f"xn2_stored{i}") for i in range(2)]
        x2_turned = sem("x2_turned")
        x2T_ready = sem("x2T_ready")
        router_done = sem("router_done")
        logitsT_ready = sem("logitsT_ready")
        logits_done = sem("logits_done")
        scores_ready = sem("scores_ready")
        mask_ready = sem("mask_ready")
        pos_done = sem("pos_done")
        moving_ready = sem("moving_ready")
        onehot_ready = sem("onehot_ready")
        placed_done = sem("placed_done")
        parts_summed = sem("parts_summed")
        index_ready = sem("index_ready")
        gu_done = sem("gate_up_done")
        silu_ready = sem("silu_ready")
        hid_ready = sem("hidden_ready")
        hid_turned = sem("hidden_turned")
        hidT_ready = sem("hiddenT_ready")
        down_done = sem("down_done")
        shared_added = sem("shared_added")
        w_ready = sem("slot_weight_ready")
        y_scaled = sem("y_scaled")
        gathered = [sem(f"gathered{i}") for i in range(3)]
        g_turned = sem("gathered_turned")
        gT_ready = sem("gatheredT_ready")
        scattered = [sem(f"scattered{i}") for i in range(3)]
        more_counted = sem("further_blocks_counted")
        more_listed = sem("further_blocks_listed")
        further_step = sem("further_index_steps")
        ov_onehot = sem("further_onehot_ready")
        ov_placed = sem("further_index_product_done")
        ov_indexed = sem("further_index_ready")
        ov_gathered = sem("further_gathered")
        ov_scattered = sem("further_scattered")
        pool_waited = sem("pool_waited")
        more_ended = sem("further_block_ended")
        rows_loaded = [sem(f"rows_loaded{i}") for i in range(NSLOT)]
        rows_summed = sem("rows_summed")
        out_ready = sem("out_ready")
        out_stored = sem("out_stored")

        x_rows = a["x"][0].rearrange("(p t) d -> p t d", t=T)
        out_rows = out[0].rearrange("(p t) d -> p t d", t=T)
        w_in = a["w_in"][0].rearrange("(p k) n -> p k n", k=K)
        w_out = a["w_out"][0].rearrange("(p k) n -> p k n", k=K)
        wba = a["w_branch_a"][0].rearrange("(j p) n -> p j n", p=P)
        wbb = a["w_branch_b"][0].rearrange("(j p) n -> p j n", p=P)
        w_router = a["w_router"][0].rearrange("(p k) e -> p k e", k=K)
        wr_s = sb("w_router_s", K * E)
        wr = wr_s[:, :].rearrange("p (k e) -> p k e", k=K)
        xn2_t = xn2_rows.rearrange("(p t) d -> p t d", t=T)
        y_tok = y_rows.rearrange("(p t c) d -> p t c d", t=T, c=TOPK)

        def slot(load):
            return ring[:, (load % NSLOT) * SLOT:(load % NSLOT + 1) * SLOT]


        def high_of(eng, dst, src):
            return eng.copy(dst, src)

        def low_of(eng, dst, src, high):
            return eng.tensor_tensor(dst, src, high.bitcast(F32), ALU.subtract)

        def low_piece(n, k):
            if n == 0:
                return w_low_dve, k + 1
            if k % 2 == 0:
                return w_low_dve, K + K // 2 * (n - 1) + k // 2 + 1
            return w_low_pool, K // 2 * (n - 1) + k // 2 + 1

        def wait_split(eng, n):
            for k in (K - 2, K - 1):
                eng.wait_ge(*low_piece(n, k))

        def wait_chunk_used(eng, n, k):
            if k < K - 1:
                eng.wait_ge(piece_used, (K - 1) * n + k + 1)
            elif n < L_GATE:
                eng.wait_ge(proj_done, T * (n + 1))
            elif n < L_OUT:
                eng.wait_ge(gate_done, T * (n + 1 - L_GATE))
            else:
                eng.wait_ge(out_done, T * (n + 1 - L_OUT))

        def split_low(eng, waiter, n, pieces, done):
            for k in pieces:
                waiter.wait_ge(w_high_ready, K * n + k + 1)
                low_of(eng, w_low[:, k, :], chunk[:, k, :], w_high[:, k, :]).then_inc(done, 1)

        per_slot = [3 * 16 if L_SHARED % NSLOT == i else 0 for i in range(NSLOT)]

        def wait_load(eng, n):
            eng.wait_ge(ring_loaded[n % NSLOT], per_slot[n % NSLOT])

        def expert_slot(ex):
            return (L_EXPERT + ex.c) % NSLOT

        def wait_expert(eng, ex):
            s = expert_slot(ex)
            eng.wait_ge(ring_loaded[s], per_slot[s] + 48 * (ex.third + 1))

        EXPERTS_IN_0 = sum((L_EXPERT + e) % NSLOT == 0 for e in range(E))

        def ffn_parts(s):
            w = ring[:, s * SLOT:(s + 1) * SLOT]
            return (w[:, 0:2 * K * FF].rearrange("p (s k f) -> p s k f", s=2, k=K),
                    w[:, 2 * K * FF:].rearrange("p (c d) -> p c d", c=2))

        NP = QKV_CHUNKS * T
        UNITS = []
        for r in range(T * HA):
            t, h = divmod(r, HA)
            UNITS += [("A", t, h), ("B", t, 2 * h), ("B", t, 2 * h + 1)]
        NU = len(UNITS)
        NM = 2 * 2 * T
        NC = 2 * T
        LOOP0, LOOPS = 4, (E - 8) // 3
        LAST0 = LOOP0 + 3 * LOOPS
        AHEAD = 4

        block = ctx.enter_context(nc.Block())

        def store_out(sp, u):
            t, half = divmod(u, 2)
            sp.wait_ge(out_ready, u + 1)
            sp.dma_start(out_rows[:, t, half * HALF:(half + 1) * HALF],
                         xs[:, t, half * HALF:(half + 1) * HALF]).then_inc(out_stored, 16)

        def further_blocks(eng, body):
            eng.wait_ge(more_counted, 1)
            count = eng.value_load(ov_list[0:1, 0:1], min_val=0, max_val=NOV)
            with eng.If(count > 0):
                eng.wait_ge(more_listed, 1)
                with eng.Fori(0, count) as j:
                    body(j, eng.value_load(ov_list[0:1, bass.ds(j + 1, 1)], min_val=0, max_val=E - 1))

        @block.sync
        def _(sp):
            for t in range(T):
                sp.dma_start(xs[:, t, :], x_rows[:, t, :]).then_inc(x_loaded[t], 16)
                if t == 0:
                    sp.dma_start(misc_t[:, :], a["misc"]).then_inc(first_loaded, 16)
                    sp.dma_start(g1c, a["norm1_g"].rearrange("o (p k) -> (o p) k", k=K)).then_inc(first_loaded, 16)
                if t == 2:
                    for dst, src in [
                        (row_t[0:1, 0:64], a["q_norm_a"]), (row_t[0:1, 64:128], a["k_norm_a"]),
                        (row_t[0:1, 128:192], a["q_norm_b"]), (row_t[0:1, 192:256], a["k_norm_b"]),
                        (row_t[0:1, 256:320], a["router_bias"]),
                    ]:
                        sp.dma_start(dst, src).then_inc(row_loaded, 16)

            for n in range(L_SHARED):
                if n >= 1:
                    wait_split(sp, n - 1)
                if n == L_GATE + 1:
                    sp.wait_ge(pairs_turned, NP)
                    sp.dma_start(wa_branch, wba).then_inc(wa_loaded, 16)
                if n in (L_GATE + 1, L_GATE + 3):
                    half = (n - L_GATE) // 2
                    if half == 1:
                        sp.wait_ge(gate_done, 2 * T)
                    sp.dma_start(wb_branch, wbb[:, :, half * HALF:(half + 1) * HALF]).then_inc(wb_loaded, 16)
                if n < L_GATE:
                    src, c0 = w_in, n * HALF
                elif n < L_OUT:
                    half, br = divmod(n - L_GATE, 2)
                    src, c0 = w_in, GATE_COL0 + br * D + half * HALF
                else:
                    src, c0 = w_out, (n - L_OUT) * HALF
                sp.dma_start(chunk, src[:, :, c0:c0 + HALF]).then_inc(chunk_loaded, 16)
                if n == 0:
                    sp.dma_start(pairs_t[:, 0:4 * T * HD], a["rope"]).then_inc(rope_loaded, 16)
                if n == 1:
                    for dst, src in [
                        (mask_t[:, :], a["masks"]), (wr, w_router),
                        (g2c, a["norm2_g"].rearrange("o (p k) -> (o p) k", k=K)),
                    ]:
                        sp.dma_start(dst, src).then_inc(second_loaded, 16)

            def load(n, dst, src):
                sp.dma_start(dst, src).then_inc(ring_loaded[n % NSLOT], 16)

            def load_ffn(n, gate, up, down):
                w = slot(n)
                load(n, w[:, 0:K * FF], gate.rearrange("(p k) f -> p (k f)", k=K))
                load(n, w[:, K * FF:2 * K * FF], up.rearrange("(p k) f -> p (k f)", k=K))
                load(n, w[:, 2 * K * FF:], down.rearrange("(p c) d -> p (c d)", c=2))

            wait_split(sp, L_SHARED - 1)
            sp.wait_ge(gate_done, NM)
            load_ffn(L_SHARED, a["ws_gate"][0], a["ws_up"][0], a["ws_down"][0])

            def store_xn2(t):
                sp.wait_ge(xn2_ready, t + 1)
                sp.dma_start(xn2_t[:, t, :], xnorm[t % 2]).then_inc(xn2_stored[t % 2], 16)

            def load_expert(ex, free_sem, free_at):
                if free_sem is not None:
                    sp.wait_ge(free_sem, free_at)
                n = ex.n
                load_ffn(L_EXPERT + ex.c, pick(a["we_gate"][0], n), pick(a["we_up"][0], n),
                         pick(a["we_down"][0], n))

            def pick(w, n):
                if isinstance(n, int):
                    return w[n]
                return w[bass.ds(n, 1)].rearrange("o r c -> (o r) c")

            for t in range(T - 1):
                store_xn2(t)
            load_expert(Expert(0), out_done, 2 * T)
            store_xn2(T - 1)
            load_expert(Expert(1), out_done, 2 * T)
            load_expert(Expert(2), down_done, T)
            load_expert(Expert(3), down_done, T + 1)
            with sp.Fori(0, LOOPS) as i:
                for j in range(3):
                    ex = Expert(LOOP0 + j, i)
                    load_expert(ex, down_done, ex.n + (T - 2))
            for c in range(LAST0, E):
                load_expert(Expert(c), down_done, c + T - 2)

            def further(j, e):
                sp.wait_ge(down_done, j + (E + T))
                w = ring[:, 0:SLOT]
                for i, name in enumerate(("we_gate", "we_up")):
                    sp.dma_start(w[:, i * K * FF:(i + 1) * K * FF],
                                 pick(a[name][0], e).rearrange("(p k) f -> p (k f)", k=K)
                                 ).then_inc(ring_loaded[0], 16)
                sp.dma_start(w[:, 2 * K * FF:], pick(a["we_down"][0], e).rearrange("(p c) d -> p (c d)", c=2)
                             ).then_inc(ring_loaded[0], 16)
                sp.wait_ge(ov_scattered, 16 * j + 16)
                sp.sem_inc(more_ended, 1)

            further_blocks(sp, further)
            for b in range(3):
                sp.wait_ge(scattered[b], 16 * ((E - b + 2) // 3))
            for u in range(NC):
                t, half = divmod(u, 2)
                if u < NSLOT:
                    sp.wait_ge(down_done, E + T)
                else:
                    sp.wait_ge(rows_summed, u - NSLOT + 1)
                sp.dma_start(ring[:, (u % NSLOT) * SLOT:(u % NSLOT) * SLOT + TOPK * HALF]
                             .rearrange("p (c d) -> p c d", c=TOPK),
                             y_tok[:, t, :, half * HALF:(half + 1) * HALF]).then_inc(rows_loaded[u % NSLOT], 16)
                if u >= 2:
                    store_out(sp, u - 2)
            store_out(sp, NC - 2)
            store_out(sp, NC - 1)
            sp.wait_ge(out_stored, 16 * NC)

        @block.scalar
        def _(act_e):
            act_e.wait_ge(ones_ready, 1)
            nc.scalar.activation(first_root, eps_c, ACT.Sqrt)
            for t in range(T + 1):
                if t < T:
                    act_e.wait_ge(x_loaded[t], 16)
                    nc.scalar.activation(junk1, xs[:, t, :], ACT.Square, accum_out=ssq[:, t:t + 1]).then_inc(act, 1)
                    act_e.wait_ge(act, t + 1)
                    nc.scalar.activation(std[:, t:t + 1], ssq[:, t:t + 1], ACT.Sqrt, bias=eps_c,
                                         scale=1.0 / D).then_inc(std1_ready, 1)
                if t >= 1:
                    act_e.wait_ge(xT_ready, t)
                    own = slice((t - 1) * P, t * P)
                    high_of(nc.scalar, x_high[:, :, own], x_full[:, :, own]).then_inc(x_high_ready, 1)

            def split_high(n):
                act_e.wait_ge(chunk_loaded, 16 * (n + 1))
                for k in range(K):
                    if n >= 1:
                        wait_chunk_used(act_e, n - 1, k)
                    high_of(nc.scalar, w_high[:, k, :], chunk[:, k, :]).then_inc(w_high_ready, 1)

            split_high(0)

            def store_pairs(m):
                c, t = divmod(m, T)
                pr = CHUNKS[c]["pairs"]
                act_e.wait_ge(pairs_turned, m + 1)
                if m == 0:
                    act_e.wait_ge(tables_ready, 1)
                nc.scalar.copy(pairs[:, pr[0]:pr[0] + len(pr), t * P:(t + 1) * P],
                               bank(4 + m % 2, len(pr) * P).rearrange("p (j q) -> p j q", q=P)
                               ).then_inc(pairs_ready, 1)

            for m in range(NP):
                c, t = divmod(m, T)
                act_e.wait_ge(proj_done, m + 1)
                wait_for(act_e, sums_ready, m - 1)
                nc.scalar.activation(squares[m % 2], bank(m % 4).rearrange("p (h d) -> p h d", d=HD),
                                     ACT.Square).then_inc(squares_ready, 1)
                for c0, n, (br, g) in CHUNKS[c]["value"]:
                    dst = vA[:, t, g, :] if br == "A" else vB[:, t, :]
                    nc.scalar.copy(dst, bank(m % 4, n, c0))
                act_e.wait_ge(sums_ready, m + 1)
                wait_for(act_e, normed_ready, m - 1)
                nc.scalar.activation(hstd[m % 2], hss[m % 2], ACT.Sqrt, bias=eps_c,
                                     scale=1.0 / HD).then_inc(hstd_ready, 1)
                if m >= 1:
                    store_pairs(m - 1)
                if t == T - 2:
                    split_high(c + 1)
            store_pairs(NP - 1)

            for n in range(NU + 1):
                if n < NU:
                    a_unit, i = n % 3 == 0, n % 3
                    act_e.wait_ge(max_ready, n + 1)
                    wait_for(act_e, probs_turned, n - 2)
                    nc.scalar.activation(prob[i], prob[i] if a_unit else bank(1 + i), ACT.Exp, bias=neg_max[i],
                                         accum_out=den[i]).then_inc(probs_ready, 1)
                if n >= 1:
                    m = n - 1
                    act_e.wait_ge(probs_turned, m + 1)
                    wait_for(act_e, pv_done, m - 2)
                    nc.scalar.copy(probT[m % 3][:, 0:4, :],
                                   bank(5 if m % 3 == 2 else 4).rearrange("p (j q) -> p j q", q=P)
                                   ).then_inc(probT_act, 1)

            for m in range(NM):
                act_e.wait_ge(gate_done, m + 1)
                wait_for(act_e, product_ready, m - 1)
                nc.scalar.activation(gated[m % 2], bank(4 + 2 * (m % 2)), ACT.Sigmoid).then_inc(gated_ready, 1)
                if m % T == T - 2:
                    split_high(L_GATE + m // T + 1)
            for t in range(T):
                act_e.wait_ge(merged_turned, t + 1)
                for h in range(2):
                    ins = high_of(nc.scalar, x_high[:, 4 * h:4 * h + 4, t * P:(t + 1) * P],
                                  bank(2 * (t % 2) + h).rearrange("p (j q) -> p j q", q=P))
                ins.then_inc(m_high_ready, 1)
            split_high(L_OUT + 1)
            for t in range(T):
                act_e.wait_ge(h_ready, T + t + 1)
                nc.scalar.activation(junk2, xs[:, t, :], ACT.Square, accum_out=ssq2[:, t:t + 1]).then_inc(act, 1)
                act_e.wait_ge(act, T + t + 1)
                nc.scalar.activation(std2[:, t:t + 1], ssq2[:, t:t + 1], ACT.Sqrt, bias=eps_c,
                                     scale=1.0 / D).then_inc(std2_ready, 1)

            def silu(u, m=CAP):
                act_e.wait_ge(gu_done, u + 1)
                wait_for(act_e, hid_ready, u)
                nc.scalar.activation(act_s[0:m], bank(2, FF)[0:m], ACT.Silu).then_inc(silu_ready, 1)

            def scale_rows(ex):
                act_e.wait_ge(down_done, ex.n + (T + 1))
                act_e.wait_ge(w_ready, ex.n + 1)
                wait_for(act_e, scattered[ex.buf], 16 * ex.third)
                nc.scalar.activation(y_s[ex.buf][0:CAP], bank2(4)[0:CAP], ACT.Copy,
                                     scale=w_b[0:CAP, ex.buf:ex.buf + 1]).then_inc(y_scaled, 1)

            silu(0, P)
            act_e.wait_ge(router_done, T)
            nc.scalar.copy(logitsT[0:E], bank(7)[0:E]).then_inc(logitsT_ready, 1)
            act_e.wait_ge(logits_done, 1)
            for i in range(2):
                act_e.wait_ge(xn2_stored[i], 16 * (T // 2))
            nc.scalar.activation(scores, bank(6, T * E).rearrange("p (t e) -> p t e", e=E),
                                 ACT.Sigmoid).then_inc(scores_ready, 1)
            for u in range(1, T):
                silu(u, P)
            silu(T)
            for c in range(1, LOOP0):
                silu(T + c)
                scale_rows(Expert(c - 1))
            with act_e.Fori(0, LOOPS) as i:
                for j in range(3):
                    ex = Expert(LOOP0 + j, i)
                    silu(ex.n + T)
                    scale_rows(ex.next(-1))
            for c in range(LAST0, E):
                silu(T + c)
                scale_rows(Expert(c - 1))
            scale_rows(Expert(E - 1))

            def further(j, e):
                silu(j + (E + T))
                act_e.wait_ge(down_done, j + (E + T + 1))
                nc.scalar.activation(y_s[0][0:CAP], bank2(4)[0:CAP], ACT.Copy,
                                     scale=w_b[0:CAP, 0:1]).then_inc(y_scaled, 1)

            further_blocks(act_e, further)

        @block.vector
        def _(v):
            step = Steps(v, dve)
            nc.vector.memset(ones_t[:, :], 1.0)
            nc.vector.memset(eps_c, EPS).then_inc(ones_ready, 1)

            def spread(col, n, w):
                return col.unsqueeze(2).to_broadcast([P, n, w])

            def norm_rows(t, std_sem, std_c, rstd_c, waits):
                v.wait_ge(std_sem, t + 1)
                step.done(nc.vector.reciprocal(rstd_c[:, t:t + 1], std_c[:, t:t + 1]))
                step.wait()
                for s_, n_ in waits:
                    wait_for(v, s_, n_)
                return nc.vector.tensor_scalar(xnorm[t % 2], xs[:, t, :], rstd_c[:, t:t + 1], None, ALU.mult)

            def store_turned(t, src0, gain, dst):
                for h in range(2):
                    ins = nc.vector.tensor_tensor(
                        dst[:, 4 * h:4 * h + 4, t * P:(t + 1) * P],
                        bank(src0 + h).rearrange("p (j q) -> p j q", q=P),
                        spread(gain[:, 4 * h:4 * h + 4], 4, P), ALU.mult)
                return ins

            v.wait_ge(first_loaded, 16 * 2)
            nc.vector.tensor_copy(below_b, below_f)
            nc.vector.memset(ones_b, 1.0)
            for t in range(T + 2):
                if t == 2:
                    v.wait_ge(gains_ps, 1)
                    for i, f in enumerate((0.125, 1.0, 0.125, 1.0)):
                        nc.vector.tensor_scalar(gains[:, i, :], bank(7, HD, i * HD), f, None, ALU.mult)
                    nc.vector.tensor_copy(bias_b, bank(7, E, 4 * HD)).then_inc(gains_ready, 1)
                if t < T:
                    norm_rows(t, std1_ready, std, rstd, [(xn_turned, t - 1)]).then_inc(xn_ready, 1)
                if 1 <= t <= T:
                    v.wait_ge(xn_turned, t)
                    store_turned(t - 1, 2 * ((t - 1) % 2), g1c, x_full).then_inc(xT_ready, 1)
                if t >= 2:
                    v.wait_ge(x_high_ready, t - 1)
                    own = slice((t - 2) * P, (t - 1) * P)
                    low_of(nc.vector, x_low[:, :, own], x_full[:, :, own], x_high[:, :, own]).then_inc(x_low_ready, 1)
            split_low(nc.vector, v, 0, range(K), w_low_dve)

            for m in range(NP):
                c, t = divmod(m, T)
                b = m % 2
                v.wait_ge(squares_ready, m + 1)
                nc.vector.tensor_reduce(hss[b], squares[b], AXIS.X, ALU.add).then_inc(sums_ready, 1)
                v.wait_ge(hstd_ready, m + 1)
                step.done(nc.vector.reciprocal(hrstd[b], hstd[b]))
                step.wait()
                wait_for(v, cos_done, m - 1)
                nc.vector.tensor_tensor(normed[b], bank(m % 4).rearrange("p (h d) -> p h d", d=HD),
                                        spread(hrstd[b], 8, HD), ALU.mult).then_inc(normed_ready, 1)
                v.wait_ge(normed_ready, m + 1)
                if m == 0:
                    v.wait_ge(tables_ready, 1)
                heads = 0
                for kind, c0, n, o0, copies in CHUNKS[c]["norm"]:
                    blocks = 1 if kind in (QA, KA) else 2
                    hw = HD // (2 * blocks)
                    src = normed[b][:, c0 // HD:c0 // HD + n, :].rearrange("p h (b s x) -> p h b s x", b=blocks, s=2)
                    tab = sing[kind][:, t, :].rearrange("p (b s x) -> p b s x", b=blocks, s=2)
                    for cp in range(copies):
                        dst = turned[b][:, o0 + cp:o0 + cp + copies * (n - 1) + 1:copies, :].rearrange(
                            "p h (b s x) -> p h b s x", b=blocks, s=2)
                        for s_ in range(2):
                            if blocks == 1:
                                last = nc.vector.tensor_tensor(
                                    dst[:, :, 0, s_, :], src[:, :, 0, 1 - s_, :],
                                    tab[:, 0, s_, :].unsqueeze(1).to_broadcast([P, n, hw]), ALU.mult)
                            else:
                                last = nc.vector.tensor_tensor(
                                    dst[:, :, :, s_, :], src[:, :, :, 1 - s_, :],
                                    tab[:, :, s_, :].unsqueeze(1).to_broadcast([P, n, blocks, hw]), ALU.mult)
                    heads = o0 + n * copies
                step.done(last)
                step.wait()
                v.wait_ge(cos_done, m + 1)
                nc.vector.tensor_tensor(rotated[b][:, 0:heads, :], rotated[b][:, 0:heads, :],
                                        turned[b][:, 0:heads, :], ALU.add).then_inc(rotated_ready, 1)
                if t == T - 2:
                    split_low(nc.vector, v, c + 1, range(0, K, 2), w_low_dve)

            for n in range(NU + 3):
                if n < NU:
                    br, t, h = UNITS[n]
                    i = n % 3
                    v.wait_ge(scores_done, n + 1)
                    if br == "A":
                        wait_for(v, probs_turned, n - 2)
                        if n == 0:
                            v.wait_ge(second_loaded, 16 * 3)
                        nc.vector.tensor_tensor_reduce(
                            out=prob[0][:, 0:HALF], in0=bank(0), in1=band[:, (3 - t) * P:(7 - t) * P],
                            scale=1.0, scalar=-3.0e38, op0=ALU.add, op1=ALU.max, accum_out=pmax[0])
                        step.done(nc.vector.tensor_tensor_reduce(
                            out=prob[0][:, HALF:768], in0=bank(1, 256), in1=strided_mask,
                            scale=1.0, scalar=-3.0e38, op0=ALU.add, op1=ALU.max, accum_out=pmax[1]))
                        step.wait()
                        nc.vector.tensor_scalar(neg_max[0], pmax[0], pmax[1], -1.0,
                                                ALU.max, ALU.mult).then_inc(max_ready, 1)
                    else:
                        wait_for(v, probs_ready, n - 2)
                        nc.vector.tensor_reduce(neg_max[i], bank(1 + i), AXIS.X, ALU.max,
                                                negate=True).then_inc(max_ready, 1)
                if 1 <= n <= NU:
                    m = n - 1
                    i = m % 3
                    v.wait_ge(probs_ready, m + 1)
                    step.done(nc.vector.reciprocal(rden[i], den[i]))
                    step.wait()
                    nc.vector.tensor_scalar(prob[i], prob[i], rden[i], None, ALU.mult).then_inc(probs_scaled, 1)
                if 2 <= n <= NU + 1 and (n - 2) % 3 == 0:
                    m = n - 2
                    v.wait_ge(probs_turned, m + 1)
                    wait_for(v, pv_done, m - 2)
                    nc.vector.tensor_copy(probT[0][:, 4:6, :], bank(5, 2 * P).rearrange("p (j q) -> p j q", q=P)
                                          ).then_inc(probT_dve, 1)
                if n >= 3:
                    m = n - 3
                    br, t, h = UNITS[m]
                    if h % 2:
                        v.wait_ge(pv_done, m + 1)
                        j, b, ready = (h // 2, 7, yT_a_ready) if br == "A" else (2 + h // 2, 6, yT_b_ready)
                        nc.vector.tensor_copy(yT[:, j, t * P:(t + 1) * P], bank(b, P)).then_inc(ready, 1)

            for m in range(NM):
                hb, t = divmod(m, T)
                half, br = divmod(hb, 2)
                v.wait_ge(gated_ready, m + 1)
                if br == 0:
                    dst = merged[:, t, half * HALF:(half + 1) * HALF]
                else:
                    i = half * T + t
                    wait_for(v, merged_ready, i - 1)
                    dst = gatedB[i % 2]
                nc.vector.tensor_tensor(dst, gated[m % 2], bank(5 + 2 * (m % 2)), ALU.mult).then_inc(product_ready, 1)
                if t == T - 2:
                    split_low(nc.vector, v, L_GATE + hb + 1, range(0, K, 2), w_low_dve)
            def merged_low(t):
                v.wait_ge(m_high_ready, t + 1)
                for h in range(2):
                    ks, own = slice(4 * h, 4 * h + 4), slice(t * P, (t + 1) * P)
                    ins = low_of(nc.vector, x_low[:, ks, own],
                                 bank(2 * (t % 2) + h).rearrange("p (j q) -> p j q", q=P), x_high[:, ks, own])
                ins.then_inc(mT_ready, 1)

            def residual(half, t):
                o = half * T + t
                v.wait_ge(out_done, o + 1)
                x_part = xs[:, t, half * HALF:(half + 1) * HALF]
                nc.vector.tensor_tensor(x_part, x_part, bank(4 + o % 3), ALU.add).then_inc(h_ready, 1)

            merged_low(0)
            merged_low(1)
            for t in range(T):
                if t == T - 1:
                    split_low(nc.vector, v, L_OUT + 1, range(0, K, 2), w_low_dve)
                residual(0, t)
                if t + 2 < T:
                    merged_low(t + 2)
            for t in range(T + 1):
                if t < T:
                    residual(1, t)
                if t >= 1:
                    v.wait_ge(x2_turned, t)
                    store_turned(t - 1, 0, g2c, x2T).then_inc(x2T_ready, 1)
                if t < T:
                    norm_rows(t, std2_ready, std2, rstd2,
                              [(x2_turned, t - 1), (xn2_stored[t % 2], 16 * (t // 2))]).then_inc(xn2_ready, 1)

            def group(x):
                return x.rearrange("p t (g e) -> p t g e", e=8)

            def route_a():
                v.wait_ge(scores_ready, 1)
                for i in range(2):
                    v.wait_ge(xn2_stored[i], 16 * (T // 2))
                step.done(nc.vector.tensor_tensor(sel, scores, bias_b.unsqueeze(1).to_broadcast([P, T, E]), ALU.add))
                nc.vector.memset(gs16, MASKED)
                nc.vector.memset(low_ones, 1.0)
                step.done(nc.vector.memset(low, 1.0))
                step.wait()
                for t in range(T):
                    for g in range(EG):
                        ins = nc.vector.max(out=m8[:, t, g, :], in_=sel[:, t, 8 * g:8 * g + 8])
                step.done(ins)
                step.wait()
                step.done(nc.vector.tensor_tensor(gs16[:, :, 0:EG], m8[:, :, :, 0], m8[:, :, :, 1], ALU.add))
                step.wait()

            def route_b():
                for t in range(T):
                    ins = nc.vector.max(out=gm8[:, t, :], in_=gs16[:, t, :])
                step.done(ins)
                step.wait()
                step.done(nc.vector.memset(gm8[:, :, TOPG:8], MASKED))
                step.wait()
                for t in range(T):
                    ins = nc.vector.match_replace(out=gr16[:, t, :], in_to_replace=gm8[:, t, :],
                                                  in_values=gs16[:, t, :], imm_value=2 * MASKED)
                step.done(ins)
                step.wait()
                step.done(nc.vector.tensor_tensor(gmask, gr16[:, :, 0:EG], gs16[:, :, 0:EG], ALU.not_equal))
                step.wait()
                nc.vector.tensor_scalar(gpen, gmask, -MASKED, MASKED, ALU.mult, ALU.add)
                step.done(nc.vector.tensor_tensor(group(selm), group(sel),
                                                  gmask.unsqueeze(3).to_broadcast([P, T, EG, 8]), ALU.mult))
                step.wait()
                step.done(nc.vector.tensor_tensor(group(selm), group(selm),
                                                  gpen.unsqueeze(3).to_broadcast([P, T, EG, 8]), ALU.add))
                step.wait()
                for t in range(T):
                    ins = nc.vector.max(out=top8[:, t, :], in_=selm[:, t, :])
                step.done(ins)
                step.wait()
                for t in range(T):
                    ins = nc.vector.match_replace(out=repl[:, t, :], in_to_replace=top8[:, t, :],
                                                  in_values=selm[:, t, :], imm_value=3 * MASKED)
                step.done(ins)
                step.wait()
                step.done(nc.vector.tensor_tensor(mask, repl, selm, ALU.not_equal))
                step.wait()
                nc.vector.tensor_copy(maskb, mask).then_inc(mask_ready, 1)

            def route_c():
                step.done(nc.vector.tensor_tensor(wts, scores, mask, ALU.mult))
                step.wait()
                step.done(nc.vector.tensor_reduce(wsum, wts, AXIS.X, ALU.add))
                step.wait()
                step.done(nc.vector.reciprocal(wrec, wsum))
                step.wait()
                step.done(nc.vector.tensor_scalar(wrec, wrec, ROUTED_SCALE, None, ALU.mult))
                for t in range(T):
                    ins = nc.vector.tensor_tensor_scan(rank[:, t, :], low[:, t, :], mask[:, t, :], 0.0,
                                                       ALU.mult, ALU.add)
                step.done(ins)
                step.wait()
                nc.vector.tensor_tensor(rank, rank, mask, ALU.subtract)
                step.done(nc.vector.tensor_tensor(wts, wts, spread(wrec, T, E), ALU.mult))
                step.wait()

            def route_d():
                for t in range(T):
                    nc.vector.tensor_copy(moving[:, t, :, 0:6],
                                          place_parts[:, t, :].unsqueeze(1).to_broadcast([P, E, 6]))
                step.done(nc.vector.tensor_copy(moving[:, :, :, 6], wts))
                step.wait()
                nc.vector.tensor_tensor(moving[:, :, :, 3], moving[:, :, :, 3], rank, ALU.add)
                step.done(nc.vector.tensor_tensor(low, wts, moving[:, :, :, 6], ALU.subtract))
                step.wait()
                step.done(nc.vector.tensor_copy(moving[:, :, :, 7], low))
                step.wait()
                step.done(nc.vector.tensor_tensor(tmp_w, low, moving[:, :, :, 7], ALU.subtract))
                step.wait()
                step.done(nc.vector.tensor_copy(moving[:, :, :, 8], tmp_w))
                step.wait()
                step.done(nc.vector.tensor_scalar(pos, mask, -4096.0, 4096.0, ALU.mult, ALU.add))
                step.wait()
                v.wait_ge(pos_done, 1)
                nc.vector.tensor_tensor(pos, pos, bank(7, T * E).rearrange("p (t e) -> p t e", e=E),
                                        ALU.add)
                nc.vector.tensor_copy(cnt, bank(7, E, T * E)).then_inc(moving_ready, 1)

            def product(u, m=CAP):
                v.wait_ge(silu_ready, u + 1)
                wait_for(v, hid_turned, u)
                nc.vector.tensor_tensor(h_s[0:m], act_s[0:m], bank(2, FF, FF)[0:m], ALU.mult).then_inc(hid_ready, 1)

            def store_hidT(u, m=CAP):
                v.wait_ge(hid_turned, u + 1)
                wait_for(v, down_done, u)
                nc.vector.tensor_copy(hT_s[:, :, 0:m], bank(3, FF).rearrange("p (c q) -> p c q", q=P)[:, :, 0:m]
                                      ).then_inc(hidT_ready, 1)

            def add_shared(u):
                v.wait_ge(down_done, u + 1)
                nc.vector.tensor_tensor(xs[:, u, :], xs[:, u, :], bank2(4), ALU.add).then_inc(shared_added, 1)

            product(0, P)
            store_hidT(0, P)
            route_a()
            product(1, P)
            add_shared(0)
            store_hidT(1, P)
            route_b()
            product(2, P)
            add_shared(1)
            route_c()
            store_hidT(2, P)
            route_d()
            def slots(x):
                return x[0:CAP]

            def one_hot(ex):
                wait_for(v, placed_done, ex.n - 2)
                nc.vector.tensor_tensor(onehot[ex.buf], slot_row[:, 0:CAP].unsqueeze(1).to_broadcast([P, T, CAP]),
                                        pos[:, :, bass.ds(ex.n, 1)].to_broadcast([P, T, CAP]),
                                        ALU.is_equal).then_inc(onehot_ready, 1)

            def store_places(ex):
                v.wait_ge(placed_done, ex.n + 1)
                nc.vector.tensor_reduce(slots(placed[:, bass.ds(ex.n, 1), :]).rearrange("p o c -> p (o c)"),
                                        slots(bank(6, 9)).rearrange("p (c j) -> p c j", j=3), AXIS.X, ALU.add
                                        ).then_inc(parts_summed, 1)
                v.wait_ge(parts_summed, ex.n + 1)
                nc.vector.tensor_scalar(slots(placed_i[:, bass.ds(ex.n, 1), :]), slots(placed[:, bass.ds(ex.n, 1), 0:2]),
                                        float(AWAY), None, ALU.add).then_inc(index_ready, 1)

            v.wait_ge(moving_ready, 1)
            for c in range(3):
                one_hot(Expert(c))
            product(3, P)
            store_places(Expert(0))
            store_places(Expert(1))
            add_shared(2)
            store_places(Expert(2))
            store_hidT(3, P)

            def store_gT(ex):
                v.wait_ge(g_turned, ex.n + 1)
                wait_for(v, gu_done, ex.n + (T - 2))
                for h in range(2):
                    ins = nc.vector.tensor_tensor(
                        xgT[ex.buf][:, 4 * h:4 * h + 4, :],
                        bank(h).rearrange("p (j q) -> p j q", q=P)[:, :, 0:CAP],
                        spread(g2c[:, 4 * h:4 * h + 4], 4, CAP), ALU.mult)
                ins.then_inc(gT_ready, 1)

            def slot_weight(ex):
                wait_for(v, y_scaled, ex.n - 2)
                nc.vector.tensor_copy(w_b[0:CAP, ex.buf:ex.buf + 1],
                                      placed[0:CAP, bass.ds(ex.n, 1), 2]).then_inc(w_ready, 1)

            store_gT(Expert(0))
            add_shared(3)
            store_gT(Expert(1))
            one_hot(Expert(3))
            one_hot(Expert(AHEAD))
            slot_weight(Expert(0))
            product(T)
            store_places(Expert(3))
            store_places(Expert(AHEAD))
            step.done(nc.vector.tensor_scalar(more_f, cnt, float(CAP), None, ALU.is_gt))
            for q in range(2, BLOCKS):
                step.wait()
                step.done(nc.vector.scalar_tensor_tensor(out=more_f, in0=cnt, scalar=float(CAP * q), in1=more_f,
                                                         op0=ALU.is_gt, op1=ALU.add))
            step.wait()
            step.done(nc.vector.tensor_reduce(ov_num, more_f, AXIS.X, ALU.add))
            step.wait()
            nc.vector.tensor_copy(ov_list[:, 0:1], ov_num).then_inc(more_counted, 1)


            def turn(ex):
                if ex.i is not None or ex.c + 1 < E:
                    store_gT(ex.next(1))
                store_hidT(ex.n + (T - 1))
                ahead = ex.i is not None or ex.c + AHEAD < E
                if ahead:
                    one_hot(ex.next(AHEAD))
                slot_weight(ex)
                product(ex.n + T)
                if ahead:
                    store_places(ex.next(AHEAD))
            for c in range(1, LOOP0):
                turn(Expert(c))
            with v.Fori(0, LOOPS) as i:
                for j in range(3):
                    turn(Expert(LOOP0 + j, i))
            for c in range(LAST0, E):
                turn(Expert(c))
            store_hidT(T + E - 1)

            def list_further():
                v.wait_ge(g_turned, E)
                for b in range(3):
                    v.wait_ge(scattered[b], 16 * ((E - b + 2) // 3))
                v.wait_ge(y_scaled, E)
                step.done(nc.vector.memset(ov_x, 1.0))
                step.wait()
                step.done(nc.vector.tensor_tensor_scan(upto_f, low_ones, more_f, 0.0, ALU.mult, ALU.add))
                step.done(nc.vector.tensor_tensor_scan(ov_base, ov_x, ov_x, -1.0, ALU.mult, ALU.add))
                step.wait()
                step.done(nc.vector.tensor_tensor(le_f, upto_f.unsqueeze(1).to_broadcast([P, NOV, E]),
                                                  ov_base.unsqueeze(2).to_broadcast([P, NOV, E]), ALU.is_le))
                step.wait()
                step.done(nc.vector.tensor_reduce(ov_e, le_f, AXIS.X, ALU.add))
                step.wait()
                step.done(nc.vector.tensor_tensor(le_f, le_f, upto_f.unsqueeze(1).to_broadcast([P, NOV, E]),
                                                  ALU.mult))
                nc.vector.tensor_scalar(ov_e, ov_e, float(E - 1), None, ALU.min)
                step.wait()
                step.done(nc.vector.tensor_reduce(ov_x, le_f, AXIS.X, ALU.max))
                step.wait()
                step.done(nc.vector.tensor_tensor(ov_base, ov_base, ov_x, ALU.subtract))
                step.wait()
                step.done(nc.vector.tensor_scalar(ov_base, ov_base, 1.0, float(CAP), ALU.add, ALU.mult))
                nc.vector.tensor_copy(ov_list[:, 1:NOV + 1], ov_e).then_inc(more_listed, 1)

            def further(j, e):
                def in_order(ins, k, of):
                    ins.then_inc(further_step, 1)
                    v.wait_ge(further_step, of * j + k)
                FS = 2
                in_order(nc.vector.tensor_scalar(ov_pos, pos[:, :, bass.ds(e, 1)].rearrange("p t o -> p (t o)"), ov_base[:, bass.ds(j, 1)], None,
                                                 ALU.subtract), 1, FS)
                nc.vector.tensor_tensor(onehot[0], slot_row[:, 0:CAP].unsqueeze(1).to_broadcast([P, T, CAP]),
                                        ov_pos.unsqueeze(2).to_broadcast([P, T, CAP]),
                                        ALU.is_equal).then_inc(ov_onehot, 1)
                v.wait_ge(ov_placed, j + 1)
                in_order(nc.vector.tensor_reduce(slots(ov_placed3), slots(bank(6, 9)).rearrange("p (c j) -> p c j", j=3),
                                                 AXIS.X, ALU.add), 2, FS)
                nc.vector.tensor_copy(slots(w_b[:, 0:1]), slots(ov_placed3[:, 2:3]))
                nc.vector.tensor_scalar(slots(tok_b[:, 0:1]), slots(ov_placed3[:, 0:1]), float(AWAY), None, ALU.add)
                nc.vector.tensor_scalar(slots(dst_b[:, 0:1]), slots(ov_placed3[:, 1:2]), float(AWAY), None,
                                        ALU.add).then_inc(ov_indexed, 1)
                v.wait_ge(g_turned, j + (E + 1))
                for h in range(2):
                    ins = nc.vector.tensor_tensor(
                        xgT[0][:, 4 * h:4 * h + 4, :], bank(h).rearrange("p (j q) -> p j q", q=P)[:, :, 0:CAP],
                        spread(g2c[:, 4 * h:4 * h + 4], 4, CAP), ALU.mult)
                ins.then_inc(gT_ready, 1)
                product(j + (E + T))
                store_hidT(j + (E + T))
                v.wait_ge(ov_scattered, 16 * j + 16)

            count = v.value_load(ov_list[0:1, 0:1], min_val=0, max_val=NOV)
            with v.If(count > 0):
                list_further()
                v.wait_ge(more_listed, 1)
                with v.Fori(0, count) as j:
                    further(j, v.value_load(ov_list[0:1, bass.ds(j + 1, 1)], min_val=0, max_val=E - 1))

            for u in range(NC):
                t, half = divmod(u, 2)
                v.wait_ge(rows_loaded[u % NSLOT], 16 * (u // NSLOT + 1))
                rows = ring[:, (u % NSLOT) * SLOT:(u % NSLOT) * SLOT + TOPK * HALF]
                red = view(xT_t, (u % 2) * HALF, HALF)
                nc.vector.tensor_reduce(red, rows.rearrange("p (c d) -> p d c", c=TOPK), AXIS.X, ALU.add
                                        ).then_inc(rows_summed, 1)
                v.wait_ge(rows_summed, u + 1)
                x_part = xs[:, t, half * HALF:(half + 1) * HALF]
                nc.vector.tensor_tensor(x_part, x_part, red, ALU.add).then_inc(out_ready, 1)

        @block.gpsimd
        def _(g):
            g.wait_ge(rope_loaded, 16)
            g.wait_ge(gains_ready, 1)
            for kind in range(4):
                cos_r, sin_r = rope_raw[2 * (kind // 2)], rope_raw[2 * (kind // 2) + 1]
                blocks = 1 if kind in (QA, KA) else 2
                hw = HD // (2 * blocks)
                nc.gpsimd.tensor_tensor(cosg[kind], cos_r, gains[:, kind, :].unsqueeze(1).to_broadcast([P, T, HD]),
                                        ALU.mult)
                for b in range(blocks):
                    for s_ in range(2):
                        o, i = (2 * b + s_) * hw, (2 * b + 1 - s_) * hw
                        last = nc.gpsimd.tensor_tensor(
                            sing[kind][:, :, o:o + hw], sin_r[:, :, o:o + hw],
                            gains[:, kind, i:i + hw].unsqueeze(1).to_broadcast([P, T, hw]), ALU.mult)
            last.then_inc(tables_ready, 1)
            g.wait_ge(tables_ready, 1)
            for m in range(NP):
                c, t = divmod(m, T)
                b = m % 2
                g.wait_ge(normed_ready, m + 1)
                wait_for(g, pairs_turned, m - 1)
                for kind, c0, n, o0, copies in CHUNKS[c]["norm"]:
                    for cp in range(copies):
                        last = nc.gpsimd.tensor_tensor(
                            rotated[b][:, o0 + cp:o0 + cp + copies * (n - 1) + 1:copies, :],
                            normed[b][:, c0 // HD:c0 // HD + n, :],
                            cosg[kind][:, t, :].unsqueeze(1).to_broadcast([P, n, HD]), ALU.mult)
                last.then_inc(cos_done, 1)
                if t == T - 2:
                    split_low(nc.gpsimd, g, c + 1, range(1, K, 2), w_low_pool)
            for m in range(NM):
                hb, t = divmod(m, T)
                half, br = divmod(hb, 2)
                if br == 1:
                    g.wait_ge(product_ready, m + 1)
                    part = merged[:, t, half * HALF:(half + 1) * HALF]
                    nc.gpsimd.tensor_tensor(part, part, gatedB[(half * T + t) % 2], ALU.add).then_inc(merged_ready, 1)
                if t == T - 2:
                    split_low(nc.gpsimd, g, L_GATE + hb + 1, range(1, K, 2), w_low_pool)
            split_low(nc.gpsimd, g, L_OUT + 1, range(1, K, 2), w_low_pool)

            step = Steps(g, pool)
            g.wait_ge(std2_ready, T)
            g.wait_ge(logits_done, 1)
            for b in range(3):
                last = nc.gpsimd.memset(xg[b], 0.0)
            step.done(last)
            step.wait()
            for i in range(2):
                g.wait_ge(xn2_stored[i], 16 * (T // 2))
            last_token, last_row = g.to_reg(S - 1), g.to_reg(S * TOPK - 1)
            def gather(ex):
                wait_for(g, g_turned, ex.n - 2)
                g.wait_ge(index_ready, ex.n + 1)
                nc.gpsimd.tensor_copy(tok_b[0:CAP, ex.buf:ex.buf + 1],
                                      placed_i[0:CAP, bass.ds(ex.n, 1), 0]).then_inc(tok_copied, 1)
                g.wait_ge(tok_copied, ex.n + 1)
                g.sem_inc(pool_waited, 1)
                nc.gpsimd.indirect_dma_start(
                    out=xg[ex.buf][0:CAP], out_offset=None, in_=xn2_rows[:, :],
                    in_offset=bass.IndirectOffsetOnAxis(ap=tok_b[0:CAP, ex.buf:ex.buf + 1], axis=0),
                    bounds_check=last_token, oob_is_err=False).then_inc(gathered[ex.buf], 16)

            def scatter(ex):
                g.wait_ge(y_scaled, ex.n + 1)
                wait_for(g, scattered[ex.buf], 16 * ex.third)
                nc.gpsimd.tensor_copy(dst_b[0:CAP, ex.buf:ex.buf + 1],
                                      placed_i[0:CAP, bass.ds(ex.n, 1), 1]).then_inc(dst_copied, 1)
                g.wait_ge(dst_copied, ex.n + 1)
                g.sem_inc(pool_waited, 1)
                nc.gpsimd.indirect_dma_start(
                    out=y_rows[:, :],
                    out_offset=bass.IndirectOffsetOnAxis(ap=dst_b[0:CAP, ex.buf:ex.buf + 1], axis=0),
                    in_=y_s[ex.buf][0:CAP], in_offset=None,
                    bounds_check=last_row, oob_is_err=False).then_inc(scattered[ex.buf], 16)

            for c in range(3):
                gather(Expert(c))
            gather(Expert(3))
            for c in range(1, LOOP0):
                gather(Expert(c + 3))
                scatter(Expert(c - 1))
            with g.Fori(0, LOOPS) as i:
                for j in range(3):
                    ex = Expert(LOOP0 + j, i)
                    gather(ex.next(3))
                    scatter(ex.next(-1))
            for c in range(LAST0, E):
                if c + 3 < E:
                    gather(Expert(c + 3))
                scatter(Expert(c - 1))
            scatter(Expert(E - 1))

            def further(j, e):
                g.wait_ge(ov_indexed, j + 1)
                g.sem_inc(pool_waited, 1)
                nc.gpsimd.indirect_dma_start(
                    out=xg[0][0:CAP], out_offset=None, in_=xn2_rows[:, :],
                    in_offset=bass.IndirectOffsetOnAxis(ap=tok_b[0:CAP, 0:1], axis=0),
                    bounds_check=last_token, oob_is_err=False).then_inc(ov_gathered, 16)
                g.wait_ge(y_scaled, j + (E + 1))
                g.sem_inc(pool_waited, 1)
                nc.gpsimd.indirect_dma_start(
                    out=y_rows[:, :], out_offset=bass.IndirectOffsetOnAxis(ap=dst_b[0:CAP, 0:1], axis=0),
                    in_=y_s[0][0:CAP], in_offset=None,
                    bounds_check=last_row, oob_is_err=False).then_inc(ov_scattered, 16)
                g.wait_ge(ov_scattered, 16 * j + 16)

            further_blocks(g, further)

        @block.tensor
        def _(pe):
            mm, turn_to = nc.tensor.matmul, nc.tensor.transpose
            pe.wait_ge(ones_ready, 1)

            def turn_rows(rows, b0, m=P):
                for k in range(K):
                    ins = turn_to(bank(b0 + k // 4, m, (k % 4) * P), rows[0:m, k:D:K], ident[0:m, 0:m])
                return ins

            pe.wait_ge(first_loaded, 16 * 2)
            for t in range(T):
                pe.wait_ge(xn_ready, t + 1)
                wait_for(pe, xT_ready, t - 1)
                turn_rows(xnorm[t % 2], 2 * (t % 2)).then_inc(xn_turned, 1)
                if t == 1:
                    pe.wait_ge(row_loaded, 16 * 5)
                    mm(bank(7, 4 * HD + E), ones_t[0:1, :], row_t[0:1, :], start=True, stop=True).then_inc(gains_ps, 1)

            def turn_pairs(m):
                c, t = divmod(m, T)
                pe.wait_ge(rotated_ready, m + 1)
                wait_for(pe, pairs_ready, m - 1)
                if m == 0:
                    pe.wait_ge(gains_ready, 1)
                flat = rotated[m % 2].rearrange("p h d -> p (h d)")
                for j in range(len(CHUNKS[c]["pairs"])):
                    ins = turn_to(bank(4 + m % 2, P, j * P), flat[:, j * P:(j + 1) * P], ident)
                ins.then_inc(pairs_turned, 1)

            def project(dst, n, t):
                own = slice(t * P, (t + 1) * P)
                for k in range(K):
                    if t == 0:
                        pe.wait_ge(*low_piece(n, k))
                    mm(dst, x_high[:, k, own], w_high[:, k, :], start=(k == 0), stop=False)
                    mm(dst, x_high[:, k, own], w_low[:, k, :], start=False, stop=False)
                    ins = mm(dst, x_low[:, k, own], w_high[:, k, :], start=False, stop=(k == K - 1))
                    if t == T - 1 and k < K - 1:
                        ins.then_inc(piece_used, 1)
                return ins

            for m in range(NP):
                c, t = divmod(m, T)
                if m == 0:
                    pe.wait_ge(x_low_ready, T)
                wait_for(pe, normed_ready, m - 3)
                project(bank(m % 4), c, t).then_inc(proj_done, 1)
                if m >= 1:
                    turn_pairs(m - 1)
            turn_pairs(NP - 1)

            def score(n):
                br, t, h = UNITS[n]
                wait_for(pe, probs_ready, n - 2)
                r = HD * (h % 2)
                b0 = (0, 2, 3)[n % 3]
                rows = slice(r, r + HD)
                own = slice(t * P, (t + 1) * P)
                if br == "A":
                    mm(bank(b0), pairs[rows, q_pair(0, h), own], pairs[rows, k_pair(0, h), :], start=True, stop=True)
                    for g in (1, 2):
                        ins = mm(bank(b0 + 1, P, (g - 1) * P), pairs[rows, q_pair(g, h), own],
                                 pairs[rows, k_pair(g, h), own], start=True, stop=True)
                else:
                    ins = mm(bank(b0), pairs[rows, PAIR_QB + h // 2, own],
                             pairs[rows, PAIR_KB + h // (HB // HKV), :], start=True, stop=True)
                ins.then_inc(scores_done, 1)

            def turn_probs(n):
                i = n % 3
                pe.wait_ge(probs_scaled, n + 1)
                wait_for(pe, probT_act, n)
                wait_for(pe, probT_dve, (n + 2) // 3)
                for j in range(6 if i == 0 else 4):
                    b = 5 if i == 2 else 4 + j // 4
                    ins = turn_to(bank(b, P, (j % 4) * P), prob[i][:, j * P:(j + 1) * P], ident)
                ins.then_inc(probs_turned, 1)

            def weigh(n):
                br, t, h = UNITS[n]
                pe.wait_ge(probT_act, n + 1)
                if br == "A":
                    pe.wait_ge(probT_dve, n // 3 + 1)
                    if h % 2 == 0:
                        wait_for(pe, yT_a_ready, n // 6)
                elif h % 2 == 0:
                    wait_for(pe, yT_b_ready, n // 3)
                hs = slice(h * HD, (h + 1) * HD)
                if br == "A":
                    vals = [vA[:, u, 0, hs] for u in range(T)] + [vA[:, t, 1, hs], vA[:, t, 2, hs]]
                else:
                    kv = h // (HB // HKV)
                    vals = [vB[:, u, kv * HD:(kv + 1) * HD] for u in range(T)]
                r = HD * (h % 2)
                for j, val in enumerate(vals):
                    ins = mm(bank(7 if br == "A" else 6, P)[r:r + HD], val, probT[n % 3][:, j, :],
                             start=(j == 0), stop=(j == len(vals) - 1))
                ins.then_inc(pv_done, 1)

            pe.wait_ge(pairs_ready, NP)
            score(0)
            score(1)
            for n in range(NU + 1):
                if n + 2 < NU:
                    score(n + 2)
                if n < NU:
                    turn_probs(n)
                if n >= 1:
                    weigh(n - 1)

            for m in range(NM):
                hb, t = divmod(m, T)
                half, br = divmod(hb, 2)
                wait_for(pe, product_ready, m - 1)
                bg = 4 + 2 * (m % 2)
                own = slice(t * P, (t + 1) * P)
                if m == 0:
                    project(bank(bg), L_GATE, 0)
                    pe.wait_ge(yT_a_ready, T * HA // 2)
                    pe.wait_ge(yT_b_ready, T * HB // 2)
                    pe.wait_ge(wa_loaded, 16)
                if br == 1 and t == 0:
                    pe.wait_ge(wb_loaded, 16 * (half + 1))
                js = range(0, 2) if br == 0 else range(2, 6)
                for j in js:
                    w = wa_branch[:, j, half * HALF:(half + 1) * HALF] if br == 0 else wb_branch[:, j - 2, :]
                    ins = mm(bank(bg + 1), yT[:, j, own], w, start=(j == js[0]), stop=(j == js[-1]))
                if m > 0:
                    ins = project(bank(bg), L_GATE + hb, t)
                ins.then_inc(gate_done, 1)
            def turn_merged(t):
                pe.wait_ge(merged_ready, T + t + 1)
                wait_for(pe, mT_ready, t - 1)
                turn_rows(merged[:, t, :], 2 * (t % 2)).then_inc(merged_turned, 1)

            def project_out(half, t):
                o = half * T + t
                pe.wait_ge(mT_ready, t + 1)
                wait_for(pe, h_ready, o - 2)
                project(bank(4 + o % 3), L_OUT + half, t).then_inc(out_done, 1)

            def turn_x2(t):
                pe.wait_ge(xn2_ready, t + 1)
                wait_for(pe, x2T_ready, t)
                turn_rows(xnorm[t % 2], 0).then_inc(x2_turned, 1)

            def router(t):
                pe.wait_ge(x2T_ready, t + 1)
                if t == 0:
                    pe.wait_ge(second_loaded, 16 * 3)
                for k in range(K):
                    ins = mm(bank(7, P, t * P)[0:E], wr[:, k, :], x2T[:, k, t * P:(t + 1) * P],
                             start=(k == 0), stop=(k == K - 1))
                ins.then_inc(router_done, 1)

            turn_merged(0)
            turn_merged(1)
            pe.wait_ge(product_ready, NM)
            for t in range(T):
                project_out(0, t)
                if t + 2 < T:
                    turn_merged(t + 2)
            for t in range(T):
                project_out(1, t)
                if t >= 1:
                    turn_x2(t - 1)
                if t >= 2:
                    router(t - 2)

            def gate_up(u, lhs, s, m=CAP):
                wait_for(pe, hid_ready, u)
                w, _ = ffn_parts(s)
                for k in range(K):
                    ins = mm(bank(2)[0:m].rearrange("p (s f) -> p s f", s=2), lhs(k), w[:, :, k, :],
                             start=(k == 0), stop=(k == K - 1))
                ins.then_inc(gu_done, 1)

            def turn_hidden(u, m=CAP):
                pe.wait_ge(hid_ready, u + 1)
                wait_for(pe, hidT_ready, u)
                for c in range(2):
                    ins = turn_to(bank(3, m, c * P), h_s[0:m, c:FF:2], ident[0:m, 0:m])
                ins.then_inc(hid_turned, 1)

            def down(u, s, m=CAP):
                pe.wait_ge(hidT_ready, u + 1)
                _, w = ffn_parts(s)
                for half in range(2):
                    for c in range(2):
                        ins = mm(bank(4 + half)[0:m], hT_s[:, c, 0:m], w[:, c, half * HALF:(half + 1) * HALF],
                                 start=(c == 0), stop=(c == 1))
                ins.then_inc(down_done, 1)

            def place(ex):
                pe.wait_ge(onehot_ready, ex.n + 1)
                wait_for(pe, parts_summed, ex.n)
                for t in range(T):
                    ins = mm(bank(6, 9)[0:CAP], onehot[ex.buf][:, t, :], moving_flat[:, t, bass.ds(ex.n * 9, 9)],
                             start=(t == 0), stop=(t == T - 1))
                ins.then_inc(placed_done, 1)

            wait_load(pe, L_SHARED)
            s = L_SHARED % NSLOT

            def shared_gate_up(u):
                gate_up(u, lambda k: x2T[:, k, u * P:(u + 1) * P], s, P)

            def shared_down(u):
                wait_for(pe, shared_added, u)
                down(u, s, P)

            shared_gate_up(0)
            turn_x2(T - 1)
            router(T - 2)
            turn_hidden(0, P)
            router(T - 1)
            pe.wait_ge(h_ready, 2 * T)
            pe.wait_ge(logitsT_ready, 1)
            for t in range(T):
                ins = turn_to(bank(6, E, t * E), logitsT[0:E, t * P:(t + 1) * P], ident[0:E, 0:E])
            ins.then_inc(logits_done, 1)
            shared_gate_up(1)
            shared_down(0)
            turn_hidden(1, P)
            shared_gate_up(2)
            shared_down(1)
            pe.wait_ge(mask_ready, 1)
            for t in range(T):
                mm(bank(7, E, t * E), below_b, maskb[:, t, :], start=True, stop=(t == 0))
                for q in range(t):
                    mm(bank(7, E, t * E), ones_b, maskb[:, q, :], start=False, stop=(q == t - 1))
            for t in range(T):
                ins = mm(bank(7, E, T * E), ones_b, maskb[:, t, :], start=(t == 0), stop=(t == T - 1))
            ins.then_inc(pos_done, 1)
            turn_hidden(2, P)
            shared_gate_up(3)
            pe.wait_ge(moving_ready, 1)
            place(Expert(0))
            place(Expert(1))
            shared_down(2)
            place(Expert(2))
            turn_hidden(3, P)

            def turn_gathered(ex):
                pe.wait_ge(gathered[ex.buf], 16 * (ex.third + 1))
                wait_for(pe, gT_ready, ex.n)
                turn_rows(xg[ex.buf], 0, CAP).then_inc(g_turned, 1)

            def expert_gate_up(ex):
                wait_expert(pe, ex)
                pe.wait_ge(gT_ready, ex.n + 1)
                gate_up(ex.n + T, lambda k: xgT[ex.buf][:, k, :], expert_slot(ex))

            def expert_down(ex):
                if isinstance(ex.n, int) and ex.n == 0:
                    pe.wait_ge(shared_added, T)
                else:
                    pe.wait_ge(y_scaled, ex.n)
                down(ex.n + T, expert_slot(ex))

            turn_gathered(Expert(0))
            shared_down(3)
            turn_gathered(Expert(1))
            expert_gate_up(Expert(0))
            place(Expert(3))
            place(Expert(AHEAD))

            def turn(ex):
                if ex.i is not None or ex.c + 1 < E:
                    turn_gathered(ex.next(1))
                turn_hidden(ex.n + (T - 1))
                expert_gate_up(ex)
                if ex.i is not None or ex.c + AHEAD < E:
                    place(ex.next(AHEAD))
                expert_down(ex.next(-1))
            for c in range(1, LOOP0):
                turn(Expert(c))
            with pe.Fori(0, LOOPS) as i:
                for j in range(3):
                    turn(Expert(LOOP0 + j, i))
            for c in range(LAST0, E):
                turn(Expert(c))
            turn_hidden(T + E - 1)
            expert_down(Expert(E - 1))

            def further(j, e):
                pe.wait_ge(ov_onehot, j + 1)
                for t in range(T):
                    ins = mm(bank(6, 9)[0:CAP], onehot[0][:, t, :], moving_flat[:, t, bass.ds(e * 9, 9)],
                             start=(t == 0), stop=(t == T - 1))
                ins.then_inc(ov_placed, 1)
                pe.wait_ge(ov_gathered, 16 * j + 16)
                turn_rows(xg[0], 0, CAP).then_inc(g_turned, 1)
                pe.wait_ge(ring_loaded[0], 48 * j + (per_slot[0] + 48 * EXPERTS_IN_0 + 48))
                pe.wait_ge(gT_ready, j + (E + 1))
                gate_up(j + (E + T), lambda k: xgT[0][:, k, :], 0)
                turn_hidden(j + (E + T))
                pe.wait_ge(y_scaled, j + E)
                down(j + (E + T), 0)

            further_blocks(pe, further)


_INS = ["x", "norm1_g", "w_in", "q_norm_a", "k_norm_a", "q_norm_b", "k_norm_b", "w_branch_a", "w_branch_b",
        "w_out", "norm2_g", "w_router", "router_bias", "we_gate", "we_up", "we_down", "ws_gate", "ws_up",
        "ws_down"]


def kernel(**inputs):
    import concourse.bacc as bacc
    from concourse.bass_utils import run_bass_kernel_spmd

    nc = bacc.Bacc("TRN2", target_bir_lowering=False, num_devices=1)
    arrays = {n: np.ascontiguousarray(inputs[n]) for n in _INS}
    arrays["rope"], arrays["masks"], arrays["misc"] = host_constants()
    arrays = {f"in_{n}": x for n, x in arrays.items()}
    aps = {n[3:]: nc.dram_tensor(n, x.shape, mybir.dt.from_np(x.dtype), kind="ExternalInput").ap()
           for n, x in arrays.items()}
    out = nc.dram_tensor("out", (1, S, D), F32, kind="ExternalOutput").ap()
    xn2_rows = nc.dram_tensor("xn2_rows", (S, D), F32, kind="Internal").ap()
    y_rows = nc.dram_tensor("y_rows", (S * TOPK, D), F32, kind="Internal").ap()
    build(nc, aps, out, xn2_rows, y_rows)
    r = run_bass_kernel_spmd(nc, [arrays], core_ids=[0])
    return r.results[0]["out"]
```

```python
from contextlib import ExitStack

import numpy as np

import concourse.bass as bass
from concourse import mybir

F32 = mybir.dt.float32
F32R = mybir.dt.float32r
BF16 = mybir.dt.bfloat16
I32 = mybir.dt.int32
ALU = mybir.AluOpType
ACT = mybir.ActivationFunctionType
AXIS = mybir.AxisListType

P = 128
S, D = 512, 1024
T = S // P
K = D // P
HD = 64
HALF = 512
GRID_W = 64
THETA = 10000.0
EPS = 1e-6
DILATIONS = (1, 4, 16)
RADIUS = 64
HA, HB, HKV = 4, 8, 2
A_WIDTH = 3 * 3 * HA * HD
E, FF = 64, D // 4
EG, TOPG, TOPK = 8, 4, 8
ROUTED_SCALE = 2.5
MASKED = -1.0e30
AWAY = 65536
CAP = 96
FEWER = (64, 80)
BLOCKS = -(-S // CAP)
NOV = (S * TOPK) // (CAP + 1)

NSLOT = 3
SLOT = 3 * K * FF
QKV_CHUNKS = 6
L_GATE = QKV_CHUNKS
L_OUT = L_GATE + 4
L_SHARED = L_OUT + 2
L_EXPERT = L_SHARED + 1
GATE_COL0 = A_WIDTH + HB * HD + 2 * HKV * HD

QA, KA, QB, KB = range(4)
PAIR_QB = 12
PAIR_KB = 16
NPAIR = 18


def q_pair(g, h):
    return 4 * g + h // 2


def k_pair(g, h):
    return 4 * g + 2 + h // 2


CHUNKS = [
    dict(norm=[(QA, 0, 4, 0, 1), (KA, 256, 4, 4, 1)], value=[], pairs=[0, 1, 2, 3]),
    dict(norm=[(QA, 256, 4, 0, 1)], value=[(0, 256, ("A", 0))], pairs=[4, 5]),
    dict(norm=[(KA, 0, 4, 0, 1)], value=[(256, 256, ("A", 1))], pairs=[6, 7]),
    dict(norm=[(QA, 0, 4, 0, 1), (KA, 256, 4, 4, 1)], value=[], pairs=[8, 9, 10, 11]),
    dict(norm=[(QB, 256, 4, 0, 1)], value=[(0, 256, ("A", 2))], pairs=[12, 13]),
    dict(norm=[(QB, 0, 4, 0, 1), (KB, 256, 2, 4, 2)], value=[(384, 128, ("B", 0))],
         pairs=[14, 15, 16, 17]),
]


def host_constants():
    tok = np.arange(S)

    def angles(pos, dim):
        inv = np.float32(THETA) ** (-np.arange(0, dim, 2, dtype=np.float32) / np.float32(dim))
        a = pos.astype(np.float32)[:, None] * inv[None, :].astype(np.float32)
        sin = np.sin(a)
        return np.concatenate([np.cos(a)] * 2, -1), np.concatenate([-sin, sin], -1)

    c1, s1 = angles(tok, HD)
    cr, sr = angles(tok // GRID_W, HD // 2)
    cc, sc = angles(tok % GRID_W, HD // 2)
    rope = np.stack([c1, s1, np.concatenate([cr, cc], -1), np.concatenate([sr, sc], -1)])
    rope = rope.reshape(4, P, T, HD).transpose(1, 0, 2, 3).reshape(P, 4 * T * HD)
    q, k = np.arange(P)[:, None], np.arange(P)[None, :]
    band = np.stack([np.where(np.abs(4 * (k - q) + d) <= RADIUS, 0.0, MASKED) for d in range(-3, 4)])
    by4 = np.where(np.abs(k - q) <= RADIUS, 0.0, MASKED)
    by16 = np.where((k - q) % 4 == 0, 0.0, MASKED)
    masks = np.concatenate([band.transpose(1, 0, 2).reshape(P, 7 * P), by4, by16], -1)
    ident = np.eye(P)
    below = (q < k).astype(np.float64)
    slots = np.broadcast_to(k, (P, P))
    token = 4 * q + np.arange(T)[None, :]
    parts = np.stack([token % 256, token - token % 256, np.full_like(token, -AWAY)], -1)
    misc = np.concatenate([ident, below, slots, parts.reshape(P, T * 3), S + q], -1)
    return (np.ascontiguousarray(rope, np.float32), np.ascontiguousarray(masks, np.float32),
            np.ascontiguousarray(misc, np.float32))


class Expert:

    def __init__(self, c, i=None):
        self.c, self.i, self.buf = c, i, c % 3
        self.n = c if i is None else 3 * i + c
        self.third = c // 3 if i is None else i + c // 3

    def next(self, d):
        return Expert(self.c + d, self.i)


def wait_for(eng, sem, n):
    if not isinstance(n, int) or n > 0:
        eng.wait_ge(sem, n)


class Steps:

    def __init__(self, eng, sem):
        self.eng, self.sem, self.n, self.at = eng, sem, 0, 0

    def done(self, ins):
        ins.then_inc(self.sem, 1)
        self.n += 1
        return self.n

    def wait(self):
        self.eng.wait_ge(self.sem, self.at + self.n)


def build(nc, a, out, xn2_rows, sum_rows):
    ctx = ExitStack()
    with ctx:
        def sb(name, words, dt=F32):
            return ctx.enter_context(nc.sbuf_tensor(name, [P, words], dt))

        def sem(name):
            return ctx.enter_context(nc.semaphore(name))

        with ExitStack() as under:
            def at(name, words, dt=F32R):
                return under.enter_context(nc.sbuf_tensor(name, [P, words], dt))

            at("under_loaded_chunk", SLOT, F32)
            w_high_t, w_low_t, x_low_t, x_high_t = (at(n, K * HALF) for n in ("w_high", "w_low", "x_low", "x_high"))
            at("under_merged", T * D, F32)
            down_high_t, down_low_t = (at(n, 2 * D) for n in ("down_high", "down_low"))
            at("under_pairs_rest", NPAIR * S - 2 * T * D, F32)
            y_high_t = at("y_high", 6 * S)
            at("under_work_rest", 8 * HALF - 6 * S, F32)
            y_low_t = at("y_low", 6 * S)
        ring = sb("ring", NSLOT * SLOT)
        xT_t = sb("xT", K * S)
        pairs_t = sb("pairs", NPAIR * S)
        work_t = sb("work", 8 * HALF)
        tab_t = sb("tables", 6 * S)
        xs_t = sb("xs", T * D)
        v_t = sb("v", 3 * T * 256 + T * 128)
        mask_t = sb("masks", 9 * P)
        prob_t = sb("prob", 2 * (768 + 2 * HALF))
        misc_t = sb("misc", 3 * P + T * 3 + 1)
        ones_t = sb("ones", P)
        hid_high_t, hid_low_t = sb("hidden_high", 2 * P, F32R), sb("hidden_low", 2 * P, F32R)
        bf_t = sb("consts_bf", 2 * P, BF16)
        small_t = sb("small", 256)
        gain_t = sb("gains", 4 * HD + E)
        ps_t = ctx.enter_context(nc.psum_tensor("banks", [P, 8 * HALF], F32))

        def view(t, off, *shape):
            n = int(np.prod(shape))
            v = t[:, off:off + n]
            if len(shape) == 1:
                return v
            names = "abcd"[:len(shape)]
            return v.rearrange(f"p ({' '.join(names)}) -> p {' '.join(names)}",
                               **{c: s for c, s in zip(names[1:], shape[1:])})

        def bank(b, n=HALF, off=0):
            return ps_t[:, b * HALF + off:b * HALF + off + n]

        xs = view(xs_t, 0, T, D)
        x_high, x_low = view(x_high_t, 0, K, S), view(x_low_t, 0, K, S)
        w_high, w_low = view(w_high_t, 0, K, HALF), view(w_low_t, 0, K, HALF)
        chunk = view(ring, 0, K, HALF)
        branch_w = view(ring, K * HALF, 4, HALF)
        branch_high, branch_low = view(down_high_t, 0, 4, HALF), view(down_low_t, 0, 4, HALF)
        pairs = view(pairs_t, 0, NPAIR, S)
        merged = view(pairs_t, 0, T, D)
        x_full = view(pairs_t, T * D, K, S)
        x2T = view(pairs_t, T * D, K, S)
        vA = view(v_t, 0, T, 3, 256)
        vB = view(v_t, 3 * T * 256, T, 128)
        band = view(mask_t, 0, 7 * P)
        strided_mask = view(mask_t, 7 * P, 2 * P)
        cosg = [view(tab_t, i * T * HD, T, HD) for i in range(4)]
        sing = [view(tab_t, (4 + i) * T * HD, T, HD) for i in range(4)]
        rope_raw = [view(pairs_t, i * T * HD, T, HD) for i in range(4)]
        prob = [view(prob_t, o, w) for o, w in ((0, 768), (768, HALF), (1280, HALF))]
        probT = [view(prob_t, o, w, P) for o, w in ((1792, 6), (2560, 4), (3072, 4))]
        xnorm = [view(prob_t, i * D, D) for i in range(2)]
        y_high, y_low = view(y_high_t, 0, 6, S), view(y_low_t, 0, 6, S)
        squares = [view(work_t, i * HALF, 8, HD) for i in range(2)]
        normed = [view(work_t, (2 + i) * HALF, 8, HD) for i in range(2)]
        turned = [view(work_t, (4 + i) * HALF, 8, HD) for i in range(2)]
        rotated = [view(work_t, (6 + i) * HALF, 8, HD) for i in range(2)]
        ident = misc_t[:, 0:P]
        below_f = misc_t[:, P:2 * P]
        slot_row = misc_t[:, 2 * P:3 * P]
        place_parts = view(misc_t, 3 * P, T, 3)
        spare_row = view(misc_t, 3 * P + T * 3, 1)
        below_b, ones_b = bf_t[:, 0:P], bf_t[:, P:2 * P]
        g1c, g2c = view(small_t, 0, K), view(small_t, K, K)
        ssq, std, rstd = (view(small_t, 16 + 4 * i, T) for i in range(3))
        ssq2, std2, rstd2 = (view(small_t, 28 + 4 * i, T) for i in range(3))
        hss, hstd, hrstd = ([view(small_t, 40 + 16 * i + 8 * j, 8) for j in range(2)] for i in range(3))
        neg_max = [view(small_t, 88 + i, 1) for i in range(3)]
        den = [view(small_t, 91 + i, 1) for i in range(3)]
        rden = [view(small_t, 94 + i, 1) for i in range(3)]
        pmax = [view(small_t, 97 + i, 1) for i in range(2)]
        gains = view(gain_t, 0, 4, HD)
        bias_b = view(gain_t, 4 * HD, E)
        row_t = view(v_t, 0, 4 * HD + E)
        eps_c = small_t[:, 100:101]
        first_root = small_t[:, 101:102]

        gated = [view(v_t, i * HALF, HALF) for i in range(2)]
        gated_b = [view(v_t, (2 + i) * HALF, HALF) for i in range(2)]
        xg = [view(v_t, i * D, D) for i in range(3)]
        xgT = [view(xT_t, i * D, K, P)[:, :, 0:CAP] for i in range(3)]
        h_s = view(xT_t, 3 * D, FF)
        act_s = view(xT_t, 3 * D + FF, FF)
        hT_s = view(xT_t, 3 * D + 2 * FF, 2, P)
        y_s = [view(pairs_t, i * D, D) for i in range(3)]
        down_high, down_low = view(down_high_t, 0, 2, D), view(down_low_t, 0, 2, D)
        hid_high, hid_low = view(hid_high_t, 0, 2, P), view(hid_low_t, 0, 2, P)

        junk1 = view(work_t, 0, D)
        junk2 = view(v_t, 2 * D, D)

        def bank2(b):
            return ps_t[:, b * HALF:(b + 2) * HALF]

        logitsT = view(v_t, 0, S)
        scores = view(prob_t, 0, T, E)
        sel = view(prob_t, 256, T, E)
        selm = view(prob_t, 512, T, E)
        repl = view(prob_t, 768, T, E)
        mask = view(prob_t, 1024, T, E)
        wts = view(prob_t, 1280, T, E)
        pos = view(prob_t, 1536, T, E)
        m8 = view(prob_t, 1792, T, EG, 8)
        low = view(prob_t, 2304, T, E)
        low_ones = view(prob_t, 2816, E)
        tmp_w = view(prob_t, 2560, T, E)
        gs16 = view(work_t, 0, T, 16)
        gr16 = view(work_t, 64, T, 16)
        gm8 = view(work_t, 128, T, 8)
        gpen = view(work_t, 160, T, EG)
        gmask = view(work_t, 192, T, EG)
        top8 = view(work_t, 224, T, 8)
        wsum = view(work_t, 256, T)
        wrec = view(work_t, 260, T)
        cnt = view(work_t, 264, E)
        cnt_i = view(work_t, 336, E).bitcast(I32)
        maskb = view(work_t, 512, T * E // 2).bitcast(BF16).rearrange("p (t e) -> p t e", t=T)
        placed = view(work_t, 704, E, 2)
        placed_i = view(work_t, 896, E, 2).bitcast(I32)
        tok_b = view(work_t, 1088, 4).bitcast(I32)
        dst_b = view(work_t, 1092, 4).bitcast(I32)
        w_b = view(work_t, 1096, 4)
        onehot = [view(tab_t, i * 256, 256).bitcast(BF16).rearrange("p (t s) -> p t s", t=T)[:, :, 0:CAP]
                  for i in range(3)]
        moving = view(tab_t, 768, T * E * 6 // 2).bitcast(BF16).rearrange("p (t e c) -> p t e c", t=T, e=E)
        moving_flat = moving.rearrange("p t e c -> p t (e c)")
        more_f = view(work_t, 1100, E)
        upto_f = view(work_t, 1164, E)
        le_f = view(v_t, 0, NOV, E)
        ov_e = view(work_t, 1228, NOV)
        ov_x = view(work_t, 1276, NOV)
        ov_base = view(work_t, 1324, NOV)
        ov_list = view(work_t, 1372, NOV + 1).bitcast(I32)
        ov_pos = view(work_t, 1424, T)
        ov_placed2 = view(work_t, 1432, 2)
        ov_num = view(work_t, 1443, 1)

        x_loaded = [sem(f"x_loaded{t}") for t in range(T)]
        first_loaded = sem("first_consts_loaded")
        second_loaded = sem("second_consts_loaded")
        row_loaded = sem("gain_row_loaded")
        rope_loaded = sem("rope_loaded")
        chunk_loaded = sem("chunk_loaded")
        router_loaded = sem("router_weights_loaded")
        branch_loaded = sem("branch_weights_loaded")
        branch_high_ready = sem("branch_high_ready")
        branch_low_ready = sem("branch_low_ready")
        branch_used = sem("branch_weights_used")
        w_high_ready = sem("w_high_ready")
        w_low_dve = sem("w_low_ready_dve")
        w_low_pool = sem("w_low_ready_pool")
        piece_used = sem("weight_piece_used")
        x_high_ready = sem("x_high_ready")
        x_low_dve = sem("x_low_ready_dve")
        x_low_pool = sem("x_low_ready_pool")
        m_high_ready = sem("merged_high_ready")
        gains_ready = sem("gains_ready")
        tok_copied = sem("token_index_copied")
        dst_copied = sem("row_index_copied")
        ring_loaded = [sem(f"ring_loaded{i}") for i in range(NSLOT)]
        ones_ready = sem("ones_ready")
        gains_ps = sem("gains_broadcast_ps")
        dve = sem("dve_steps")
        act = sem("act_steps")
        pool = sem("pool_steps")
        tables_ready = sem("tables_ready")
        std1_ready = sem("std1_ready")
        xn_ready = sem("xn_ready")
        xn_turned = sem("xn_turned")
        xT_ready = sem("xT_ready")
        proj_done = sem("proj_done")
        squares_ready = sem("squares_ready")
        sums_ready = sem("sums_ready")
        hstd_ready = sem("hstd_ready")
        normed_ready = sem("normed_ready")
        cos_done = sem("cos_done")
        rotated_ready = sem("rotated_ready")
        pairs_turned = sem("pairs_turned")
        pairs_ready = sem("pairs_ready")
        scores_done = sem("scores_done")
        max_ready = sem("max_ready")
        probs_ready = sem("probs_ready")
        probs_turned = sem("probs_turned")
        probT_act = sem("probT_act")
        probT_dve = sem("probT_dve")
        pv_done = sem("pv_done")
        probs_scaled = sem("probs_scaled")
        yT_a_ready = sem("yT_a_ready")
        yT_b_ready = sem("yT_b_ready")
        gate_done = sem("gate_done")
        gated_ready = sem("gated_ready")
        product_ready = sem("product_ready")
        merged_ready = sem("merged_ready")
        merged_turned = sem("merged_turned")
        mT_ready = sem("mT_ready")
        out_done = sem("out_done")
        h_ready = sem("h_ready")
        std2_ready = sem("std2_ready")
        xn2_ready = sem("xn2_ready")
        xn2_stored = [sem(f"xn2_stored{i}") for i in range(2)]
        x2_turned = sem("x2_turned")
        x2T_ready = sem("x2T_ready")
        router_done = sem("router_done")
        logitsT_ready = sem("logitsT_ready")
        logits_done = sem("logits_done")
        scores_ready = sem("scores_ready")
        mask_ready = sem("mask_ready")
        pos_done = sem("pos_done")
        moving_ready = sem("moving_ready")
        onehot_ready = sem("onehot_ready")
        placed_done = sem("placed_done")
        parts_summed = sem("parts_summed")
        index_ready = sem("index_ready")
        gu_done = sem("gate_up_done")
        silu_ready = sem("silu_ready")
        hid_ready = sem("hidden_ready")
        hid_turned = sem("hidden_turned")
        hidT_ready = sem("hiddenT_ready")
        down_done = sem("down_done")
        down_high_ready = sem("down_high_ready")
        down_low_dve = sem("down_low_ready_dve")
        down_low_pool = sem("down_low_ready_pool")
        hid_high_ready = sem("hidden_high_ready")
        shared_added = sem("shared_added")
        w_ready = sem("slot_weight_ready")
        y_scaled = sem("y_scaled")
        gathered = [sem(f"gathered{i}") for i in range(3)]
        g_turned = sem("gathered_turned")
        gT_ready = sem("gatheredT_ready")
        scattered = [sem(f"scattered{i}") for i in range(3)]
        more_counted = sem("further_blocks_counted")
        more_listed = sem("further_blocks_listed")
        further_step = sem("further_index_steps")
        ov_onehot = sem("further_onehot_ready")
        ov_placed = sem("further_index_product_done")
        ov_indexed = sem("further_index_ready")
        ov_gathered = sem("further_gathered")
        ov_scattered = sem("further_scattered")
        pool_waited = sem("pool_waited")
        more_ended = sem("further_block_ended")
        rows_zeroed = sem("rows_zeroed")
        spare_stored = sem("spare_rows_stored")
        stream_stored = sem("stream_stored")
        out_stored = sem("out_stored")

        x_rows = a["x"][0].rearrange("(p t) d -> p t d", t=T)
        w_in = a["w_in"][0].rearrange("(p k) n -> p k n", k=K)
        w_out = a["w_out"][0].rearrange("(p k) n -> p k n", k=K)
        wba = a["w_branch_a"][0].rearrange("(j p) n -> p j n", p=P)
        wbb = a["w_branch_b"][0].rearrange("(j p) n -> p j n", p=P)
        w_router = a["w_router"][0].rearrange("(p k) e -> p k e", k=K)
        wr = view(v_t, 3 * D, K, E)
        xn2_t = xn2_rows.rearrange("(p t) d -> p t d", t=T)
        sum_t = sum_rows[0:S].rearrange("(p t) d -> p t d", t=T)

        def slot(load):
            return ring[:, (load % NSLOT) * SLOT:(load % NSLOT + 1) * SLOT]

        def high_of(eng, dst, src):
            return eng.copy(dst, src)

        def low_of(eng, dst, src, high):
            return eng.tensor_tensor(dst, src, high.bitcast(F32), ALU.subtract)

        def low_piece(n, k):
            if n == 0:
                return w_low_dve, k + 1
            if k % 2 == 0:
                return w_low_dve, K + K // 2 * (n - 1) + k // 2 + 1
            return w_low_pool, K // 2 * (n - 1) + k // 2 + 1

        def wait_split(eng, n):
            for k in (K - 2, K - 1):
                eng.wait_ge(*low_piece(n, k))

        def wait_chunk_used(eng, n, k):
            if k < K - 1:
                eng.wait_ge(piece_used, (K - 1) * n + k + 1)
            elif n < L_GATE:
                eng.wait_ge(proj_done, T * (n + 1))
            elif n < L_OUT:
                eng.wait_ge(gate_done, T * (n + 1 - L_GATE))
            else:
                eng.wait_ge(out_done, T * (n + 1 - L_OUT))

        X_LOW = [(x_low_pool, 1), (x_low_dve, 1), (x_low_pool, 2), (x_low_pool, 3)]

        def x_low_part(eng, waiter, t, done):
            waiter.wait_ge(x_high_ready, t + 1)
            own = slice(t * P, (t + 1) * P)
            low_of(eng, x_low[:, :, own], x_full[:, :, own], x_high[:, :, own]).then_inc(done, 1)

        def split_low(eng, waiter, n, pieces, done):
            for k in pieces:
                waiter.wait_ge(w_high_ready, K * n + k + 1)
                low_of(eng, w_low[:, k, :], chunk[:, k, :], w_high[:, k, :]).then_inc(done, 1)

        def split_down_low(eng, waiter, ex, c, done):
            waiter.wait_ge(down_high_ready, ex.n + 1)
            _, w = ffn_parts(expert_slot(ex))
            low_of(eng, down_low[:, c, :], w[:, c, :], down_high[:, c, :]).then_inc(done, 1)

        per_slot = [3 * 16 if L_SHARED % NSLOT == i else 0 for i in range(NSLOT)]

        def wait_load(eng, n):
            eng.wait_ge(ring_loaded[n % NSLOT], per_slot[n % NSLOT])

        def expert_slot(ex):
            return (L_EXPERT + ex.c) % NSLOT

        def wait_expert(eng, ex):
            s = expert_slot(ex)
            eng.wait_ge(ring_loaded[s], per_slot[s] + 48 * (ex.third + 1))

        EXPERTS_IN_0 = sum((L_EXPERT + e) % NSLOT == 0 for e in range(E))

        def ffn_parts(s):
            w = ring[:, s * SLOT:(s + 1) * SLOT]
            return (w[:, 0:2 * K * FF].rearrange("p (s k f) -> p s k f", s=2, k=K),
                    w[:, 2 * K * FF:].rearrange("p (c d) -> p c d", c=2))

        NP = QKV_CHUNKS * T
        UNITS = []
        for r in range(T * HA):
            t, h = divmod(r, HA)
            UNITS += [("A", t, h), ("B", t, 2 * h), ("B", t, 2 * h + 1)]
        NU = len(UNITS)
        NM = 2 * 2 * T
        BRANCH_ROWS = (HA * HD // P, HB * HD // P)
        LOOP0, LOOPS = 4, (E - 8) // 3
        LAST0 = LOOP0 + 3 * LOOPS
        AHEAD = 4

        block = ctx.enter_context(nc.Block())

        def further_blocks(eng, body):
            eng.wait_ge(more_counted, 1)
            count = eng.value_load(ov_list[0:1, 0:1], min_val=0, max_val=NOV)
            with eng.If(count > 0):
                eng.wait_ge(more_listed, 1)
                with eng.Fori(0, count) as j:
                    body(j, eng.value_load(ov_list[0:1, bass.ds(j + 1, 1)], min_val=0, max_val=E - 1))

        @block.sync
        def _(sp):
            for t in range(T):
                sp.dma_start(xs[:, t, :], x_rows[:, t, :]).then_inc(x_loaded[t], 16)
                if t == 0:
                    sp.dma_start(misc_t[:, :], a["misc"]).then_inc(first_loaded, 16)
                    sp.dma_start(g1c, a["norm1_g"].rearrange("o (p k) -> (o p) k", k=K)).then_inc(first_loaded, 16)
                if t == 2:
                    for dst, src in [
                        (row_t[0:1, 0:64], a["q_norm_a"]), (row_t[0:1, 64:128], a["k_norm_a"]),
                        (row_t[0:1, 128:192], a["q_norm_b"]), (row_t[0:1, 192:256], a["k_norm_b"]),
                        (row_t[0:1, 256:320], a["router_bias"]),
                    ]:
                        sp.dma_start(dst, src).then_inc(row_loaded, 16)

            for n in range(L_SHARED):
                if n >= 1:
                    wait_split(sp, n - 1)
                if n == L_GATE + 2:
                    sp.wait_ge(gate_done, 1)
                    sp.dma_start(wr, w_router).then_inc(router_loaded, 16)
                if L_GATE <= n < L_OUT:
                    half, br = divmod(n - L_GATE, 2)
                    if n > L_GATE:
                        sp.wait_ge(branch_low_ready, n - L_GATE)
                    src, rows = ((wba, 2), (wbb, 4))[br]
                    sp.dma_start(branch_w[:, 0:rows, :], src[:, :, half * HALF:(half + 1) * HALF]
                                 ).then_inc(branch_loaded, 16)
                if n < L_GATE:
                    src, c0 = w_in, n * HALF
                elif n < L_OUT:
                    half, br = divmod(n - L_GATE, 2)
                    src, c0 = w_in, GATE_COL0 + br * D + half * HALF
                else:
                    src, c0 = w_out, (n - L_OUT) * HALF
                sp.dma_start(chunk, src[:, :, c0:c0 + HALF]).then_inc(chunk_loaded, 16)
                if n == 0:
                    sp.dma_start(pairs_t[:, 0:4 * T * HD], a["rope"]).then_inc(rope_loaded, 16)
                if n == 1:
                    for dst, src in [
                        (mask_t[:, :], a["masks"]),
                        (g2c, a["norm2_g"].rearrange("o (p k) -> (o p) k", k=K)),
                    ]:
                        sp.dma_start(dst, src).then_inc(second_loaded, 16)

            def load(n, dst, src):
                sp.dma_start(dst, src).then_inc(ring_loaded[n % NSLOT], 16)

            def load_ffn(n, gate, up, down):
                w = slot(n)
                load(n, w[:, 0:K * FF], gate.rearrange("(p k) f -> p (k f)", k=K))
                load(n, w[:, K * FF:2 * K * FF], up.rearrange("(p k) f -> p (k f)", k=K))
                load(n, w[:, 2 * K * FF:], down.rearrange("(p c) d -> p (c d)", c=2))

            wait_split(sp, L_SHARED - 1)
            sp.wait_ge(gate_done, NM)
            load_ffn(L_SHARED, a["ws_gate"][0], a["ws_up"][0], a["ws_down"][0])

            def store_xn2(t):
                sp.wait_ge(xn2_ready, t + 1)
                sp.dma_start(xn2_t[:, t, :], xnorm[t % 2]).then_inc(xn2_stored[t % 2], 16)

            def load_expert(ex, free_sem, free_at):
                if free_sem is not None:
                    sp.wait_ge(free_sem, free_at)
                n = ex.n
                load_ffn(L_EXPERT + ex.c, pick(a["we_gate"][0], n), pick(a["we_up"][0], n),
                         pick(a["we_down"][0], n))

            def pick(w, n):
                if isinstance(n, int):
                    return w[n]
                return w[bass.ds(n, 1)].rearrange("o r c -> (o r) c")

            for t in range(T - 1):
                store_xn2(t)
            load_expert(Expert(0), out_done, 2 * T)
            store_xn2(T - 1)
            load_expert(Expert(1), out_done, 2 * T)

            def store_stream(t):
                sp.wait_ge(shared_added, t + 1)
                sp.dma_start(sum_t[:, t, :], xs[:, t, :]).then_inc(stream_stored, 16)

            store_stream(0)
            sp.wait_ge(rows_zeroed, 1)
            sp.dma_start(sum_rows[S:S + CAP, :], xg[2][0:CAP]).then_inc(spare_stored, 16)
            store_stream(1)
            store_stream(2)
            load_expert(Expert(2), down_done, T)
            store_stream(3)
            load_expert(Expert(3), down_done, T + 1)
            with sp.Fori(0, LOOPS) as i:
                for j in range(3):
                    ex = Expert(LOOP0 + j, i)
                    load_expert(ex, down_done, ex.n + (T - 2))
            for c in range(LAST0, E):
                load_expert(Expert(c), down_done, c + T - 2)

            def further(j, e):
                sp.wait_ge(down_done, j + (E + T))
                w = ring[:, 0:SLOT]
                for i, name in enumerate(("we_gate", "we_up")):
                    sp.dma_start(w[:, i * K * FF:(i + 1) * K * FF],
                                 pick(a[name][0], e).rearrange("(p k) f -> p (k f)", k=K)
                                 ).then_inc(ring_loaded[0], 16)
                sp.dma_start(w[:, 2 * K * FF:], pick(a["we_down"][0], e).rearrange("(p c) d -> p (c d)", c=2)
                             ).then_inc(ring_loaded[0], 16)
                sp.wait_ge(ov_scattered, 16 * j + 16)
                sp.sem_inc(more_ended, 1)

            further_blocks(sp, further)
            for b in range(3):
                sp.wait_ge(scattered[b], 16 * ((E - b + 2) // 3))
            sp.dma_start(out[0], sum_rows[0:S]).then_inc(out_stored, 16)
            sp.wait_ge(out_stored, 16)

        @block.scalar
        def _(act_e):
            act_e.wait_ge(ones_ready, 1)
            nc.scalar.activation(first_root, eps_c, ACT.Sqrt)
            for t in range(T):
                act_e.wait_ge(x_loaded[t], 16)
                nc.scalar.activation(junk1, xs[:, t, :], ACT.Square, accum_out=ssq[:, t:t + 1]).then_inc(act, 1)
                act_e.wait_ge(act, t + 1)
                nc.scalar.activation(std[:, t:t + 1], ssq[:, t:t + 1], ACT.Sqrt, bias=eps_c,
                                     scale=1.0 / D).then_inc(std1_ready, 1)

            def x_high_part(t):
                act_e.wait_ge(xT_ready, t + 1)
                own = slice(t * P, (t + 1) * P)
                high_of(nc.scalar, x_high[:, :, own], x_full[:, :, own]).then_inc(x_high_ready, 1)

            for t in range(T - 1):
                x_high_part(t)

            def split_high(n):
                act_e.wait_ge(chunk_loaded, 16 * (n + 1))
                for k in range(K):
                    high_piece(n, k)

            def high_piece(n, k):
                if n >= 1:
                    wait_chunk_used(act_e, n - 1, k)
                high_of(nc.scalar, w_high[:, k, :], chunk[:, k, :]).then_inc(w_high_ready, 1)

            split_high(0)
            x_high_part(T - 1)

            def store_pairs(m):
                c, t = divmod(m, T)
                pr = CHUNKS[c]["pairs"]
                act_e.wait_ge(pairs_turned, m + 1)
                if m == 0:
                    act_e.wait_ge(tables_ready, 1)
                nc.scalar.copy(pairs[:, pr[0]:pr[0] + len(pr), t * P:(t + 1) * P],
                               bank(4 + m % 2, len(pr) * P).rearrange("p (j q) -> p j q", q=P)
                               ).then_inc(pairs_ready, 1)

            for m in range(NP):
                c, t = divmod(m, T)
                act_e.wait_ge(proj_done, m + 1)
                wait_for(act_e, sums_ready, m - 1)
                nc.scalar.activation(squares[m % 2], bank(m % 4).rearrange("p (h d) -> p h d", d=HD),
                                     ACT.Square).then_inc(squares_ready, 1)
                for c0, n, (br, g) in CHUNKS[c]["value"]:
                    dst = vA[:, t, g, :] if br == "A" else vB[:, t, :]
                    nc.scalar.copy(dst, bank(m % 4, n, c0))
                act_e.wait_ge(sums_ready, m + 1)
                wait_for(act_e, normed_ready, m - 1)
                nc.scalar.activation(hstd[m % 2], hss[m % 2], ACT.Sqrt, bias=eps_c,
                                     scale=1.0 / HD).then_inc(hstd_ready, 1)
                if m >= 1:
                    store_pairs(m - 1)
                if t == T - 2 and c + 1 < QKV_CHUNKS:
                    split_high(c + 1)
            nc.scalar.activation(first_root, eps_c, ACT.Exp)
            store_pairs(NP - 1)

            for n in range(NU + 1):
                if n == 3:
                    act_e.wait_ge(chunk_loaded, 16 * (L_GATE + 1))
                if 3 <= n < 3 + K:
                    high_piece(L_GATE, n - 3)
                if n < NU:
                    a_unit, i = n % 3 == 0, n % 3
                    act_e.wait_ge(max_ready, n + 1)
                    wait_for(act_e, probs_turned, n - 2)
                    nc.scalar.activation(prob[i], prob[i] if a_unit else bank(1 + i), ACT.Exp, bias=neg_max[i],
                                         accum_out=den[i]).then_inc(probs_ready, 1)
                if n >= 1:
                    m = n - 1
                    act_e.wait_ge(probs_turned, m + 1)
                    wait_for(act_e, pv_done, m - 2)
                    nc.scalar.copy(probT[m % 3][:, 0:4, :],
                                   bank(5 if m % 3 == 2 else 4).rearrange("p (j q) -> p j q", q=P)
                                   ).then_inc(probT_act, 1)

            def split_branch_high(hb):
                act_e.wait_ge(branch_loaded, 16 * (hb + 1))
                if hb == 0:
                    act_e.wait_ge(scores_done, NU)
                else:
                    act_e.wait_ge(branch_used, hb)
                rows = BRANCH_ROWS[hb % 2]
                high_of(nc.scalar, branch_high[:, 0:rows, :], branch_w[:, 0:rows, :]).then_inc(branch_high_ready, 1)

            split_branch_high(0)
            for m in range(NM):
                act_e.wait_ge(gate_done, m + 1)
                wait_for(act_e, product_ready, m - 1)
                nc.scalar.activation(gated[m % 2], bank(4 + 2 * (m % 2)), ACT.Sigmoid).then_inc(gated_ready, 1)
                if m % T == T - 2:
                    split_high(L_GATE + m // T + 1)
                    if m // T < 3:
                        split_branch_high(m // T + 1)
            for t in range(T):
                act_e.wait_ge(merged_turned, t + 1)
                for h in range(2):
                    ins = high_of(nc.scalar, x_high[:, 4 * h:4 * h + 4, t * P:(t + 1) * P],
                                  bank(2 * (t % 2) + h).rearrange("p (j q) -> p j q", q=P))
                ins.then_inc(m_high_ready, 1)
            split_high(L_OUT + 1)
            for t in range(T):
                act_e.wait_ge(h_ready, T + t + 1)
                nc.scalar.activation(junk2, xs[:, t, :], ACT.Square, accum_out=ssq2[:, t:t + 1]).then_inc(act, 1)
                act_e.wait_ge(act, T + t + 1)
                nc.scalar.activation(std2[:, t:t + 1], ssq2[:, t:t + 1], ACT.Sqrt, bias=eps_c,
                                     scale=1.0 / D).then_inc(std2_ready, 1)

            def silu(u, m=CAP):
                act_e.wait_ge(gu_done, u + 1)
                wait_for(act_e, hid_ready, u)
                nc.scalar.activation(act_s[0:m], bank(2, FF)[0:m], ACT.Silu).then_inc(silu_ready, 1)

            def scale_rows(ex):
                act_e.wait_ge(down_done, ex.n + (T + 1))
                act_e.wait_ge(w_ready, ex.n + 1)
                wait_for(act_e, scattered[ex.buf], 16 * ex.third)
                nc.scalar.activation(y_s[ex.buf][0:CAP], bank2(4)[0:CAP], ACT.Copy,
                                     scale=w_b[0:CAP, ex.buf:ex.buf + 1]).then_inc(y_scaled, 1)

            silu(0, P)
            act_e.wait_ge(router_done, T)
            nc.scalar.copy(logitsT[0:E], bank(7)[0:E]).then_inc(logitsT_ready, 1)
            act_e.wait_ge(logits_done, 1)
            for i in range(2):
                act_e.wait_ge(xn2_stored[i], 16 * (T // 2))
            nc.scalar.activation(scores, bank(6, T * E).rearrange("p (t e) -> p t e", e=E),
                                 ACT.Sigmoid).then_inc(scores_ready, 1)
            for u in range(1, T):
                silu(u, P)

            def split_down_high(ex):
                wait_expert(act_e, ex)
                if isinstance(ex.n, int) and ex.n == 0:
                    act_e.wait_ge(gu_done, T)
                else:
                    act_e.wait_ge(down_done, ex.n + T)
                _, w = ffn_parts(expert_slot(ex))
                high_of(nc.scalar, down_high, w).then_inc(down_high_ready, 1)

            silu(T)
            split_down_high(Expert(0))
            for c in range(1, LOOP0):
                silu(T + c)
                scale_rows(Expert(c - 1))
                if c < E - 1:
                    split_down_high(Expert(c))
            with act_e.Fori(0, LOOPS) as i:
                for j in range(3):
                    ex = Expert(LOOP0 + j, i)
                    silu(ex.n + T)
                    scale_rows(ex.next(-1))
                    split_down_high(ex)
            for c in range(LAST0, E):
                silu(T + c)
                scale_rows(Expert(c - 1))
                if c < E - 1:
                    split_down_high(Expert(c))
            scale_rows(Expert(E - 1))

            def further(j, e):
                silu(j + (E + T))
                act_e.wait_ge(down_done, j + (E + T + 1))
                nc.scalar.activation(y_s[0][0:CAP], bank2(4)[0:CAP], ACT.Copy,
                                     scale=w_b[0:CAP, 0:1]).then_inc(y_scaled, 1)

            further_blocks(act_e, further)

        @block.vector
        def _(v):
            step = Steps(v, dve)
            nc.vector.memset(ones_t[:, :], 1.0)
            nc.vector.memset(eps_c, EPS).then_inc(ones_ready, 1)

            def spread(col, n, w):
                return col.unsqueeze(2).to_broadcast([P, n, w])

            def norm_rows(t, std_sem, std_c, rstd_c, waits):
                v.wait_ge(std_sem, t + 1)
                step.done(nc.vector.reciprocal(rstd_c[:, t:t + 1], std_c[:, t:t + 1]))
                step.wait()
                for s_, n_ in waits:
                    wait_for(v, s_, n_)
                return nc.vector.tensor_scalar(xnorm[t % 2], xs[:, t, :], rstd_c[:, t:t + 1], None, ALU.mult)

            def store_turned(t, src0, gain, dst):
                for h in range(2):
                    ins = nc.vector.tensor_tensor(
                        dst[:, 4 * h:4 * h + 4, t * P:(t + 1) * P],
                        bank(src0 + h).rearrange("p (j q) -> p j q", q=P),
                        spread(gain[:, 4 * h:4 * h + 4], 4, P), ALU.mult)
                return ins

            v.wait_ge(first_loaded, 16 * 2)
            nc.vector.tensor_copy(below_b, below_f)
            nc.vector.memset(ones_b, 1.0)
            for t in range(T + 1):
                if t == 2:
                    v.wait_ge(gains_ps, 1)
                    for i, f in enumerate((0.125, 1.0, 0.125, 1.0)):
                        nc.vector.tensor_scalar(gains[:, i, :], bank(7, HD, i * HD), f, None, ALU.mult)
                    nc.vector.tensor_copy(bias_b, bank(7, E, 4 * HD)).then_inc(gains_ready, 1)
                if t < T:
                    norm_rows(t, std1_ready, std, rstd, [(xn_turned, t - 1)]).then_inc(xn_ready, 1)
                if t >= 1:
                    v.wait_ge(xn_turned, t)
                    store_turned(t - 1, 2 * ((t - 1) % 2), g1c, x_full).then_inc(xT_ready, 1)
            split_low(nc.vector, v, 0, range(K), w_low_dve)
            x_low_part(nc.vector, v, 1, x_low_dve)

            for m in range(NP):
                c, t = divmod(m, T)
                b = m % 2
                v.wait_ge(squares_ready, m + 1)
                nc.vector.tensor_reduce(hss[b], squares[b], AXIS.X, ALU.add).then_inc(sums_ready, 1)
                v.wait_ge(hstd_ready, m + 1)
                step.done(nc.vector.reciprocal(hrstd[b], hstd[b]))
                step.wait()
                wait_for(v, cos_done, m - 1)
                nc.vector.tensor_tensor(normed[b], bank(m % 4).rearrange("p (h d) -> p h d", d=HD),
                                        spread(hrstd[b], 8, HD), ALU.mult).then_inc(normed_ready, 1)
                v.wait_ge(normed_ready, m + 1)
                if m == 0:
                    v.wait_ge(tables_ready, 1)
                heads = 0
                for kind, c0, n, o0, copies in CHUNKS[c]["norm"]:
                    blocks = 1 if kind in (QA, KA) else 2
                    hw = HD // (2 * blocks)
                    src = normed[b][:, c0 // HD:c0 // HD + n, :].rearrange("p h (b s x) -> p h b s x", b=blocks, s=2)
                    tab = sing[kind][:, t, :].rearrange("p (b s x) -> p b s x", b=blocks, s=2)
                    for cp in range(copies):
                        dst = turned[b][:, o0 + cp:o0 + cp + copies * (n - 1) + 1:copies, :].rearrange(
                            "p h (b s x) -> p h b s x", b=blocks, s=2)
                        for s_ in range(2):
                            if blocks == 1:
                                last = nc.vector.tensor_tensor(
                                    dst[:, :, 0, s_, :], src[:, :, 0, 1 - s_, :],
                                    tab[:, 0, s_, :].unsqueeze(1).to_broadcast([P, n, hw]), ALU.mult)
                            else:
                                last = nc.vector.tensor_tensor(
                                    dst[:, :, :, s_, :], src[:, :, :, 1 - s_, :],
                                    tab[:, :, s_, :].unsqueeze(1).to_broadcast([P, n, blocks, hw]), ALU.mult)
                    heads = o0 + n * copies
                step.done(last)
                step.wait()
                v.wait_ge(cos_done, m + 1)
                nc.vector.tensor_tensor(rotated[b][:, 0:heads, :], rotated[b][:, 0:heads, :],
                                        turned[b][:, 0:heads, :], ALU.add).then_inc(rotated_ready, 1)
                if t == T - 2 and c + 1 < QKV_CHUNKS:
                    split_low(nc.vector, v, c + 1, range(0, K, 2), w_low_dve)

            for n in range(NU + 3):
                if 5 <= n < 5 + K and n % 2:
                    split_low(nc.vector, v, L_GATE, [n - 5], w_low_dve)
                if n < NU:
                    br, t, h = UNITS[n]
                    i = n % 3
                    v.wait_ge(scores_done, n + 1)
                    if br == "A":
                        wait_for(v, probs_turned, n - 2)
                        if n == 0:
                            v.wait_ge(second_loaded, 16 * 2)
                        nc.vector.tensor_tensor_reduce(
                            out=prob[0][:, 0:HALF], in0=bank(0), in1=band[:, (3 - t) * P:(7 - t) * P],
                            scale=1.0, scalar=-3.0e38, op0=ALU.add, op1=ALU.max, accum_out=pmax[0])
                        step.done(nc.vector.tensor_tensor_reduce(
                            out=prob[0][:, HALF:768], in0=bank(1, 256), in1=strided_mask,
                            scale=1.0, scalar=-3.0e38, op0=ALU.add, op1=ALU.max, accum_out=pmax[1]))
                        step.wait()
                        nc.vector.tensor_scalar(neg_max[0], pmax[0], pmax[1], -1.0,
                                                ALU.max, ALU.mult).then_inc(max_ready, 1)
                    else:
                        wait_for(v, probs_ready, n - 2)
                        nc.vector.tensor_reduce(neg_max[i], bank(1 + i), AXIS.X, ALU.max,
                                                negate=True).then_inc(max_ready, 1)
                if 1 <= n <= NU:
                    m = n - 1
                    i = m % 3
                    v.wait_ge(probs_ready, m + 1)
                    step.done(nc.vector.reciprocal(rden[i], den[i]))
                    step.wait()
                    nc.vector.tensor_scalar(prob[i], prob[i], rden[i], None, ALU.mult).then_inc(probs_scaled, 1)
                if 2 <= n <= NU + 1 and (n - 2) % 3 == 0:
                    m = n - 2
                    v.wait_ge(probs_turned, m + 1)
                    wait_for(v, pv_done, m - 2)
                    nc.vector.tensor_copy(probT[0][:, 4:6, :], bank(5, 2 * P).rearrange("p (j q) -> p j q", q=P)
                                          ).then_inc(probT_dve, 1)
                if n >= 3:
                    m = n - 3
                    br, t, h = UNITS[m]
                    if h % 2:
                        v.wait_ge(pv_done, m + 1)
                        j, b, ready = (h // 2, 7, yT_a_ready) if br == "A" else (2 + h // 2, 6, yT_b_ready)
                        own = slice(t * P, (t + 1) * P)
                        step.done(nc.vector.tensor_copy(y_high[:, j, own], bank(b, P)))
                        step.wait()
                        low_of(nc.vector, y_low[:, j, own], bank(b, P), y_high[:, j, own]).then_inc(ready, 1)

            def split_branch_low(hb):
                v.wait_ge(branch_high_ready, hb + 1)
                rows = BRANCH_ROWS[hb % 2]
                low_of(nc.vector, branch_low[:, 0:rows, :], branch_w[:, 0:rows, :],
                       branch_high[:, 0:rows, :]).then_inc(branch_low_ready, 1)

            split_branch_low(0)
            for m in range(NM):
                hb, t = divmod(m, T)
                half, br = divmod(hb, 2)
                v.wait_ge(gated_ready, m + 1)
                if br == 0:
                    dst = merged[:, t, half * HALF:(half + 1) * HALF]
                else:
                    i = half * T + t
                    wait_for(v, merged_ready, i - 1)
                    dst = gated_b[i % 2]
                nc.vector.tensor_tensor(dst, gated[m % 2], bank(5 + 2 * (m % 2)), ALU.mult).then_inc(product_ready, 1)
                if t == T - 2:
                    split_low(nc.vector, v, L_GATE + hb + 1, range(0, K, 2), w_low_dve)
                    if hb < 3:
                        split_branch_low(hb + 1)
            def merged_low(t):
                v.wait_ge(m_high_ready, t + 1)
                for h in range(2):
                    ks, own = slice(4 * h, 4 * h + 4), slice(t * P, (t + 1) * P)
                    ins = low_of(nc.vector, x_low[:, ks, own],
                                 bank(2 * (t % 2) + h).rearrange("p (j q) -> p j q", q=P), x_high[:, ks, own])
                ins.then_inc(mT_ready, 1)

            def residual(half, t):
                o = half * T + t
                v.wait_ge(out_done, o + 1)
                x_part = xs[:, t, half * HALF:(half + 1) * HALF]
                nc.vector.tensor_tensor(x_part, x_part, bank(4 + o % 3), ALU.add).then_inc(h_ready, 1)

            merged_low(0)
            merged_low(1)
            for t in range(T):
                if t == T - 1:
                    split_low(nc.vector, v, L_OUT + 1, range(0, K, 2), w_low_dve)
                residual(0, t)
                if t + 2 < T:
                    merged_low(t + 2)
            for t in range(T + 1):
                if t < T:
                    residual(1, t)
                if t >= 1:
                    v.wait_ge(x2_turned, t)
                    store_turned(t - 1, 0, g2c, x2T).then_inc(x2T_ready, 1)
                if t < T:
                    norm_rows(t, std2_ready, std2, rstd2,
                              [(x2_turned, t - 1), (xn2_stored[t % 2], 16 * (t // 2))]).then_inc(xn2_ready, 1)

            def group(x):
                return x.rearrange("p t (g e) -> p t g e", e=8)

            def route_a():
                v.wait_ge(scores_ready, 1)
                for i in range(2):
                    v.wait_ge(xn2_stored[i], 16 * (T // 2))
                step.done(nc.vector.tensor_tensor(sel, scores, bias_b.unsqueeze(1).to_broadcast([P, T, E]), ALU.add))
                nc.vector.memset(gs16, MASKED)
                nc.vector.memset(low_ones, 1.0)
                step.done(nc.vector.memset(low, 1.0))
                step.wait()
                for t in range(T):
                    for g in range(EG):
                        ins = nc.vector.max(out=m8[:, t, g, :], in_=sel[:, t, 8 * g:8 * g + 8])
                step.done(ins)
                step.wait()
                step.done(nc.vector.tensor_tensor(gs16[:, :, 0:EG], m8[:, :, :, 0], m8[:, :, :, 1], ALU.add))
                step.wait()

            def route_b():
                for t in range(T):
                    ins = nc.vector.max(out=gm8[:, t, :], in_=gs16[:, t, :])
                step.done(ins)
                step.wait()
                step.done(nc.vector.memset(gm8[:, :, TOPG:8], MASKED))
                step.wait()
                for t in range(T):
                    ins = nc.vector.match_replace(out=gr16[:, t, :], in_to_replace=gm8[:, t, :],
                                                  in_values=gs16[:, t, :], imm_value=2 * MASKED)
                step.done(ins)
                step.wait()
                step.done(nc.vector.tensor_tensor(gmask, gr16[:, :, 0:EG], gs16[:, :, 0:EG], ALU.not_equal))
                step.wait()
                nc.vector.tensor_scalar(gpen, gmask, -MASKED, MASKED, ALU.mult, ALU.add)
                step.done(nc.vector.tensor_tensor(group(selm), group(sel),
                                                  gmask.unsqueeze(3).to_broadcast([P, T, EG, 8]), ALU.mult))
                step.wait()
                step.done(nc.vector.tensor_tensor(group(selm), group(selm),
                                                  gpen.unsqueeze(3).to_broadcast([P, T, EG, 8]), ALU.add))
                step.wait()
                for t in range(T):
                    ins = nc.vector.max(out=top8[:, t, :], in_=selm[:, t, :])
                step.done(ins)
                step.wait()
                for t in range(T):
                    ins = nc.vector.match_replace(out=repl[:, t, :], in_to_replace=top8[:, t, :],
                                                  in_values=selm[:, t, :], imm_value=3 * MASKED)
                step.done(ins)
                step.wait()
                step.done(nc.vector.tensor_tensor(mask, repl, selm, ALU.not_equal))
                step.wait()
                nc.vector.tensor_copy(maskb, mask).then_inc(mask_ready, 1)

            def route_c():
                step.done(nc.vector.tensor_tensor(wts, scores, mask, ALU.mult))
                step.wait()
                step.done(nc.vector.tensor_reduce(wsum, wts, AXIS.X, ALU.add))
                step.wait()
                step.done(nc.vector.reciprocal(wrec, wsum))
                step.wait()
                step.done(nc.vector.tensor_scalar(wrec, wrec, ROUTED_SCALE, None, ALU.mult))
                step.wait()
                step.done(nc.vector.tensor_tensor(wts, wts, spread(wrec, T, E), ALU.mult))
                step.wait()

            def route_d():
                for t in range(T):
                    nc.vector.tensor_copy(moving[:, t, :, 0:3],
                                          place_parts[:, t, :].unsqueeze(1).to_broadcast([P, E, 3]))
                step.done(nc.vector.tensor_copy(moving[:, :, :, 3], wts))
                step.wait()
                step.done(nc.vector.tensor_tensor(low, wts, moving[:, :, :, 3], ALU.subtract))
                step.wait()
                step.done(nc.vector.tensor_copy(moving[:, :, :, 4], low))
                step.wait()
                step.done(nc.vector.tensor_tensor(tmp_w, low, moving[:, :, :, 4], ALU.subtract))
                step.wait()
                step.done(nc.vector.tensor_copy(moving[:, :, :, 5], tmp_w))
                step.wait()
                step.done(nc.vector.tensor_scalar(pos, mask, -4096.0, 4096.0, ALU.mult, ALU.add))
                step.wait()
                v.wait_ge(pos_done, 1)
                nc.vector.tensor_tensor(pos, pos, bank(7, T * E).rearrange("p (t e) -> p t e", e=E),
                                        ALU.add)
                nc.vector.tensor_copy(cnt_i, bank(7, E, T * E))
                nc.vector.tensor_copy(cnt, bank(7, E, T * E)).then_inc(moving_ready, 1)

            def product(u, m=CAP):
                v.wait_ge(silu_ready, u + 1)
                wait_for(v, hid_turned, u)
                nc.vector.tensor_tensor(h_s[0:m], act_s[0:m], bank(2, FF, FF)[0:m], ALU.mult).then_inc(hid_ready, 1)

            def store_hidT(u, m=CAP):
                v.wait_ge(hid_turned, u + 1)
                wait_for(v, down_done, u)
                nc.vector.tensor_copy(hT_s[:, :, 0:m], bank(3, FF).rearrange("p (c q) -> p c q", q=P)[:, :, 0:m]
                                      ).then_inc(hidT_ready, 1)

            def add_shared(u):
                v.wait_ge(down_done, u + 1)
                nc.vector.tensor_tensor(xs[:, u, :], xs[:, u, :], bank2(4), ALU.add).then_inc(shared_added, 1)

            product(0, P)
            store_hidT(0, P)
            route_a()
            product(1, P)
            add_shared(0)
            store_hidT(1, P)
            route_b()
            product(2, P)
            add_shared(1)
            route_c()
            store_hidT(2, P)
            route_d()
            def slots(x):
                return x[0:CAP]

            def one_hot(ex):
                wait_for(v, placed_done, ex.n - 2)
                nc.vector.tensor_tensor(onehot[ex.buf], slot_row[:, 0:CAP].unsqueeze(1).to_broadcast([P, T, CAP]),
                                        pos[:, :, bass.ds(ex.n, 1)].to_broadcast([P, T, CAP]),
                                        ALU.is_equal).then_inc(onehot_ready, 1)

            def indices(gather_from, add_to, token):
                nc.vector.tensor_scalar(slots(gather_from), slots(token), float(AWAY), None, ALU.add)
                return nc.vector.tensor_scalar(slots(add_to), slots(token), float(AWAY), slots(spare_row),
                                               ALU.add, ALU.min)

            def store_places(ex):
                v.wait_ge(placed_done, ex.n + 1)
                nc.vector.tensor_reduce(slots(placed[:, bass.ds(ex.n, 1), :]).rearrange("p o c -> p (o c)"),
                                        slots(bank(6, 6)).rearrange("p (c j) -> p c j", j=3), AXIS.X, ALU.add
                                        ).then_inc(parts_summed, 1)
                v.wait_ge(parts_summed, ex.n + 1)
                own = bass.ds(ex.n, 1)
                indices(placed_i[:, own, 0], placed_i[:, own, 1], placed[:, own, 0]).then_inc(index_ready, 1)

            v.wait_ge(moving_ready, 1)
            for c in range(3):
                one_hot(Expert(c))
            product(3, P)
            store_places(Expert(0))
            store_places(Expert(1))
            add_shared(2)
            store_places(Expert(2))
            store_hidT(3, P)

            def store_gT(ex):
                v.wait_ge(g_turned, ex.n + 1)
                wait_for(v, gu_done, ex.n + (T - 2))
                for h in range(2):
                    ins = nc.vector.tensor_tensor(
                        xgT[ex.buf][:, 4 * h:4 * h + 4, :],
                        bank(h).rearrange("p (j q) -> p j q", q=P)[:, :, 0:CAP],
                        spread(g2c[:, 4 * h:4 * h + 4], 4, CAP), ALU.mult)
                ins.then_inc(gT_ready, 1)

            def slot_weight(ex):
                wait_for(v, y_scaled, ex.n - 2)
                nc.vector.tensor_copy(w_b[0:CAP, ex.buf:ex.buf + 1],
                                      placed[0:CAP, bass.ds(ex.n, 1), 1]).then_inc(w_ready, 1)

            store_gT(Expert(0))
            add_shared(3)
            store_gT(Expert(1))
            one_hot(Expert(3))
            one_hot(Expert(AHEAD))
            slot_weight(Expert(0))
            product(T)
            store_places(Expert(3))
            store_places(Expert(AHEAD))
            step.done(nc.vector.tensor_scalar(more_f, cnt, float(CAP), None, ALU.is_gt))
            for q in range(2, BLOCKS):
                step.wait()
                step.done(nc.vector.scalar_tensor_tensor(out=more_f, in0=cnt, scalar=float(CAP * q), in1=more_f,
                                                         op0=ALU.is_gt, op1=ALU.add))
            step.wait()
            step.done(nc.vector.tensor_reduce(ov_num, more_f, AXIS.X, ALU.add))
            step.wait()
            nc.vector.tensor_copy(ov_list[:, 0:1], ov_num).then_inc(more_counted, 1)


            def store_hidT_parts(ex):
                u = ex.n + T
                v.wait_ge(hid_turned, u + 1)
                wait_for(v, down_done, u)
                turned_rows = bank(3, FF).rearrange("p (c q) -> p c q", q=P)[:, :, 0:CAP]
                nc.vector.tensor_copy(hid_high[:, :, 0:CAP], turned_rows).then_inc(hid_high_ready, 1)
                v.wait_ge(hid_high_ready, ex.n + 1)
                low_of(nc.vector, hid_low[:, :, 0:CAP], turned_rows, hid_high[:, :, 0:CAP]).then_inc(hidT_ready, 1)

            def turn(ex):
                if ex.i is not None or ex.c + 1 < E:
                    store_gT(ex.next(1))
                store_hidT_parts(ex.next(-1))
                split_down_low(nc.vector, v, ex.next(-1), 0, down_low_dve)
                ahead = ex.i is not None or ex.c + AHEAD < E
                if ahead:
                    one_hot(ex.next(AHEAD))
                slot_weight(ex)
                product(ex.n + T)
                if ahead:
                    store_places(ex.next(AHEAD))
            for c in range(1, LOOP0):
                turn(Expert(c))
            with v.Fori(0, LOOPS) as i:
                for j in range(3):
                    turn(Expert(LOOP0 + j, i))
            for c in range(LAST0, E):
                turn(Expert(c))
            store_hidT(T + E - 1)

            def list_further():
                v.wait_ge(g_turned, E)
                for b in range(3):
                    v.wait_ge(scattered[b], 16 * ((E - b + 2) // 3))
                v.wait_ge(y_scaled, E)
                step.done(nc.vector.memset(ov_x, 1.0))
                step.wait()
                step.done(nc.vector.tensor_tensor_scan(upto_f, low_ones, more_f, 0.0, ALU.mult, ALU.add))
                step.done(nc.vector.tensor_tensor_scan(ov_base, ov_x, ov_x, -1.0, ALU.mult, ALU.add))
                step.wait()
                step.done(nc.vector.tensor_tensor(le_f, upto_f.unsqueeze(1).to_broadcast([P, NOV, E]),
                                                  ov_base.unsqueeze(2).to_broadcast([P, NOV, E]), ALU.is_le))
                step.wait()
                step.done(nc.vector.tensor_reduce(ov_e, le_f, AXIS.X, ALU.add))
                step.wait()
                step.done(nc.vector.tensor_tensor(le_f, le_f, upto_f.unsqueeze(1).to_broadcast([P, NOV, E]),
                                                  ALU.mult))
                nc.vector.tensor_scalar(ov_e, ov_e, float(E - 1), None, ALU.min)
                step.wait()
                step.done(nc.vector.tensor_reduce(ov_x, le_f, AXIS.X, ALU.max))
                step.wait()
                step.done(nc.vector.tensor_tensor(ov_base, ov_base, ov_x, ALU.subtract))
                step.wait()
                step.done(nc.vector.tensor_scalar(ov_base, ov_base, 1.0, float(CAP), ALU.add, ALU.mult))
                nc.vector.tensor_copy(ov_list[:, 1:NOV + 1], ov_e).then_inc(more_listed, 1)

            def further(j, e):
                def in_order(ins, k, of):
                    ins.then_inc(further_step, 1)
                    v.wait_ge(further_step, of * j + k)
                FS = 2
                in_order(nc.vector.tensor_scalar(ov_pos, pos[:, :, bass.ds(e, 1)].rearrange("p t o -> p (t o)"), ov_base[:, bass.ds(j, 1)], None,
                                                 ALU.subtract), 1, FS)
                nc.vector.tensor_tensor(onehot[0], slot_row[:, 0:CAP].unsqueeze(1).to_broadcast([P, T, CAP]),
                                        ov_pos.unsqueeze(2).to_broadcast([P, T, CAP]),
                                        ALU.is_equal).then_inc(ov_onehot, 1)
                v.wait_ge(ov_placed, j + 1)
                in_order(nc.vector.tensor_reduce(slots(ov_placed2), slots(bank(6, 6)).rearrange("p (c j) -> p c j", j=3),
                                                 AXIS.X, ALU.add), 2, FS)
                nc.vector.tensor_copy(slots(w_b[:, 0:1]), slots(ov_placed2[:, 1:2]))
                indices(tok_b[:, 0:1], dst_b[:, 0:1], ov_placed2[:, 0:1]).then_inc(ov_indexed, 1)
                v.wait_ge(g_turned, j + (E + 1))
                for h in range(2):
                    ins = nc.vector.tensor_tensor(
                        xgT[0][:, 4 * h:4 * h + 4, :], bank(h).rearrange("p (j q) -> p j q", q=P)[:, :, 0:CAP],
                        spread(g2c[:, 4 * h:4 * h + 4], 4, CAP), ALU.mult)
                ins.then_inc(gT_ready, 1)
                product(j + (E + T))
                store_hidT(j + (E + T))
                v.wait_ge(ov_scattered, 16 * j + 16)

            count = v.value_load(ov_list[0:1, 0:1], min_val=0, max_val=NOV)
            with v.If(count > 0):
                list_further()
                v.wait_ge(more_listed, 1)
                with v.Fori(0, count) as j:
                    further(j, v.value_load(ov_list[0:1, bass.ds(j + 1, 1)], min_val=0, max_val=E - 1))

        @block.gpsimd
        def _(g):
            x_low_part(nc.gpsimd, g, 0, x_low_pool)
            g.wait_ge(rope_loaded, 16)
            g.wait_ge(gains_ready, 1)
            for kind in range(4):
                cos_r, sin_r = rope_raw[2 * (kind // 2)], rope_raw[2 * (kind // 2) + 1]
                blocks = 1 if kind in (QA, KA) else 2
                hw = HD // (2 * blocks)
                nc.gpsimd.tensor_tensor(cosg[kind], cos_r, gains[:, kind, :].unsqueeze(1).to_broadcast([P, T, HD]),
                                        ALU.mult)
                for b in range(blocks):
                    for s_ in range(2):
                        o, i = (2 * b + s_) * hw, (2 * b + 1 - s_) * hw
                        last = nc.gpsimd.tensor_tensor(
                            sing[kind][:, :, o:o + hw], sin_r[:, :, o:o + hw],
                            gains[:, kind, i:i + hw].unsqueeze(1).to_broadcast([P, T, hw]), ALU.mult)
            last.then_inc(tables_ready, 1)
            x_low_part(nc.gpsimd, g, 2, x_low_pool)
            x_low_part(nc.gpsimd, g, 3, x_low_pool)
            g.wait_ge(tables_ready, 1)
            for m in range(NP):
                c, t = divmod(m, T)
                b = m % 2
                g.wait_ge(normed_ready, m + 1)
                wait_for(g, pairs_turned, m - 1)
                for kind, c0, n, o0, copies in CHUNKS[c]["norm"]:
                    for cp in range(copies):
                        last = nc.gpsimd.tensor_tensor(
                            rotated[b][:, o0 + cp:o0 + cp + copies * (n - 1) + 1:copies, :],
                            normed[b][:, c0 // HD:c0 // HD + n, :],
                            cosg[kind][:, t, :].unsqueeze(1).to_broadcast([P, n, HD]), ALU.mult)
                last.then_inc(cos_done, 1)
                if t == T - 2 and c + 1 < QKV_CHUNKS:
                    split_low(nc.gpsimd, g, c + 1, range(1, K, 2), w_low_pool)
            split_low(nc.gpsimd, g, L_GATE, range(1, K, 2), w_low_pool)
            for m in range(NM):
                hb, t = divmod(m, T)
                half, br = divmod(hb, 2)
                if br == 1:
                    g.wait_ge(product_ready, m + 1)
                    part = merged[:, t, half * HALF:(half + 1) * HALF]
                    nc.gpsimd.tensor_tensor(part, part, gated_b[(half * T + t) % 2], ALU.add).then_inc(merged_ready, 1)
                if t == T - 2:
                    split_low(nc.gpsimd, g, L_GATE + hb + 1, range(1, K, 2), w_low_pool)
            split_low(nc.gpsimd, g, L_OUT + 1, range(1, K, 2), w_low_pool)

            step = Steps(g, pool)
            g.wait_ge(std2_ready, T)
            g.wait_ge(logits_done, 1)
            for b in range(3):
                last = nc.gpsimd.memset(xg[b], 0.0)
            last.then_inc(rows_zeroed, 1)
            g.wait_ge(rows_zeroed, 1)
            for i in range(2):
                g.wait_ge(xn2_stored[i], 16 * (T // 2))
            last_token, last_row = g.to_reg(S - 1), g.to_reg(S + CAP - 1)
            def move_rows(ex, move):
                tokens = g.value_load(cnt_i[0:1, bass.ds(ex.n, 1)], min_val=0, max_val=S)
                low, mid = FEWER
                with g.If(tokens > mid):
                    move(CAP)
                with g.Else():
                    with g.If(tokens > low):
                        move(mid)
                    with g.Else():
                        move(low)

            def gather(ex):
                wait_for(g, g_turned, ex.n - 2)
                g.wait_ge(index_ready, ex.n + 1)
                nc.gpsimd.tensor_copy(tok_b[0:CAP, ex.buf:ex.buf + 1],
                                      placed_i[0:CAP, bass.ds(ex.n, 1), 0]).then_inc(tok_copied, 1)
                g.wait_ge(tok_copied, ex.n + 1)
                g.sem_inc(pool_waited, 1)
                move_rows(ex, lambda rows: nc.gpsimd.indirect_dma_start(
                    out=xg[ex.buf][0:rows], out_offset=None, in_=xn2_rows[:, :],
                    in_offset=bass.IndirectOffsetOnAxis(ap=tok_b[0:rows, ex.buf:ex.buf + 1], axis=0),
                    bounds_check=last_token, oob_is_err=False).then_inc(gathered[ex.buf], 16))

            def scatter(ex):
                g.wait_ge(y_scaled, ex.n + 1)
                wait_for(g, scattered[ex.buf], 16 * ex.third)
                nc.gpsimd.tensor_copy(dst_b[0:CAP, ex.buf:ex.buf + 1],
                                      placed_i[0:CAP, bass.ds(ex.n, 1), 1]).then_inc(dst_copied, 1)
                g.wait_ge(dst_copied, ex.n + 1)
                if isinstance(ex.n, int) and ex.n == 0:
                    g.wait_ge(stream_stored, 16 * T)
                    g.wait_ge(spare_stored, 16)
                else:
                    before = Expert(ex.c + 2, ex.i)
                    g.wait_ge(scattered[before.buf], 16 * before.third)
                g.sem_inc(pool_waited, 1)
                move_rows(ex, lambda rows: nc.gpsimd.indirect_dma_start(
                    out=sum_rows[:, :],
                    out_offset=bass.IndirectOffsetOnAxis(ap=dst_b[0:rows, ex.buf:ex.buf + 1], axis=0),
                    in_=y_s[ex.buf][0:rows], in_offset=None,
                    bounds_check=last_row, oob_is_err=True, compute_op=ALU.add).then_inc(scattered[ex.buf], 16))

            for c in range(4):
                if c == 2:
                    g.wait_ge(spare_stored, 16)
                gather(Expert(c))
            split_down_low(nc.gpsimd, g, Expert(0), 1, down_low_pool)
            for c in range(1, LOOP0):
                gather(Expert(c + 3))
                scatter(Expert(c - 1))
                split_down_low(nc.gpsimd, g, Expert(c), 1, down_low_pool)
            with g.Fori(0, LOOPS) as i:
                for j in range(3):
                    ex = Expert(LOOP0 + j, i)
                    gather(ex.next(3))
                    scatter(ex.next(-1))
                    split_down_low(nc.gpsimd, g, ex, 1, down_low_pool)
            for c in range(LAST0, E):
                if c + 3 < E:
                    gather(Expert(c + 3))
                scatter(Expert(c - 1))
                if c < E - 1:
                    split_down_low(nc.gpsimd, g, Expert(c), 1, down_low_pool)
            scatter(Expert(E - 1))
            last_expert = Expert(E - 1)
            g.wait_ge(scattered[last_expert.buf], 16 * (last_expert.third + 1))

            def further(j, e):
                g.wait_ge(ov_indexed, j + 1)
                g.sem_inc(pool_waited, 1)
                nc.gpsimd.indirect_dma_start(
                    out=xg[0][0:CAP], out_offset=None, in_=xn2_rows[:, :],
                    in_offset=bass.IndirectOffsetOnAxis(ap=tok_b[0:CAP, 0:1], axis=0),
                    bounds_check=last_token, oob_is_err=False).then_inc(ov_gathered, 16)
                g.wait_ge(y_scaled, j + (E + 1))
                g.sem_inc(pool_waited, 1)
                nc.gpsimd.indirect_dma_start(
                    out=sum_rows[:, :], out_offset=bass.IndirectOffsetOnAxis(ap=dst_b[0:CAP, 0:1], axis=0),
                    in_=y_s[0][0:CAP], in_offset=None,
                    bounds_check=last_row, oob_is_err=True, compute_op=ALU.add).then_inc(ov_scattered, 16)
                g.wait_ge(ov_scattered, 16 * j + 16)

            further_blocks(g, further)

        @block.tensor
        def _(pe):
            mm, turn_to = nc.tensor.matmul, nc.tensor.transpose
            pe.wait_ge(ones_ready, 1)

            def turn_rows(rows, b0, m=P):
                for k in range(K):
                    ins = turn_to(bank(b0 + k // 4, m, (k % 4) * P), rows[0:m, k:D:K], ident[0:m, 0:m])
                return ins

            pe.wait_ge(first_loaded, 16 * 2)
            for t in range(T):
                pe.wait_ge(xn_ready, t + 1)
                wait_for(pe, xT_ready, t - 1)
                turn_rows(xnorm[t % 2], 2 * (t % 2)).then_inc(xn_turned, 1)
                if t == 1:
                    pe.wait_ge(row_loaded, 16 * 5)
                    mm(bank(7, 4 * HD + E), ones_t[0:1, :], row_t[0:1, :], start=True, stop=True).then_inc(gains_ps, 1)

            def turn_pairs(m):
                c, t = divmod(m, T)
                pe.wait_ge(rotated_ready, m + 1)
                wait_for(pe, pairs_ready, m - 1)
                if m == 0:
                    pe.wait_ge(gains_ready, 1)
                flat = rotated[m % 2].rearrange("p h d -> p (h d)")
                for j in range(len(CHUNKS[c]["pairs"])):
                    ins = turn_to(bank(4 + m % 2, P, j * P), flat[:, j * P:(j + 1) * P], ident)
                ins.then_inc(pairs_turned, 1)

            def project(dst, n, t):
                own = slice(t * P, (t + 1) * P)
                for k in range(K):
                    if t == 0:
                        pe.wait_ge(*low_piece(n, k))
                    mm(dst, x_high[:, k, own], w_high[:, k, :], start=(k == 0), stop=False)
                    mm(dst, x_high[:, k, own], w_low[:, k, :], start=False, stop=False)
                    ins = mm(dst, x_low[:, k, own], w_high[:, k, :], start=False, stop=(k == K - 1))
                    if t == T - 1 and k < K - 1:
                        ins.then_inc(piece_used, 1)
                return ins

            for m in range(NP):
                c, t = divmod(m, T)
                if m == 0:
                    pe.wait_ge(xT_ready, T)
                if c == 0:
                    pe.wait_ge(*X_LOW[t])
                wait_for(pe, normed_ready, m - 3)
                project(bank(m % 4), c, t).then_inc(proj_done, 1)
                if m >= 1:
                    turn_pairs(m - 1)

            def score(n):
                br, t, h = UNITS[n]
                wait_for(pe, probs_ready, n - 2)
                r = HD * (h % 2)
                b0 = (0, 2, 3)[n % 3]
                rows = slice(r, r + HD)
                own = slice(t * P, (t + 1) * P)
                if br == "A":
                    mm(bank(b0), pairs[rows, q_pair(0, h), own], pairs[rows, k_pair(0, h), :], start=True, stop=True)
                    for g in (1, 2):
                        ins = mm(bank(b0 + 1, P, (g - 1) * P), pairs[rows, q_pair(g, h), own],
                                 pairs[rows, k_pair(g, h), own], start=True, stop=True)
                else:
                    ins = mm(bank(b0), pairs[rows, PAIR_QB + h // 2, own],
                             pairs[rows, PAIR_KB + h // (HB // HKV), :], start=True, stop=True)
                ins.then_inc(scores_done, 1)

            def turn_probs(n):
                i = n % 3
                pe.wait_ge(probs_scaled, n + 1)
                wait_for(pe, probT_act, n)
                wait_for(pe, probT_dve, (n + 2) // 3)
                for j in range(6 if i == 0 else 4):
                    b = 5 if i == 2 else 4 + j // 4
                    ins = turn_to(bank(b, P, (j % 4) * P), prob[i][:, j * P:(j + 1) * P], ident)
                ins.then_inc(probs_turned, 1)

            def weigh(n):
                br, t, h = UNITS[n]
                pe.wait_ge(probT_act, n + 1)
                if br == "A":
                    pe.wait_ge(probT_dve, n // 3 + 1)
                    if h % 2 == 0:
                        wait_for(pe, yT_a_ready, n // 6)
                elif h % 2 == 0:
                    wait_for(pe, yT_b_ready, n // 3)
                hs = slice(h * HD, (h + 1) * HD)
                if br == "A":
                    vals = [vA[:, u, 0, hs] for u in range(T)] + [vA[:, t, 1, hs], vA[:, t, 2, hs]]
                else:
                    kv = h // (HB // HKV)
                    vals = [vB[:, u, kv * HD:(kv + 1) * HD] for u in range(T)]
                r = HD * (h % 2)
                for j, val in enumerate(vals):
                    ins = mm(bank(7 if br == "A" else 6, P)[r:r + HD], val, probT[n % 3][:, j, :],
                             start=(j == 0), stop=(j == len(vals) - 1))
                ins.then_inc(pv_done, 1)

            pe.wait_ge(pairs_ready, NP - T)
            pe.wait_ge(normed_ready, NP - 2)
            score(0)
            turn_pairs(NP - 1)
            pe.wait_ge(pairs_ready, NP)
            score(1)
            for n in range(NU + 1):
                if n + 2 < NU:
                    score(n + 2)
                if n < NU:
                    turn_probs(n)
                if n >= 1:
                    weigh(n - 1)

            for m in range(NM):
                hb, t = divmod(m, T)
                half, br = divmod(hb, 2)
                wait_for(pe, product_ready, m - 1)
                bg = 4 + 2 * (m % 2)
                own = slice(t * P, (t + 1) * P)
                if t == 0:
                    project(bank(bg), L_GATE + hb, t)
                    pe.wait_ge(branch_low_ready, hb + 1)
                if m == 0:
                    pe.wait_ge(yT_a_ready, T * HA // 2)
                    pe.wait_ge(yT_b_ready, T * HB // 2)
                rows, first = BRANCH_ROWS[br], br * BRANCH_ROWS[0]
                for j in range(rows):
                    high, low = y_high[:, first + j, own], y_low[:, first + j, own]
                    mm(bank(bg + 1), high, branch_high[:, j, :], start=(j == 0), stop=False)
                    mm(bank(bg + 1), high, branch_low[:, j, :], start=False, stop=False)
                    ins = mm(bank(bg + 1), low, branch_high[:, j, :], start=False, stop=(j == rows - 1))
                if t == T - 1:
                    ins.then_inc(branch_used, 1)
                if t > 0:
                    ins = project(bank(bg), L_GATE + hb, t)
                ins.then_inc(gate_done, 1)
            def turn_merged(t):
                pe.wait_ge(merged_ready, T + t + 1)
                wait_for(pe, mT_ready, t - 1)
                turn_rows(merged[:, t, :], 2 * (t % 2)).then_inc(merged_turned, 1)

            def project_out(half, t):
                o = half * T + t
                pe.wait_ge(mT_ready, t + 1)
                wait_for(pe, h_ready, o - 2)
                project(bank(4 + o % 3), L_OUT + half, t).then_inc(out_done, 1)

            def turn_x2(t):
                pe.wait_ge(xn2_ready, t + 1)
                wait_for(pe, x2T_ready, t)
                turn_rows(xnorm[t % 2], 0).then_inc(x2_turned, 1)

            def router(t):
                pe.wait_ge(x2T_ready, t + 1)
                if t == 0:
                    pe.wait_ge(router_loaded, 16)
                for k in range(K):
                    ins = mm(bank(7, P, t * P)[0:E], wr[:, k, :], x2T[:, k, t * P:(t + 1) * P],
                             start=(k == 0), stop=(k == K - 1))
                ins.then_inc(router_done, 1)

            turn_merged(0)
            turn_merged(1)
            pe.wait_ge(product_ready, NM)
            for t in range(T):
                project_out(0, t)
                if t + 2 < T:
                    turn_merged(t + 2)
            for t in range(T):
                project_out(1, t)
                if t >= 1:
                    turn_x2(t - 1)
                if t >= 2:
                    router(t - 2)

            def gate_up(u, lhs, s, m=CAP):
                wait_for(pe, hid_ready, u)
                w, _ = ffn_parts(s)
                for k in range(K):
                    ins = mm(bank(2)[0:m].rearrange("p (s f) -> p s f", s=2), lhs(k), w[:, :, k, :],
                             start=(k == 0), stop=(k == K - 1))
                ins.then_inc(gu_done, 1)

            def turn_hidden(u, m=CAP):
                pe.wait_ge(hid_ready, u + 1)
                wait_for(pe, hidT_ready, u)
                for c in range(2):
                    ins = turn_to(bank(3, m, c * P), h_s[0:m, c:FF:2], ident[0:m, 0:m])
                ins.then_inc(hid_turned, 1)

            def down(u, s, m=CAP):
                pe.wait_ge(hidT_ready, u + 1)
                _, w = ffn_parts(s)
                for half in range(2):
                    for c in range(2):
                        ins = mm(bank(4 + half)[0:m], hT_s[:, c, 0:m], w[:, c, half * HALF:(half + 1) * HALF],
                                 start=(c == 0), stop=(c == 1))
                ins.then_inc(down_done, 1)

            def place(ex):
                pe.wait_ge(onehot_ready, ex.n + 1)
                wait_for(pe, parts_summed, ex.n)
                for t in range(T):
                    ins = mm(bank(6, 6)[0:CAP], onehot[ex.buf][:, t, :], moving_flat[:, t, bass.ds(ex.n * 6, 6)],
                             start=(t == 0), stop=(t == T - 1))
                ins.then_inc(placed_done, 1)

            wait_load(pe, L_SHARED)
            s = L_SHARED % NSLOT

            def shared_gate_up(u):
                gate_up(u, lambda k: x2T[:, k, u * P:(u + 1) * P], s, P)

            def shared_down(u):
                wait_for(pe, shared_added, u)
                down(u, s, P)

            shared_gate_up(0)
            turn_x2(T - 1)
            router(T - 2)
            turn_hidden(0, P)
            router(T - 1)
            pe.wait_ge(h_ready, 2 * T)
            pe.wait_ge(logitsT_ready, 1)
            for t in range(T):
                ins = turn_to(bank(6, E, t * E), logitsT[0:E, t * P:(t + 1) * P], ident[0:E, 0:E])
            ins.then_inc(logits_done, 1)
            shared_gate_up(1)
            shared_down(0)
            turn_hidden(1, P)
            shared_gate_up(2)
            shared_down(1)
            pe.wait_ge(mask_ready, 1)
            for t in range(T):
                mm(bank(7, E, t * E), below_b, maskb[:, t, :], start=True, stop=(t == 0))
                for q in range(t):
                    mm(bank(7, E, t * E), ones_b, maskb[:, q, :], start=False, stop=(q == t - 1))
            for t in range(T):
                ins = mm(bank(7, E, T * E), ones_b, maskb[:, t, :], start=(t == 0), stop=(t == T - 1))
            ins.then_inc(pos_done, 1)
            turn_hidden(2, P)
            shared_gate_up(3)
            pe.wait_ge(moving_ready, 1)
            place(Expert(0))
            place(Expert(1))
            shared_down(2)
            place(Expert(2))
            turn_hidden(3, P)

            def turn_gathered(ex):
                pe.wait_ge(gathered[ex.buf], 16 * (ex.third + 1))
                wait_for(pe, gT_ready, ex.n)
                turn_rows(xg[ex.buf], 0, CAP).then_inc(g_turned, 1)

            def expert_gate_up(ex):
                wait_expert(pe, ex)
                pe.wait_ge(gT_ready, ex.n + 1)
                gate_up(ex.n + T, lambda k: xgT[ex.buf][:, k, :], expert_slot(ex))

            def expert_down(ex):
                if isinstance(ex.n, int) and ex.n == 0:
                    pe.wait_ge(shared_added, T)
                else:
                    pe.wait_ge(y_scaled, ex.n)
                if isinstance(ex.n, int) and ex.n == E - 1:
                    down(ex.n + T, expert_slot(ex))
                    return
                pe.wait_ge(hidT_ready, ex.n + (T + 1))
                pe.wait_ge(down_low_dve, ex.n + 1)
                pe.wait_ge(down_low_pool, ex.n + 1)
                for half in range(2):
                    dst, cols = bank(4 + half)[0:CAP], slice(half * HALF, (half + 1) * HALF)
                    for c in range(2):
                        high, low = hid_high[:, c, 0:CAP], hid_low[:, c, 0:CAP]
                        mm(dst, high, down_high[:, c, cols], start=(c == 0), stop=False)
                        mm(dst, high, down_low[:, c, cols], start=False, stop=False)
                        ins = mm(dst, low, down_high[:, c, cols], start=False, stop=(c == 1))
                ins.then_inc(down_done, 1)

            turn_gathered(Expert(0))
            shared_down(3)
            turn_gathered(Expert(1))
            expert_gate_up(Expert(0))
            place(Expert(3))

            def turn(ex):
                if ex.i is not None or ex.c + 1 < E:
                    turn_gathered(ex.next(1))
                turn_hidden(ex.n + (T - 1))
                if isinstance(ex.n, int) and ex.n == 1:
                    place(Expert(AHEAD))
                expert_gate_up(ex)
                if ex.i is not None or ex.c + AHEAD < E:
                    place(ex.next(AHEAD))
                expert_down(ex.next(-1))
            for c in range(1, LOOP0):
                turn(Expert(c))
            with pe.Fori(0, LOOPS) as i:
                for j in range(3):
                    turn(Expert(LOOP0 + j, i))
            for c in range(LAST0, E):
                turn(Expert(c))
            turn_hidden(T + E - 1)
            expert_down(Expert(E - 1))

            def further(j, e):
                pe.wait_ge(ov_onehot, j + 1)
                for t in range(T):
                    ins = mm(bank(6, 6)[0:CAP], onehot[0][:, t, :], moving_flat[:, t, bass.ds(e * 6, 6)],
                             start=(t == 0), stop=(t == T - 1))
                ins.then_inc(ov_placed, 1)
                pe.wait_ge(ov_gathered, 16 * j + 16)
                turn_rows(xg[0], 0, CAP).then_inc(g_turned, 1)
                pe.wait_ge(ring_loaded[0], 48 * j + (per_slot[0] + 48 * EXPERTS_IN_0 + 48))
                pe.wait_ge(gT_ready, j + (E + 1))
                gate_up(j + (E + T), lambda k: xgT[0][:, k, :], 0)
                turn_hidden(j + (E + T))
                pe.wait_ge(y_scaled, j + E)
                down(j + (E + T), 0)

            further_blocks(pe, further)


_INS = ["x", "norm1_g", "w_in", "q_norm_a", "k_norm_a", "q_norm_b", "k_norm_b", "w_branch_a", "w_branch_b",
        "w_out", "norm2_g", "w_router", "router_bias", "we_gate", "we_up", "we_down", "ws_gate", "ws_up",
        "ws_down"]


def kernel(**inputs):
    import concourse.bacc as bacc
    from concourse.bass_utils import run_bass_kernel_spmd

    nc = bacc.Bacc("TRN2", target_bir_lowering=False, num_devices=1)
    arrays = {n: np.ascontiguousarray(inputs[n]) for n in _INS}
    arrays["rope"], arrays["masks"], arrays["misc"] = host_constants()
    arrays = {f"in_{n}": x for n, x in arrays.items()}
    aps = {n[3:]: nc.dram_tensor(n, x.shape, mybir.dt.from_np(x.dtype), kind="ExternalInput").ap()
           for n, x in arrays.items()}
    out = nc.dram_tensor("out", (1, S, D), F32, kind="ExternalOutput").ap()
    xn2_rows = nc.dram_tensor("xn2_rows", (S, D), F32, kind="Internal").ap()
    sum_rows = nc.dram_tensor("sum_rows", (S + CAP, D), F32, kind="Internal").ap()
    build(nc, aps, out, xn2_rows, sum_rows)
    r = run_bass_kernel_spmd(nc, [arrays], core_ids=[0])
    return r.results[0]["out"]
```
